# Optimizing a Trainium2 kernel written in Bass

```python
import jax, jax.numpy as jnp
from jax import lax
import numpy as np

D_MODEL = 2048
BATCH = 1
SEQ = 256
DEPTH = 1

N_HEADS = 16
QK_NOPE_DIM = 128
QK_ROPE_DIM = 64
QK_HEAD_DIM = QK_NOPE_DIM + QK_ROPE_DIM
V_HEAD_DIM = 128
Q_LORA_RANK = 512
KV_LORA_RANK = 512
ROPE_THETA = 10000.0
Q_BLOCK = 128
POOL_WINDOWS = (2, 4, 8, 16)
POOL_GROUPS = 4
POOL_GROUP_DIM = D_MODEL // 8
POOL_WIDTH = POOL_GROUPS * POOL_GROUP_DIM
N_BRANCHES = 2
D_FF = (8 * D_MODEL + 3 * 256 - 1) // (3 * 256) * 256
EPS = 1e-6

IN_SPLITS = (Q_LORA_RANK, KV_LORA_RANK, QK_ROPE_DIM, POOL_WIDTH, N_BRANCHES * D_MODEL)
D_IN = sum(IN_SPLITS)


def rmsnorm(x, g):
    x32 = x.astype(jnp.float32)
    inv = lax.rsqrt(jnp.mean(x32 * x32, axis=-1, keepdims=True) + EPS)
    return (x32 * inv).astype(x.dtype) * g

def apply_rope(t, positions):
    half = QK_ROPE_DIM // 2
    inv_freq = ROPE_THETA ** (-jnp.arange(half, dtype=jnp.float32) / half)
    ang = positions.astype(jnp.float32)[..., None] * inv_freq
    cos = jnp.cos(ang)[:, :, None, :]
    sin = jnp.sin(ang)[:, :, None, :]
    t32 = t.astype(jnp.float32)
    t1, t2 = t32[..., :half], t32[..., half:]
    out = jnp.concatenate([t1 * cos - t2 * sin, t2 * cos + t1 * sin], axis=-1)
    return out.astype(t.dtype)

def causal_multiscale_pool(u):
    B, S, _ = u.shape
    ug = u.reshape(B, S, POOL_GROUPS, POOL_GROUP_DIM)
    cs = jnp.cumsum(ug.astype(jnp.float32), axis=1)
    cs = jnp.pad(cs, ((0, 0), (1, 0), (0, 0), (0, 0)))
    t = jnp.arange(S)
    outs = []
    for g, w in enumerate(POOL_WINDOWS):
        cs_g = cs[:, :, g]
        lo = jnp.maximum(t + 1 - w, 0)
        window_sum = cs_g[:, t + 1] - cs_g[:, lo]
        count = (t + 1 - lo).astype(jnp.float32)
        outs.append(window_sum / count[None, :, None] - ug[:, :, g].astype(jnp.float32))
    return jnp.stack(outs, axis=2).astype(u.dtype)

def causal_block_attention(q, k, v):
    B, S, H, Dq = q.shape
    nb = S // Q_BLOCK
    qb = q.reshape(B, nb, Q_BLOCK, H, Dq).transpose(1, 0, 2, 3, 4)
    kpos = jnp.arange(S)
    scale = QK_HEAD_DIM ** -0.5

    def one_block(args):
        i, qi = args
        s = jnp.einsum('bqhd,bkhd->bhqk', qi, k, preferred_element_type=jnp.float32) * scale
        qpos = i * Q_BLOCK + jnp.arange(Q_BLOCK)
        mask = kpos[None, :] <= qpos[:, None]
        s = jnp.where(mask[None, None], s, -jnp.inf)
        p = jax.nn.softmax(s, axis=-1).astype(v.dtype)
        return jnp.einsum('bhqk,bkhd->bqhd', p, v)

    out = lax.map(one_block, (jnp.arange(nb), qb))
    return out.transpose(1, 0, 2, 3, 4).reshape(B, S, H, v.shape[-1])

def first_inputs(seed: int = 0) -> dict:
    key = jax.random.key(seed)
    ks = jax.random.split(key, 24)

    def w(k, shape, fan_in):
        return jax.random.normal(k, shape, jnp.float32) * fan_in ** -0.5

    def gain(k, shape):
        return 1.0 + 0.02 * jax.random.normal(k, shape, jnp.float32)

    L = DEPTH
    return {
        "x": jax.random.normal(ks[0], (BATCH, SEQ, D_MODEL), jnp.float32),
        "positions": jnp.broadcast_to(jnp.arange(SEQ, dtype=jnp.int32), (BATCH, SEQ)),
        "attn_norm_g": gain(ks[1], (L, D_MODEL)),
        "w_in": w(ks[2], (L, D_MODEL, D_IN), D_MODEL),
        "b_gate": 0.02 * jax.random.normal(ks[3], (L, N_BRANCHES * D_MODEL), jnp.float32),
        "q_a_norm_g": gain(ks[4], (L, Q_LORA_RANK)),
        "w_q_b": w(ks[5], (L, Q_LORA_RANK, N_HEADS * QK_HEAD_DIM), Q_LORA_RANK),
        "kv_a_norm_g": gain(ks[6], (L, KV_LORA_RANK)),
        "w_kv_b": w(ks[7], (L, KV_LORA_RANK, N_HEADS * (QK_NOPE_DIM + V_HEAD_DIM)), KV_LORA_RANK),
        "q_norm_g": gain(ks[8], (L, QK_HEAD_DIM)),
        "k_norm_g": gain(ks[9], (L, QK_HEAD_DIM)),
        "w_attn_o": w(ks[10], (L, N_HEADS * V_HEAD_DIM, D_MODEL), N_HEADS * V_HEAD_DIM),
        "w_pool_grp": w(ks[11], (L, POOL_GROUPS, POOL_GROUP_DIM, POOL_GROUP_DIM), POOL_GROUP_DIM),
        "pool_scale": gain(ks[12], (L, POOL_GROUPS, POOL_GROUP_DIM)),
        "w_pool_o": w(ks[13], (L, POOL_WIDTH, D_MODEL), POOL_WIDTH),
        "w_out": w(ks[14], (L, D_MODEL, D_MODEL), D_MODEL),
        "ffn_norm_g": gain(ks[15], (L, D_MODEL)),
        "w_ffn_gate": w(ks[16], (L, D_MODEL, D_FF), D_MODEL),
        "w_ffn_up": w(ks[17], (L, D_MODEL, D_FF), D_MODEL),
        "w_ffn_down": w(ks[18], (L, D_FF, D_MODEL), D_FF),
    }

def first_block(x, positions, attn_norm_g, w_in, b_gate, q_a_norm_g, w_q_b, kv_a_norm_g, w_kv_b,
              q_norm_g, k_norm_g, w_attn_o, w_pool_grp, pool_scale, w_pool_o, w_out,
              ffn_norm_g, w_ffn_gate, w_ffn_up, w_ffn_down):
    B, S, _ = x.shape
    offsets = list(np.cumsum(IN_SPLITS)[:-1])
    for l in range(DEPTH):
        h = rmsnorm(x, attn_norm_g[l])
        proj = h @ w_in[l]
        c_q, c_kv, k_rope, u_pool, gate_logits = jnp.split(proj, offsets, axis=-1)
        gates = jax.nn.sigmoid(gate_logits + b_gate[l])
        g_pool, g_attn = gates[..., :D_MODEL], gates[..., D_MODEL:]

        pooled = causal_multiscale_pool(u_pool)
        pooled = jnp.einsum('bsgc,gcd->bsgd', pooled, w_pool_grp[l]) * pool_scale[l]
        y_pool = pooled.reshape(B, S, POOL_WIDTH) @ w_pool_o[l]

        q = (rmsnorm(c_q, q_a_norm_g[l]) @ w_q_b[l]).reshape(B, S, N_HEADS, QK_HEAD_DIM)
        kv = (rmsnorm(c_kv, kv_a_norm_g[l]) @ w_kv_b[l]).reshape(B, S, N_HEADS, QK_NOPE_DIM + V_HEAD_DIM)
        k_nope, v = kv[..., :QK_NOPE_DIM], kv[..., QK_NOPE_DIM:]
        k_rope_h = jnp.broadcast_to(k_rope[:, :, None, :], (B, S, N_HEADS, QK_ROPE_DIM))
        k = jnp.concatenate([k_nope, k_rope_h], axis=-1)
        q = rmsnorm(q, q_norm_g[l])
        k = rmsnorm(k, k_norm_g[l])
        q = jnp.concatenate([q[..., :QK_NOPE_DIM], apply_rope(q[..., QK_NOPE_DIM:], positions)], axis=-1)
        k = jnp.concatenate([k[..., :QK_NOPE_DIM], apply_rope(k[..., QK_NOPE_DIM:], positions)], axis=-1)
        attn = causal_block_attention(q, k, v)
        y_attn = attn.reshape(B, S, N_HEADS * V_HEAD_DIM) @ w_attn_o[l]

        mixed = g_pool * y_pool + g_attn * y_attn
        x = x + mixed @ w_out[l]

        h2 = rmsnorm(x, ffn_norm_g[l])
        x = x + (jax.nn.silu(h2 @ w_ffn_gate[l]) * (h2 @ w_ffn_up[l])) @ w_ffn_down[l]
    return x


CHUNK = 64
SB_HEADS = 8
SB_HEAD_DIM = 128
SB_WIDTH = SB_HEADS * SB_HEAD_DIM
SGU_GROUPS = 8
SGU_GROUP_DIM = 128
SGU_WIDTH = SGU_GROUPS * SGU_GROUP_DIM
SGU_LEN = 128
D_FF_2 = 4 * D_MODEL
IN_COLS = 3 * SB_WIDTH + 2 * SGU_WIDTH + 2 * D_MODEL


def rms_norm(x, g):
    xf = x.astype(jnp.float32)
    y = xf * lax.rsqrt(jnp.mean(xf * xf, axis=-1, keepdims=True) + EPS)
    return (y * g.astype(jnp.float32)).astype(x.dtype)

def layer_norm(x, g, b):
    xf = x.astype(jnp.float32)
    mu = jnp.mean(xf, axis=-1, keepdims=True)
    xc = xf - mu
    y = xc * lax.rsqrt(jnp.mean(xc * xc, axis=-1, keepdims=True) + EPS)
    return (y * g.astype(jnp.float32) + b.astype(jnp.float32)).astype(x.dtype)

def stick_breaking_attention(q, k, v):
    seq = q.shape[2]
    scale = SB_HEAD_DIM ** -0.5
    outs = []
    for blk in range(seq // Q_BLOCK):
        q0 = blk * Q_BLOCK
        kend = q0 + Q_BLOCK
        qb = q[:, :, q0:kend].astype(jnp.float32)
        kb = k[:, :, :kend].astype(jnp.float32)
        vb = v[:, :, :kend]
        z = jnp.einsum('bhtd,bhsd->bhts', qb, kb) * scale
        t_idx = q0 + jnp.arange(Q_BLOCK)[:, None]
        s_idx = jnp.arange(kend)[None, :]
        past = s_idx < t_idx
        log_keep = jnp.where(past, jax.nn.log_sigmoid(-z), 0.0)
        tail = lax.cumsum(log_keep, axis=3, reverse=True) - log_keep
        log_a = jax.nn.log_sigmoid(z) + tail
        a = jnp.where(past, jnp.exp(log_a), 0.0)
        outs.append(jnp.einsum('bhts,bhsd->bhtd', a.astype(v.dtype), vb))
    return jnp.concatenate(outs, axis=2)

def spatial_gating(u, v, ln_g, ln_b, w_s, b_s):
    bsz, seq, _ = v.shape
    v = layer_norm(v, ln_g, ln_b)
    vc = v.reshape(bsz, seq // SGU_LEN, SGU_LEN, SGU_GROUPS, SGU_GROUP_DIM)
    pos = jnp.arange(SGU_LEN)
    mask = (pos[None, :] // CHUNK) <= (pos[:, None] // CHUNK)
    w = jnp.where(mask[None], w_s, jnp.zeros_like(w_s))
    mixed = jnp.einsum('gij,bcjgd->bcigd', w, vc) + b_s.T[:, :, None]
    return u * mixed.reshape(bsz, seq, SGU_WIDTH)

def second_inputs(seed: int = 0) -> dict:
    key = jax.random.key(seed)
    ks = jax.random.split(key, 16)
    f32 = jnp.float32
    nrm = lambda k, shape, s: jax.random.normal(k, shape, f32) * s
    return {
        "x": nrm(ks[0], (BATCH, SEQ, D_MODEL), 1.0),
        "g_mix": 1.0 + nrm(ks[1], (DEPTH, D_MODEL), 0.05),
        "w_in": nrm(ks[2], (DEPTH, D_MODEL, IN_COLS), D_MODEL ** -0.5),
        "g_q": 1.0 + nrm(ks[3], (DEPTH, SB_HEADS, SB_HEAD_DIM), 0.05),
        "g_k": 1.0 + nrm(ks[4], (DEPTH, SB_HEADS, SB_HEAD_DIM), 0.05),
        "sgu_ln_g": 1.0 + nrm(ks[5], (DEPTH, SGU_WIDTH), 0.05),
        "sgu_ln_b": nrm(ks[6], (DEPTH, SGU_WIDTH), 0.02),
        "w_spatial": nrm(ks[7], (DEPTH, SGU_GROUPS, SGU_LEN, SGU_LEN), SGU_LEN ** -0.5),
        "b_spatial": 1.0 + nrm(ks[8], (DEPTH, SGU_GROUPS, SGU_LEN), 0.05),
        "w_oa": nrm(ks[9], (DEPTH, SB_WIDTH, D_MODEL), SB_WIDTH ** -0.5),
        "w_ob": nrm(ks[10], (DEPTH, SGU_WIDTH, D_MODEL), SGU_WIDTH ** -0.5),
        "w_out": nrm(ks[11], (DEPTH, D_MODEL, D_MODEL), D_MODEL ** -0.5),
        "g_ff": 1.0 + nrm(ks[12], (DEPTH, D_MODEL), 0.05),
        "w_ff1": nrm(ks[13], (DEPTH, D_MODEL, D_FF_2), D_MODEL ** -0.5),
        "w_ff2": nrm(ks[14], (DEPTH, D_FF_2, D_MODEL), D_FF_2 ** -0.5),
    }

def second_block(x, g_mix, w_in, g_q, g_k, sgu_ln_g, sgu_ln_b, w_spatial, b_spatial,
              w_oa, w_ob, w_out, g_ff, w_ff1, w_ff2):
    bsz, seq, _ = x.shape
    splits = [SB_WIDTH, 2 * SB_WIDTH, 3 * SB_WIDTH,
              3 * SB_WIDTH + SGU_WIDTH, 3 * SB_WIDTH + 2 * SGU_WIDTH,
              3 * SB_WIDTH + 2 * SGU_WIDTH + D_MODEL]
    for l in range(DEPTH):
        h = rms_norm(x, g_mix[l])
        proj = h @ w_in[l]
        q, k, v_sb, u, v_sg, gate_a, gate_b = jnp.split(proj, splits, axis=-1)

        q = rms_norm(q.reshape(bsz, seq, SB_HEADS, SB_HEAD_DIM), g_q[l])
        k = rms_norm(k.reshape(bsz, seq, SB_HEADS, SB_HEAD_DIM), g_k[l])
        v_sb = v_sb.reshape(bsz, seq, SB_HEADS, SB_HEAD_DIM)
        o = stick_breaking_attention(q.transpose(0, 2, 1, 3), k.transpose(0, 2, 1, 3),
                                     v_sb.transpose(0, 2, 1, 3))
        y_a = o.transpose(0, 2, 1, 3).reshape(bsz, seq, SB_WIDTH) @ w_oa[l]

        u = jax.nn.gelu(u, approximate=False)
        v_sg = jax.nn.gelu(v_sg, approximate=False)
        s = spatial_gating(u, v_sg, sgu_ln_g[l], sgu_ln_b[l], w_spatial[l], b_spatial[l])
        y_b = s @ w_ob[l]

        merged = jax.nn.sigmoid(gate_a) * y_a + jax.nn.sigmoid(gate_b) * y_b
        x = x + merged @ w_out[l]

        h2 = rms_norm(x, g_ff[l])
        x = x + jnp.square(jax.nn.relu(h2 @ w_ff1[l])) @ w_ff2[l]
    return x


def setup_inputs(seed=0):
    out = dict(first_inputs(seed))
    for name, value in second_inputs(seed + 1).items():
        if name != "x":
            out[name + "_2"] = value
    return out


def reference(
    x, positions, attn_norm_g, w_in, b_gate, q_a_norm_g, w_q_b, kv_a_norm_g, w_kv_b, q_norm_g,
    k_norm_g, w_attn_o, w_pool_grp, pool_scale, w_pool_o, w_out, ffn_norm_g, w_ffn_gate,
    w_ffn_up, w_ffn_down, g_mix_2, w_in_2, g_q_2, g_k_2, sgu_ln_g_2, sgu_ln_b_2, w_spatial_2,
    b_spatial_2, w_oa_2, w_ob_2, w_out_2, g_ff_2, w_ff1_2, w_ff2_2,
):
    x = first_block(
        x, positions, attn_norm_g, w_in, b_gate, q_a_norm_g, w_q_b, kv_a_norm_g, w_kv_b,
        q_norm_g, k_norm_g, w_attn_o, w_pool_grp, pool_scale, w_pool_o, w_out, ffn_norm_g,
        w_ffn_gate, w_ffn_up, w_ffn_down,
    )
    return second_block(
        x, g_mix_2, w_in_2, g_q_2, g_k_2, sgu_ln_g_2, sgu_ln_b_2, w_spatial_2, b_spatial_2,
        w_oa_2, w_ob_2, w_out_2, g_ff_2, w_ff1_2, w_ff2_2,
    )


_drawn_inputs = setup_inputs


def setup_inputs(seed=0):
    import zlib

    import numpy as np

    out = dict(_drawn_inputs(seed))
    spreads = {}
    factors = {'attn_norm_g': 4.413,
     'b_gate': 8.0,
     'q_a_norm_g': 8.0,
     'kv_a_norm_g': 8.0,
     'q_norm_g': 8.0,
     'k_norm_g': 8.0,
     'pool_scale': 14.532,
     'ffn_norm_g': 12.816,
     'g_q_2': 200.0,
     'g_k_2': 200.0,
     'sgu_ln_g_2': 38.384,
     'sgu_ln_b_2': 200.0,
     'b_spatial_2': 31.616,
     'g_mix_2': 5.24,
     'g_ff_2': 8.0}
    for name, (base, spread) in spreads.items():
        noise = np.random.default_rng([zlib.crc32(name.encode()), seed]).standard_normal(out[name].shape)
        drawn = base * np.exp(spread * noise) if base else spread * noise
        out[name] = __import__('jax').numpy.asarray(drawn.astype(out[name].dtype))
    for name, factor in factors.items():
        out[name] = (out[name] * factor).astype(out[name].dtype)
    return out
```

```python
import numpy as np

import concourse.bass as bass
from concourse import mybir

F32 = mybir.dt.float32
F32R = mybir.dt.float32r
I32 = mybir.dt.int32
ALU = mybir.AluOpType
ACT = mybir.ActivationFunctionType
AX = mybir.AxisListType

P = 128
TOK = 2
S = TOK * P
D = 2048
KC = D // P
N = 512
EPS = 1e-6

Q_RANK, KV_RANK, ROPE, POOL = 512, 512, 64, 1024
NOPE, VDIM, HEADS = 128, 128, 16
QK = NOPE + ROPE
HALF = ROPE // 2
POOL_WINDOWS = (2, 4, 8, 16)
D_FF = 5632
COL_KV = Q_RANK
COL_KR = COL_KV + KV_RANK
COL_POOL = COL_KR + ROPE
COL_GATE = COL_POOL + POOL
PAIRS = HEADS // 2
SM_SCALE = QK ** -0.5

SB = 1024
SB_HEADS = 8
SGU = 1024
GROUPS = 8
CHUNK = 64
D_FF2 = 8192
COL_U = 3 * SB
COL_VS = COL_U + SGU
COL_GATE2 = COL_VS + SGU
SB_SCALE = 128 ** -0.5

RAW = 4
SPLIT = 4
LEAD = 4
LO_CREDIT = 2 * RAW
EVAC_CREDIT = 2

NB1 = D_FF // N
NB2 = D_FF2 // N

C_ID, C_CAUSAL, C_AFTER, C_ONES, C_PAST, C_FREQ = 0, 128, 512, 640, 768, 896
C_END = 928
TWO_PI = 2 * np.pi
PI_1 = 6.28125
PI_2 = float(np.float32(np.round((TWO_PI - PI_1) * 2 ** 21) / 2 ** 21))
PI_3 = float(TWO_PI - PI_1 - PI_2)
MAGIC = 1.5 * 2 ** 23
PI_MAX = 3.1415925


FULL = (KC, N)
SHORT = (4, N)
SUB = [FULL, (4, 2 * QK), SHORT]
PLAN = [
    ("in", 1, [FULL, FULL, (KC, ROPE), FULL, FULL]),
    ("pool", 2, [(8, N), (8, N)]),
    ("heads_first", 1, SUB),
    ("heads", (PAIRS - 2) // 2, SUB + SUB),
    ("heads_last", 1, SUB),
    ("attn_o", 1, [FULL] * 4),
    ("out", 1, [FULL] * 4),
    ("ffn_first", 1, [FULL, FULL]),
    ("ffn", NB1 - 1, [FULL, FULL] + [SHORT] * 4),
    ("ffn_last", 1, [SHORT] * 4),
    ("qk2", 1, [FULL] * 4),
    ("uv2", 2, [FULL] * 2),
    ("v2", 1, [FULL] * 2),
    ("gates2", 4, [FULL] * 2),
    ("mix2", 4, [(8, N), (8, N)]),
    ("out2", 1, [FULL] * 4),
    ("ffn2_first", 1, [FULL]),
    ("ffn2", NB2 - 1, [FULL] + [SHORT] * 4),
    ("ffn2_last", 1, [SHORT] * 4),
]


class At:

    def __init__(self, name, i=0):
        gran = panel = 0
        for stage, turns, panels in PLAN:
            sizes = [k // 2 for k, _ in panels]
            if stage == name:
                break
            gran += turns * sum(sizes)
            panel += turns * len(panels)
        self.i, self.panels = i, panels
        self.gran0, self.panel0 = gran, panel
        self.starts = [sum(sizes[:p]) for p in range(len(sizes) + 1)]
        self.per = self.starts[-1]
        assert turns == 1 or self.per % (2 * RAW) == 0

    def gran(self, p, k=0):
        return self.i * self.per + (self.gran0 + self.starts[p] + k)

    def slot(self, p, k=0):
        return (self.gran0 + self.starts[p] + k) % SPLIT

    def raw_slot(self, p, k=0):
        return (self.gran0 + self.starts[p] + k) // 2 % RAW

    def loads(self, p, k=0):
        return self.i * (16 * self.per // (2 * RAW)) + 16 * ((self.gran0 + self.starts[p] + k) // (2 * RAW) + 1)

    def end(self, p):
        return self.gran(p, self.panels[p][0] // 2)

    def panel(self, p):
        return self.i * len(self.panels) + (self.panel0 + p)

    def pair(self, p):
        return (self.panel0 + p) % 2


def two_blocks(nc, x, positions, attn_norm_g, w_in, b_gate, q_a_norm_g, w_q_b, kv_a_norm_g, w_kv_b,
               q_norm_g, k_norm_g, w_attn_o, w_pool_grp, pool_scale, w_pool_o, w_out, ffn_norm_g,
               w_ffn_gate, w_ffn_up, w_ffn_down, g_mix_2, w_in_2, g_q_2, g_k_2, sgu_ln_g_2,
               sgu_ln_b_2, w_spatial_2, b_spatial_2, w_oa_2, w_ob_2, w_out_2, g_ff_2, w_ff1_2,
               w_ff2_2, consts, pool_mats, out):
    at_byte = [(nc.sbuf_base + 31) // 32 * 32]

    def place(name, shape, dtype=F32, offset=None):
        size = 4 * int(np.prod(shape[1:]))
        if offset is None:
            offset = at_byte[0]
            at_byte[0] += (size + 31) // 32 * 32
        return nc.alloc_sbuf_tensor_at(name, shape, dtype, offset=offset)

    xres = place("xres", [P, TOK, D])
    lhs_hi = place("lhs_hi", [P, KC, S], F32R)
    lhs_lo = place("lhs_lo", [P, KC, S], F32R)
    raw = place("raw", [P, RAW, 4, N])
    w_hi = place("w_hi", [P, SPLIT, 2, N], F32R)
    w_lo = place("w_lo", [P, SPLIT, 2, N], F32R)
    mix = place("mix", [P, TOK, 2 * D])
    act_t = place("act_t", [P, KC, S])
    low_at = at_byte[0]
    low_hi = place("low_hi", [P, 8, S], F32R)
    low_lo = place("low_lo", [P, 8, S], F32R)
    qk_t = place("qk_t", [P, 16, S], offset=low_at)
    con = place("con", [P, C_END])
    cols = place("cols", [P, 16])
    small = place("small", [P, 96])
    cosd = place("cosd", [P, TOK, ROPE])
    sind = place("sind", [P, TOK, ROPE])
    krr = place("krr", [P, TOK, ROPE])
    pos_i = place("pos_i", [P, TOK], I32)
    arena_at = at_byte[0]
    arena = place("arena", [P, 6144])
    assert at_byte[0] <= nc.sbuf_base + nc.sbuf_bytes_remaining, at_byte[0]

    def part(start, *shape):
        size = int(np.prod(shape))
        ap = arena[:, start:start + size]
        if len(shape) == 2:
            return ap.rearrange("p (a b) -> p a b", a=shape[0])
        if len(shape) == 3:
            return ap.rearrange("p (a b c) -> p a b c", a=shape[0], b=shape[1])
        return ap

    gain = part(0, D)
    pool_a = part(2048, 4, 384)
    gain_cq = part(3584, N)
    gain_ckv = part(4096, N)
    junk = part(4608, N)
    q_rows = part(0, TOK, 2, QK)
    k_rows = part(768, TOK, 2, QK)
    v_rows = part(1536, TOK, 2, VDIM)
    q_tn = part(2048, 2, S)
    k_tn = part(2560, 2, S)
    p_t = part(2048, 2, 384)
    q_tr = part(3072, 2, S)
    k_tr = part(3584, 2, S)
    gate_tmp = part(3072, TOK, N)
    probs = part(4096, 2, 384)
    squares = part(4096, TOK, 2, QK)
    rope_a = part(4096, TOK, 2, ROPE)
    rope_b = part(4352, TOK, 2, ROPE)
    gain_q = part(5120, QK)
    gain_k = part(5312, QK)
    bias = part(5504, N)
    act_f = part(2048, TOK, N)
    hid = part(3072, TOK, N)
    vs = part(0, TOK, SGU)
    us = part(2048, TOK, SGU)
    vb = part(4096, TOK, SB)
    z_neg = part(0, 384)
    z_pos = part(384, 384)
    z_abs = part(768, 384)
    att = part(1152, 384)
    k_head = part(1536, S)
    v_head = part(1792, TOK, P)
    gate2_tmp = part(2048, TOK, N)
    gain_qk = mix[:, 0, D:2 * D]
    qk_rows = mix[:, 1, D:D + 1024].rearrange("p (a b) -> p a b", a=TOK)
    qk_sq = mix[:, 1, D + 1024:2 * D].rearrange("p (a b) -> p a b", a=TOK)
    ln_g, ln_b = mix[:, 0, 0:SGU], mix[:, 0, SGU:2 * SGU]
    ws_raw = mix[:, 1, 0:1024].rearrange("p (g j) -> p g j", g=GROUPS)
    ws_t = mix[:, 1, 1024:2048].rearrange("p (g i) -> p g i", g=GROUPS)
    w_grp = act_t[:, 8:16, :].rearrange("p (g c) d -> p g c d", g=4)
    cq_rows = mix[:, :, D:D + N]
    ckv_rows = mix[:, :, D + N:D + 2 * N]
    u_rows = mix[:, :, D + 2 * N:2 * D]

    ident = con[:, C_ID:C_ID + P]
    causal = con[:, C_CAUSAL:C_CAUSAL + 384]
    after = con[:, C_AFTER:C_AFTER + P]
    ones = con[:, C_ONES:C_ONES + P]
    past = con[:, C_PAST:C_PAST + P]
    freq = con[:, C_FREQ:C_FREQ + HALF]
    ss, inv = small[:, 0:8], small[:, 8:16]
    kr_ss, cq_ss, cq_inv = small[:, 16:18], small[:, 18:20], small[:, 20:22]
    row_max, row_sum, row_inv = small[:, 24:28], small[:, 28:32], small[:, 32:36]
    pos_f = small[:, 36:38]
    ln_mv, ln_inv = small[:, 40:44], small[:, 44:46]
    ln_stats = small[:, 48:72]

    pairs = [nc.alloc_psum_tensor(f"pair{i}", [P, TOK, N], F32) for i in range(2)]
    aux = nc.alloc_psum_tensor("aux", [P, 4, N], F32)
    third = aux[:, 2:4, :]

    sem = nc.alloc_semaphore
    raw_loaded = [sem(f"raw_loaded{r}") for r in range(RAW)]
    hi_ready = sem("hi_ready")
    lo_ready = sem("lo_ready")
    gran_used = sem("gran_used")
    evac_done = sem("evac_done")
    x_loaded = sem("x_loaded")
    loaded = {n: sem("loaded_" + n) for n in (
        "con", "pos", "cols", "cq", "pool", "qk", "bias", "gain", "qk2", "ln")}
    side_go = sem("side_go")
    bias_used = sem("bias_used")
    sumsq = sem("sumsq")
    ms_ready = sem("ms_ready")
    rms_ready = sem("rms_ready")
    rows_ready = sem("rows_ready")
    turned = sem("turned")
    lhs_hi_ready = sem("lhs_hi_ready")
    lhs_ready = sem("lhs_ready")
    angles = sem("angles")
    sines = sem("sines")
    pool_rows = sem("pool_rows")
    pool_mm = sem("pool_mm")
    pool_out = sem("pool_out")
    low_rows = sem("low_rows")
    low_turned = sem("low_turned")
    low_hi_ready = sem("low_hi_ready")
    low_ready = sem("low_ready")
    mix_ones = sem("mix_ones")
    kr_sq = sem("kr_sq")
    gate_in = sem("gate_in")
    gate_out = sem("gate_out")
    q_sq = sem("q_sq")
    kv_sq = sem("kv_sq")
    qk_done = sem("qk_done")
    qk_turned = sem("qk_turned")
    qk_copied = sem("qk_copied")
    scored = sem("scored")
    max_ready = sem("max_ready")
    exp_done = sem("exp_done")
    p_ready = sem("p_ready")
    p_turned = sem("p_turned")
    p_copied = sem("p_copied")
    av_done = sem("av_done")
    av_stored = sem("av_stored")
    act_ready = sem("act_ready")
    hid_ready = sem("hid_ready")
    hid_turned = sem("hid_turned")
    hid_hi_ready = sem("hid_hi_ready")
    hid_lo_ready = sem("hid_lo_ready")
    qk2_sq = sem("qk2_sq")
    qk2_ready = sem("qk2_ready")
    qk2_turned = sem("qk2_turned")
    qk2_copied = sem("qk2_copied")
    gelu_done = sem("gelu_done")
    ln_done = sem("ln_done")
    ws_turned = sem("ws_turned")
    ws_ready = sem("ws_ready")
    sgu_mm = sem("sgu_mm")
    sgu_rows = sem("sgu_rows")
    sgu_turned = sem("sgu_turned")
    sgu_copied = sem("sgu_copied")
    head_copied = sem("head_copied")
    z_done = sem("z_done")
    z_split = sem("z_split")
    z_log = sem("z_log")
    keep_ready = sem("keep_ready")
    tail_done = sem("tail_done")
    log_a = sem("log_a")
    a_exp = sem("a_exp")
    a_ready = sem("a_ready")
    out_done = sem("out_done")

    def token_rows(ap):
        return ap.rearrange("(t p) n -> p t n", p=P)

    block = nc.Block()
    with block:
        @block.sync
        def _(sp):
            def load(at, p, w, col, row0=0):
                kch, n = at.panels[p]
                for g in range(kch // 4):
                    k = 2 * g
                    sp.wait_ge(lo_ready, at.gran(p, k) + 2)
                    rows = w[bass.ds(row0 + g * 4 * P, 4 * P), bass.ds(col, n)]
                    sp.dma_start(raw[:, at.raw_slot(p, k), :, 0:n],
                                 rows.rearrange("(c p) n -> p c n", p=P)
                                 ).then_inc(raw_loaded[at.raw_slot(p, k)], 16)

            sp.dma_start(xres[:], token_rows(x[0])).then_inc(x_loaded, 16)
            w1, w2 = w_in[0], w_in_2[0]
            at = At("in")
            for p, col in enumerate((COL_POOL, COL_POOL + N, COL_KR, 0, COL_KV)):
                load(at, p, w1, col)
            with sp.Fori(0, 2) as i:
                for p in range(2):
                    load(At("pool", i), p, w_pool_o[0], i * (2 * N) + p * N)

            def sub(at, p, u):
                load(at, p, w1, u * N + COL_GATE)
                load(at, p + 1, w_q_b[0], u * (2 * QK))
                load(at, p + 2, w_kv_b[0], (u * P) * 4)

            sub(At("heads_first"), 0, 0)
            with sp.Fori(0, (PAIRS - 2) // 2) as i:
                for s in range(2):
                    sub(At("heads", i), 3 * s, i * 2 + (1 + s))
            sub(At("heads_last"), 0, PAIRS - 1)
            for name, w in (("attn_o", w_attn_o), ("out", w_out)):
                for p in range(4):
                    load(At(name), p, w[0], p * N)
            at = At("ffn_first")
            load(at, 0, w_ffn_gate[0], 0)
            load(at, 1, w_ffn_up[0], 0)
            with sp.Fori(0, NB1 - 1) as i:
                at = At("ffn", i)
                load(at, 0, w_ffn_gate[0], i * N + N)
                load(at, 1, w_ffn_up[0], i * N + N)
                for j in range(4):
                    load(at, 2 + j, w_ffn_down[0], j * N, i * N)
            for j in range(4):
                load(At("ffn_last"), j, w_ffn_down[0], j * N, (NB1 - 1) * N)

            for p in range(4):
                load(At("qk2"), p, w2, p * N)
            with sp.Fori(0, 2) as i:
                for p in range(2):
                    load(At("uv2", i), p, w2, i * (-SGU) + (COL_VS + p * N))
            for p in range(2):
                load(At("v2"), p, w2, 2 * SB + p * N)
            with sp.Fori(0, 4) as i:
                for p in range(2):
                    load(At("gates2", i), p, w2, i * (2 * N) + (COL_GATE2 + p * N))
            with sp.Fori(0, 4) as i:
                load(At("mix2", i), 0, w_oa_2[0], i * N)
                load(At("mix2", i), 1, w_ob_2[0], i * N)
            for p in range(4):
                load(At("out2"), p, w_out_2[0], p * N)
            load(At("ffn2_first"), 0, w_ff1_2[0], 0)
            with sp.Fori(0, NB2 - 1) as i:
                at = At("ffn2", i)
                load(at, 0, w_ff1_2[0], i * N + N)
                for j in range(4):
                    load(at, 1 + j, w_ff2_2[0], j * N, i * N)
            for j in range(4):
                load(At("ffn2_last"), j, w_ff2_2[0], j * N, (NB2 - 1) * N)
            last = At("ffn2_last")
            for j in range(4):
                sp.wait_ge(evac_done, last.panel(j) + 1 + EVAC_CREDIT)
                sp.dma_start(token_rows(out[0])[:, :, j * N:(j + 1) * N],
                             xres[:, :, j * N:(j + 1) * N]).then_inc(out_done, 16)
            sp.wait_ge(out_done, 4 * 16)

        @block.gpsimd
        def _(pool):
            def to_all(dst, row, what):
                pool.dma_start(dst, row.partition_broadcast(P)).then_inc(loaded[what], 16)

            pool.dma_start(con[:], consts).then_inc(loaded["con"], 16)
            to_all(gain, attn_norm_g[0], "gain")
            with nc.allow_non_contiguous_dma("a few columns"):
                pool.dma_start(pos_i[:], positions[0].rearrange("(t p) -> p t", p=P)).then_inc(loaded["pos"], 16)
                pool.dma_start(cols[:, 0:8], pool_scale[0].rearrange("g (c p) -> p (g c)", p=P)
                               ).then_inc(loaded["cols"], 16)
                pool.dma_start(cols[:, 8:16], b_spatial_2[0].rearrange("g p -> p g")).then_inc(loaded["cols"], 16)
            to_all(gain_k, k_norm_g[0], "qk")
            to_all(gain_q, q_norm_g[0], "qk")
            to_all(gain_cq, q_a_norm_g[0], "cq")
            to_all(gain_ckv, kv_a_norm_g[0], "cq")
            pool.dma_start(pool_a, pool_mats).then_inc(loaded["pool"], 16)
            pool.dma_start(w_grp, w_pool_grp[0].rearrange("g (c p) d -> p g c d", p=P)
                           ).then_inc(loaded["pool"], 16)
            pool.wait_ge(low_turned, 4)
            nc.gpsimd.memset(mix[:, :, D:2 * D], 1.0).then_inc(mix_ones, 1)
            to_all(bias, b_gate[0, 0:N], "bias")
            with pool.Fori(1, PAIRS) as u:
                pool.wait_ge(bias_used, u)
                to_all(bias, b_gate[0, bass.ds(u * N, N)], "bias")
            pool.wait_ge(side_go, 1)
            to_all(gain, ffn_norm_g[0], "gain")
            pool.wait_ge(side_go, 2)
            to_all(gain, g_mix_2[0], "gain")
            to_all(gain_qk[:, 0:SB], g_q_2[0].rearrange("h d -> (h d)"), "qk2")
            to_all(gain_qk[:, SB:2 * SB], g_k_2[0].rearrange("h d -> (h d)"), "qk2")
            pool.wait_ge(side_go, 3)
            to_all(ln_g, sgu_ln_g_2[0], "ln")
            to_all(ln_b, sgu_ln_b_2[0], "ln")
            pool.dma_start(ws_raw, w_spatial_2[0].rearrange("g i j -> i g j")).then_inc(loaded["ln"], 16)
            pool.wait_ge(side_go, 4)
            to_all(gain, g_ff_2[0], "gain")

        @block.scalar
        def _(act):
            def hi(at, p, k0, k1, after_panel=None):
                for k in range(k0, k1):
                    width = at.panels[p][1] if after_panel is None else after_panel
                    act.wait_ge(raw_loaded[at.raw_slot(p, k)], at.loads(p, k))
                    act.wait_ge(gran_used, at.gran(p, k) + 1)
                    h = (at.gran0 + at.starts[p] + k) % 2
                    nc.scalar.activation(w_hi[:, at.slot(p, k), :, 0:width],
                                         raw[:, at.raw_slot(p, k), 2 * h:2 * h + 2, 0:width],
                                         ACT.Copy).then_inc(hi_ready, 1)

            def panel_done(at, p):
                act.wait_ge(gran_used, at.end(p) + SPLIT)

            def root(n_before, dst, src):
                act.wait_ge(ms_ready, n_before + 1)
                nc.scalar.activation(dst, src, ACT.Sqrt).then_inc(rms_ready, 1)

            def norm(r, n_roots, stage=None):
                if stage:
                    act.wait_ge(evac_done, At(stage).panel(0) + EVAC_CREDIT)
                nc.scalar.activation(mix[:, 0, 0:D], xres[:, 0, :], ACT.Square,
                                     accum_out=ss[:, 0:1])
                act.drain().then_inc(sumsq, 1)
                root(n_roots, inv[:, 0:2], inv[:, 0:2])

            def fill_piece(r, f, p):
                act.wait_ge(turned, 8 * r + p + 1)
                kq, t = p // 2, p % 2
                nc.scalar.activation(lhs_hi[:, 4 * kq:4 * kq + 4, t * P:(t + 1) * P],
                                     aux[:, p % 4, :].rearrange("p (c t) -> p c t", c=4),
                                     ACT.Copy).then_inc(lhs_hi_ready, 1)

            def fill(r, f, at):
                for p in range(4):
                    fill_piece(r, f, p)
                for kq in (2, 3):
                    hi(at, 0, 2 * kq, 2 * kq + 2)
                    fill_piece(r, f, 2 * kq)
                    fill_piece(r, f, 2 * kq + 1)

            def refill(f, at):
                for kq in range(4):
                    if kq >= 2:
                        hi(at, 0, 2 * kq, 2 * kq + 2)
                    nc.scalar.activation(lhs_hi[:, 4 * kq:4 * kq + 4, :], act_t[:, 4 * kq:4 * kq + 4, :],
                                         ACT.Copy).then_inc(lhs_hi_ready, 1)

            act.sem_inc(gran_used, SPLIT)
            act.wait_ge(angles, 1)
            nc.scalar.activation(cosd[:, :, 0:HALF], cosd[:, :, HALF:ROPE], ACT.Sin)
            nc.scalar.activation(sind[:, :, HALF:ROPE], sind[:, :, 0:HALF], ACT.Sin)
            act.drain().then_inc(sines, 1)

            at = At("in")
            act.wait_ge(x_loaded, 16)
            norm(0, 0)
            hi(at, 0, 0, 4)
            fill(0, 0, at)
            for p in range(1, 5):
                hi(at, p, 0, 4)
                if p == 4:
                    panel_done(at, 3)
                    for t in range(TOK):
                        nc.scalar.activation(junk, pairs[at.pair(3)][:, t, :], ACT.Square,
                                             accum_out=cq_ss[:, t:t + 1])
                        act.drain()
                    act.sem_inc(sumsq, 1)
                    root(1, cq_inv, cq_inv)
                if p == 3:
                    panel_done(at, 2)
                    for t in range(TOK):
                        nc.scalar.activation(junk[:, 0:ROPE], pairs[at.pair(2)][:, t, 0:ROPE], ACT.Square,
                                             accum_out=kr_ss[:, t:t + 1])
                        act.drain()
                    act.sem_inc(kr_sq, 1)
                hi(at, p, 4, 8)
                if p == 4:
                    for b in range(4):
                        act.wait_ge(pool_mm, b + 1)
                        nc.scalar.activation(act_t[:, 2 * b:2 * b + 2, :],
                                             aux[:, b, :].rearrange("p (c t) -> p c t", c=2), ACT.Copy)
                    act.drain().then_inc(pool_out, 1)
            nxt = At("pool")
            hi(nxt, 0, 0, 4)
            panel_done(at, 4)
            for t in range(TOK):
                nc.scalar.activation(junk, pairs[at.pair(4)][:, t, :], ACT.Square, accum_out=cq_ss[:, t:t + 1])
                act.drain()
            act.sem_inc(sumsq, 1)
            root(2, cq_inv, cq_inv)
            for j in range(8):
                act.wait_ge(pool_mm, 4 + j // 2 + 1)
                act.wait_ge(loaded["cols"], 32)
                nc.scalar.activation(low_hi[:, j, :], aux[:, j // 2, (j % 2) * S:(j % 2 + 1) * S], ACT.Copy,
                                     scale=cols[:, j:j + 1]).then_inc(low_hi_ready, 1)
            with act.Fori(0, 2) as i:
                at = At("pool", i)
                for p in range(2):
                    hi(at, p, 4, 8)
            for q in range(4):
                act.wait_ge(low_turned, q + 1)
                c0, t = 4 * (q // 2), q % 2
                nc.scalar.activation(low_hi[:, c0:c0 + 4, t * P:(t + 1) * P],
                                     aux[:, q, :].rearrange("p (c t) -> p c t", c=4),
                                     ACT.Copy).then_inc(low_hi_ready, 1)

            def attend_a(u):
                root(u + 2, inv, inv)

            def attend_b(u):
                act.wait_ge(qk_turned, u)
                nc.scalar.activation(q_tn, aux[:, 0, :].rearrange("p (h t) -> p h t", h=2), ACT.Copy)
                nc.scalar.activation(k_tn, aux[:, 1, :].rearrange("p (h t) -> p h t", h=2), ACT.Copy)
                nc.scalar.activation(q_tr[0:ROPE], aux[0:ROPE, 2, :].rearrange("p (h t) -> p h t", h=2), ACT.Copy)
                nc.scalar.activation(k_tr[0:ROPE], aux[0:ROPE, 3, :].rearrange("p (h t) -> p h t", h=2), ACT.Copy)
                act.drain().then_inc(qk_copied, 1)

            def attend_c(u):
                act.wait_ge(max_ready, u)
                for h in range(2):
                    for t in range(TOK):
                        c = slice(0, P) if t == 0 else slice(P, 3 * P)
                        nc.scalar.activation(probs[:, h, c], probs[:, h, c], ACT.Exp,
                                             bias=row_max[:, 2 * t + h:2 * t + h + 1],
                                             accum_out=row_sum[:, 2 * t + h:2 * t + h + 1])
                act.drain().then_inc(exp_done, 1)

            def attend_d(u):
                act.wait_ge(p_turned, u)
                nc.scalar.activation(p_t, aux[:, 2:4, 0:384], ACT.Copy).then_inc(p_copied, 1)

            def attend_e(u):
                act.wait_ge(av_done, u)
                nc.scalar.activation(act_t[:, bass.ds(u * 2 - 2, 2), :],
                                     aux[:, 0, :].rearrange("p (h t) -> p h t", h=2), ACT.Copy
                                     ).then_inc(av_stored, 1)

            def rows_q(at, p, u):
                panel_done(at, p)
                nc.scalar.activation(squares, pairs[at.pair(p)][:, :, 0:2 * QK].rearrange(
                    "p t (h d) -> p t h d", h=2), ACT.Square).then_inc(q_sq, 1)

            def rows_kv(at, p, u):
                panel_done(at, p)
                kv = pairs[at.pair(p)][:].rearrange("p t (h d) -> p t h d", h=2)
                act.wait_ge(q_sq, u * 2 + 2)
                nc.scalar.activation(squares[:, :, :, 0:NOPE], kv[:, :, :, 0:NOPE], ACT.Square)
                nc.scalar.activation(v_rows, kv[:, :, :, NOPE:NOPE + VDIM], ACT.Copy)
                act.drain().then_inc(kv_sq, 1)

            def sub(at, p, u, has_last):
                if has_last:
                    attend_a(u)
                hi(at, p, 4, 6)
                hi(at, p, 6, 8)
                if has_last:
                    attend_b(u)
                hi(at, p + 1, 0, 2)
                if has_last:
                    attend_c(u)
                hi(at, p + 2, 0, 2)
                if has_last:
                    attend_d(u)
                act.wait_ge(gate_in, u + 1)
                nc.scalar.activation(gate_tmp, gate_tmp, ACT.Sigmoid).then_inc(gate_out, 1)
                rows_q(at, p + 1, u)
                if has_last:
                    attend_e(u)
                hi(at, p + 2, 2, 4, N)
                rows_kv(at, p + 2, u)
                hi(at, p + 2, 4, 6, N)

            sub(At("heads_first"), 0, 0, False)
            with act.Fori(0, (PAIRS - 2) // 2) as i:
                for s in range(2):
                    sub(At("heads", i), 3 * s, i * 2 + (1 + s), True)
            sub(At("heads_last"), 0, PAIRS - 1, True)
            attend_a(PAIRS)
            attend_b(PAIRS)
            attend_c(PAIRS)
            attend_d(PAIRS)
            attend_e(PAIRS)
            act.drain()

            at = At("attn_o")
            refill(1, at)
            for p in range(4):
                if p:
                    hi(at, p, 4, 8)
                hi(at, p, 8, 12)
            at = At("out")
            fill(1, 2, at)
            for p in range(4):
                if p:
                    hi(at, p, 4, 8)
                hi(at, p, 8, 12)

            def hid_turn(b):
                for t in range(TOK):
                    act.wait_ge(hid_turned, b * 2 + t + 1)
                    nc.scalar.activation(low_hi[:, 0:4, t * P:(t + 1) * P],
                                         aux[:, t, :].rearrange("p (c t) -> p c t", c=4),
                                         ACT.Copy).then_inc(hid_hi_ready, 1)

            def gate_function(at, p, b, func, src):
                panel_done(at, p)
                act.wait_ge(hid_ready, b + 1)
                nc.scalar.activation(act_f, src, func).then_inc(act_ready, 1)

            act.sem_inc(hid_ready, 1)
            norm(2, 11, "ffn_first")
            at = At("ffn_first")
            fill(2, 3, at)
            hi(at, 1, 0, 4)
            gate_function(at, 0, 0, ACT.Sigmoid, pairs[at.pair(0)][:])
            hi(at, 1, 4, 8)
            hi(at, 1, 8, 12)
            hid_turn(0)
            with act.Fori(0, NB1 - 1) as i:
                at = At("ffn", i)
                hi(at, 0, 4, 8)
                hi(at, 1, 0, 4)
                gate_function(at, 0, i + 1, ACT.Sigmoid, pairs[at.pair(0)][:])
                hi(at, 1, 4, 8)
                for j in range(4):
                    hi(at, 2 + j, 0, 2)
                hi(at, 5, 2, 6)
                hid_turn(i + 1)
            at = At("ffn_last")
            hi(at, 0, 4, 12)

            norm(3, 12, "qk2")
            at = At("qk2")
            fill(3, 4, at)
            for p in range(4):
                if p:
                    hi(at, p, 4, 8)
                hi(at, p, 8, 12)
                panel_done(at, p)
                act.wait_ge(qk2_sq, 2 * p + 1)
                nc.scalar.activation(qk_sq, pairs[at.pair(p)][:], ACT.Square).then_inc(qk2_sq, 1)
                root(13 + p, inv, inv)
                for t in range(TOK):
                    act.wait_ge(qk2_turned, 2 * p + t + 1)
                    nc.scalar.activation(qk_t[:, 4 * p:4 * p + 4, t * P:(t + 1) * P],
                                         aux[:, t, :].rearrange("p (c t) -> p c t", c=4),
                                         ACT.Copy).then_inc(qk2_copied, 1)
            with act.Fori(0, 2) as i:
                at = At("uv2", i)
                for p in range(2):
                    hi(at, p, 4, 12)
                    panel_done(at, p)
                    nc.scalar.activation(arena[:, bass.ds(i * 2048, 2048)].rearrange(
                        "p (t n) -> p t n", t=TOK)[:, :, p * N:(p + 1) * N],
                        pairs[at.pair(p)][:], ACT.Gelu).then_inc(gelu_done, 1)
            at = At("v2")
            for p in range(2):
                hi(at, p, 4, 12)
                if p == 0:
                    root(17, ln_inv, ln_inv)
                panel_done(at, p)
                nc.scalar.activation(vb[:, :, p * N:(p + 1) * N], pairs[at.pair(p)][:],
                                     ACT.Copy).then_inc(gelu_done, 1)
                if p == 0:
                    act.wait_ge(ws_turned, 1)
                    for b in range(2):
                        nc.scalar.activation(ws_t[:, 4 * b:4 * b + 4, :],
                                             aux[:, b, :].rearrange("p (g i) -> p g i", g=4), ACT.Copy)
                    act.drain().then_inc(ws_ready, 1)
            for b in range(4):
                act.wait_ge(sgu_turned, b + 1)
                nc.scalar.activation(act_t[:, 8 + 2 * b:10 + 2 * b, :],
                                     aux[:, b, :].rearrange("p (c t) -> p c t", c=2), ACT.Copy)
            act.drain().then_inc(sgu_copied, 1)

            with act.Fori(0, 4) as i:
                at = At("gates2", i)
                for p in range(2):
                    head = i * 2 + p
                    act.wait_ge(av_stored, head + PAIRS)
                    nc.scalar.activation(k_head, qk_t[:, bass.ds(head + 8, 1), :].rearrange("p a t -> p (a t)"), ACT.Copy)
                    nc.scalar.activation(v_head, vb[:, :, bass.ds(head * P, P)], ACT.Copy)
                    act.drain().then_inc(head_copied, 1)
                    hi(at, p, 4, 6)
                    act.wait_ge(z_done, head + 1)
                    nc.scalar.activation(z_abs, aux[:, 0, 0:384], ACT.Abs, scale=SB_SCALE)
                    act.drain().then_inc(z_split, 1)
                    nc.scalar.activation(z_abs, z_abs, ACT.Exp, scale=-1.0)
                    act.drain()
                    nc.scalar.activation(z_abs, z_abs, ACT.Ln, bias=1.0).then_inc(z_log, 1)
                    hi(at, p, 6, 8)
                    act.wait_ge(log_a, head + 1)
                    nc.scalar.activation(att, z_neg, ACT.Exp).then_inc(a_exp, 1)
                    hi(at, p, 8, 10)
                    act.wait_ge(av_done, head + PAIRS + 1)
                    nc.scalar.activation(act_t[:, bass.ds(head, 1), :].rearrange("p a t -> p (a t)"),
                                         aux[:, 2, 0:S], ACT.Copy).then_inc(av_stored, 1)
                    hi(at, p, 10, 12)
                    act.wait_ge(gate_in, head + PAIRS + 1)
                    nc.scalar.activation(gate2_tmp, gate2_tmp, ACT.Sigmoid).then_inc(gate_out, 1)
            act.drain()
            at = At("mix2")
            refill_at = at
            for kq in range(4):
                if kq >= 2:
                    hi(refill_at, 0, 2 * kq, 2 * kq + 2)
                nc.scalar.activation(lhs_hi[:, 4 * kq:4 * kq + 4, :], act_t[:, 4 * kq:4 * kq + 4, :],
                                     ACT.Copy).then_inc(lhs_hi_ready, 1)
            hi(at, 0, 8, 12)
            with act.Fori(1, 4) as i:
                hi(At("mix2", i), 0, 4, 8)
                hi(At("mix2", i), 0, 8, 12)
            at = At("out2")
            fill(4, 6, at)
            for p in range(4):
                if p:
                    hi(at, p, 4, 8)
                hi(at, p, 8, 12)

            norm(5, 18, "ffn2_first")
            at = At("ffn2_first")
            fill(5, 7, at)
            hi(at, 0, 8, 12)
            gate_function(at, 0, NB1, ACT.Relu, pairs[0][:])
            hid_turn(NB1)
            with act.Fori(0, NB2 - 1) as i:
                at = At("ffn2", i)
                hi(at, 0, 4, 8)
                hi(at, 1, 0, 4)
                gate_function(at, 0, i + (NB1 + 1), ACT.Relu, third)
                hi(at, 1, 4, 8)
                hi(at, 4, 2, 6)
                hid_turn(i + (NB1 + 1))
            at = At("ffn2_last")
            hi(at, 0, 4, 8)

        @block.vector
        def _(dve):
            v = nc.vector

            def lo(at, p, k0, k1, width=None):
                for k in range(k0, k1):
                    n = at.panels[p][1] if width is None else width
                    h = (at.gran0 + at.starts[p] + k) % 2
                    dve.wait_ge(hi_ready, at.gran(p, k) + 1)
                    v.tensor_tensor(w_lo[:, at.slot(p, k), :, 0:n],
                                    raw[:, at.raw_slot(p, k), 2 * h:2 * h + 2, 0:n],
                                    w_hi[:, at.slot(p, k), :, 0:n].bitcast(F32),
                                    ALU.subtract).then_inc(lo_ready, 1)

            def panel_done(at, p):
                dve.wait_ge(gran_used, at.end(p) + SPLIT)

            def inverse_root(n_roots, dst, src, count):
                v.tensor_scalar(dst, src, 1.0 / count, EPS, ALU.mult, ALU.add).then_inc(ms_ready, 1)
                dve.wait_ge(rms_ready, n_roots + 1)
                v.reciprocal(dst, dst)
                dve.drain()

            def norm(n_sums, n_roots):
                v.tensor_tensor(mix[:, 1, 0:D], xres[:, 1, :], xres[:, 1, :], ALU.mult)
                dve.drain()
                v.tensor_reduce(ss[:, 1:2], mix[:, 1, 0:D], AX.X, ALU.add)
                dve.drain()
                dve.wait_ge(sumsq, n_sums + 1)
                inverse_root(n_roots, inv[:, 0:2], ss[:, 0:2], D)

            def norm_rows(p):
                kq, t = p // 2, p % 2
                c = slice(kq * N, (kq + 1) * N)
                v.scalar_tensor_tensor(mix[:, t, c], xres[:, t, c], inv[:, t:t + 1], gain[:, c],
                                       ALU.mult, ALU.mult).then_inc(rows_ready, 1)

            def fill_piece(f, p, n_hi):
                kq, t = p // 2, p % 2
                dst = slice(t * P, (t + 1) * P)
                dve.wait_ge(lhs_hi_ready, n_hi + p + 1)
                v.tensor_tensor(lhs_lo[:, 4 * kq:4 * kq + 4, dst],
                                aux[:, p % 4, :].rearrange("p (c t) -> p c t", c=4),
                                lhs_hi[:, 4 * kq:4 * kq + 4, dst].bitcast(F32),
                                ALU.subtract).then_inc(lhs_ready, 1)

            def fill(f, at, n_hi, rows):
                if rows:
                    for p in range(4):
                        norm_rows(p)
                fill_piece(f, 0, n_hi)
                fill_piece(f, 1, n_hi)
                if rows:
                    norm_rows(4)
                    norm_rows(5)
                fill_piece(f, 2, n_hi)
                fill_piece(f, 3, n_hi)
                lo(at, 0, 4, 6)
                if rows:
                    norm_rows(6)
                    norm_rows(7)
                fill_piece(f, 4, n_hi)
                fill_piece(f, 5, n_hi)
                lo(at, 0, 6, 8)
                fill_piece(f, 6, n_hi)
                fill_piece(f, 7, n_hi)

            def refill(at, n_hi):
                for kq in range(4):
                    if kq >= 2:
                        lo(at, 0, 2 * kq, 2 * kq + 2)
                    dve.wait_ge(lhs_hi_ready, n_hi + kq + 1)
                    c = slice(4 * kq, 4 * kq + 4)
                    v.tensor_tensor(lhs_lo[:, c, :], act_t[:, c, :], lhs_hi[:, c, :].bitcast(F32),
                                    ALU.subtract).then_inc(lhs_ready, 2)

            def rope(dst, src, tmp_a, tmp_b, heads):
                def table(t):
                    return t if heads is None else t.unsqueeze(2).broadcast_to([P, TOK, heads, ROPE])
                def halves(ap):
                    if heads is None:
                        return ap[:, :, 0:HALF], ap[:, :, HALF:ROPE]
                    return ap[:, :, :, 0:HALF], ap[:, :, :, HALF:ROPE]
                c, s = table(cosd[:]), table(sind[:])
                v.tensor_tensor(tmp_a, src, c, ALU.mult)
                v.tensor_tensor(halves(tmp_b)[0], halves(src)[1], halves(s)[0], ALU.mult)
                v.tensor_tensor(halves(tmp_b)[1], halves(src)[0], halves(s)[1], ALU.mult)
                dve.drain()
                v.tensor_tensor(dst, tmp_a, tmp_b, ALU.add)
                dve.drain()

            dve.sem_inc(lo_ready, LO_CREDIT)
            dve.sem_inc(evac_done, EVAC_CREDIT)
            dve.wait_ge(loaded["con"], 16)
            dve.wait_ge(loaded["pos"], 16)
            v.tensor_copy(pos_f, pos_i[:])
            dve.drain()
            ang, turns = junk[:, 0:64].rearrange("p (t f) -> p t f", t=TOK), junk[:, 64:128].rearrange(
                "p (t f) -> p t f", t=TOK)
            for t in range(TOK):
                v.tensor_scalar(ang[:, t, :], freq, pos_f[:, t:t + 1], None, ALU.mult)
            dve.drain()
            v.tensor_scalar(turns, ang, float(1 / TWO_PI), MAGIC, ALU.mult, ALU.add)
            dve.drain()
            v.tensor_scalar(turns, turns, -MAGIC, None, ALU.add)
            dve.drain()
            for c in (PI_1, PI_2, PI_3):
                v.scalar_tensor_tensor(ang, turns, -float(c), ang, ALU.mult, ALU.add)
                dve.drain()
            v.tensor_scalar(sind[:, :, 0:HALF], ang, PI_MAX, -PI_MAX, ALU.min, ALU.max)
            v.tensor_scalar(ang, ang, float(TWO_PI / 4), None, ALU.add)
            dve.drain()
            v.tensor_scalar(turns, ang, float(TWO_PI / 2), -float(TWO_PI), ALU.is_gt, ALU.mult)
            dve.drain()
            v.tensor_tensor(ang, ang, turns, ALU.add)
            dve.drain()
            v.tensor_scalar(cosd[:, :, HALF:ROPE], ang, PI_MAX, -PI_MAX, ALU.min, ALU.max)
            dve.drain().then_inc(angles, 1)
            dve.wait_ge(sines, 1)
            v.tensor_copy(cosd[:, :, HALF:ROPE], cosd[:, :, 0:HALF])
            v.tensor_scalar(sind[:, :, 0:HALF], sind[:, :, HALF:ROPE], -1.0, None, ALU.mult)

            at = At("in")
            dve.wait_ge(x_loaded, 16)
            dve.wait_ge(loaded["gain"], 16)
            norm(0, 0)
            lo(at, 0, 0, 4)
            fill(0, at, 0, True)

            def low_norm(p, n_sums, n_roots, gains, rows):
                dve.wait_ge(sumsq, n_sums + 1)
                inverse_root(n_roots, cq_inv, cq_ss, Q_RANK)
                for t in range(TOK):
                    ins = v.scalar_tensor_tensor(rows[:, t, :], pairs[at.pair(p)][:, t, :],
                                                 cq_inv[:, t:t + 1], gains, ALU.mult, ALU.mult)
                dve.drain().then_inc(evac_done, 1)

            for p in range(1, 5):
                lo(at, p, 0, 4)
                panel_done(at, p - 1)
                if p <= 2:
                    v.tensor_copy(u_rows[:, :, (p - 1) * N:p * N], pairs[at.pair(p - 1)][:]).then_inc(evac_done, 1)
                if p == 3:
                    dve.wait_ge(loaded["qk"], 32)
                    dve.wait_ge(kr_sq, 1)
                    g = gain_k[:, NOPE:QK].unsqueeze(1).broadcast_to([P, TOK, ROPE])
                    v.tensor_tensor(krr[:], pairs[at.pair(2)][:, :, 0:ROPE], g, ALU.mult).then_inc(evac_done, 1)
                    dve.drain()
                    ta = junk[:, 128:256].rearrange("p (t f) -> p t f", t=TOK)
                    tb = junk[:, 256:384].rearrange("p (t f) -> p t f", t=TOK)
                    rope(krr[:], krr[:], ta, tb, None)
                if p == 4:
                    dve.wait_ge(loaded["cq"], 32)
                    low_norm(3, 1, 1, gain_cq, cq_rows)
                lo(at, p, 4, 8)
            nxt = At("pool")
            lo(nxt, 0, 0, 4)
            panel_done(at, 4)
            low_norm(4, 2, 2, gain_ckv, ckv_rows)
            dve.sem_inc(low_rows, 1)
            for j in range(8):
                dve.wait_ge(low_hi_ready, j // 2 * 2 + 2)
                v.scalar_tensor_tensor(low_lo[:, j, :], aux[:, j // 2, (j % 2) * S:(j % 2 + 1) * S],
                                       cols[:, j:j + 1], low_hi[:, j, :].bitcast(F32),
                                       ALU.mult, ALU.subtract).then_inc(low_ready, 1)
            with dve.Fori(0, 2) as i:
                at = At("pool", i)
                for p in range(2):
                    lo(at, p, 4, 8)
                    panel_done(at, p)
                    v.tensor_copy(mix[:, :, bass.ds(i * (2 * N) + p * N, N)], pairs[at.pair(p)][:]
                                  ).then_inc(evac_done, 1)
            for q in range(4):
                dve.wait_ge(low_hi_ready, 8 + q + 1)
                c0, t = 4 * (q // 2), q % 2
                v.tensor_tensor(low_lo[:, c0:c0 + 4, t * P:(t + 1) * P],
                                aux[:, q, :].rearrange("p (c t) -> p c t", c=4),
                                low_hi[:, c0:c0 + 4, t * P:(t + 1) * P].bitcast(F32),
                                ALU.subtract).then_inc(low_ready, 1)

            def per_head(first, n):
                return inv[:, first:first + 4].rearrange("p (t h) -> p t h", t=TOK).unsqueeze(3).broadcast_to(
                    [P, TOK, 2, n])

            def attend_a(u):
                v.tensor_tensor(ss[:, 4:8].rearrange("p (t h) -> p t h", t=TOK),
                                ss[:, 4:8].rearrange("p (t h) -> p t h", t=TOK),
                                kr_ss.unsqueeze(2).broadcast_to([P, TOK, 2]), ALU.add)
                dve.drain()
                inverse_root(u + 2, inv, ss, QK)
                v.tensor_tensor(q_rows, q_rows, per_head(0, QK), ALU.mult)
                v.tensor_tensor(k_rows[:, :, :, 0:NOPE], k_rows[:, :, :, 0:NOPE], per_head(4, NOPE), ALU.mult)
                v.tensor_tensor(k_rows[:, :, :, NOPE:QK], krr[:].unsqueeze(2).broadcast_to([P, TOK, 2, ROPE]),
                                per_head(4, ROPE), ALU.mult)
                dve.drain()

            def attend_b(u):
                qr = q_rows[:, :, :, NOPE:QK]
                rope(qr, qr, rope_a, rope_b, 2)
                dve.sem_inc(qk_done, 1)

            def attend_c(u):
                dve.wait_ge(scored, u)
                v.scalar_tensor_tensor(probs, aux[:, 0:2, 0:384], SM_SCALE,
                                       causal.unsqueeze(1).broadcast_to([P, 2, 384]), ALU.mult, ALU.add)
                dve.drain()
                v.tensor_reduce(row_max[:, 0:2], probs[:, :, 0:P], AX.X, ALU.max)
                v.tensor_reduce(row_max[:, 2:4], probs[:, :, P:3 * P], AX.X, ALU.max)
                dve.drain()
                v.tensor_scalar(row_max, row_max, -1.0, None, ALU.mult).then_inc(max_ready, 1)
                dve.wait_ge(exp_done, u)
                v.reciprocal(row_inv, row_sum)
                dve.drain()
                v.tensor_tensor(probs[:, :, 0:P], probs[:, :, 0:P],
                                row_inv[:, 0:2].unsqueeze(2).broadcast_to([P, 2, P]), ALU.mult)
                v.tensor_tensor(probs[:, :, P:3 * P], probs[:, :, P:3 * P],
                                row_inv[:, 2:4].unsqueeze(2).broadcast_to([P, 2, 2 * P]), ALU.mult)
                dve.drain().then_inc(p_ready, 1)

            def sub(at, p, u, has_last):
                if has_last:
                    attend_a(u)
                lo(at, p, 4, 6)
                if has_last:
                    attend_b(u)
                lo(at, p, 6, 8)
                lo(at, p + 1, 0, 2)
                if has_last:
                    attend_c(u)
                lo(at, p + 2, 0, 2)
                panel_done(at, p)
                dve.wait_ge(loaded["bias"], u * 16 + 16)
                v.tensor_tensor(gate_tmp, pairs[at.pair(p)][:], bias.unsqueeze(1).broadcast_to([P, TOK, N]),
                                ALU.add)
                dve.drain().then_inc(evac_done, 1)
                dve.sem_inc(gate_in, 1)
                dve.sem_inc(bias_used, 1)
                dve.wait_ge(q_sq, u * 2 + 1)
                gq = gain_q.unsqueeze(1).broadcast_to([P, 2 * TOK, QK])
                v.tensor_reduce(ss[:, 0:4].rearrange("p (t h) -> p t h", t=TOK), squares, AX.X, ALU.add)
                dve.drain().then_inc(q_sq, 1)
                qp = pairs[at.pair(p + 1)][:, :, 0:2 * QK].rearrange("p t (h d) -> p t h d", h=2)
                v.tensor_tensor(q_rows, qp, gain_q.unsqueeze(1).unsqueeze(1).broadcast_to([P, TOK, 2, QK]),
                                ALU.mult)
                dve.drain().then_inc(evac_done, 1)
                lo(at, p + 2, 2, 4, N)
                dve.wait_ge(gate_out, u + 1)
                m = mix[:, :, bass.ds(u * N, N)]
                v.tensor_tensor(m, m, gate_tmp, ALU.mult)
                dve.wait_ge(kv_sq, u + 1)
                v.tensor_reduce(ss[:, 4:8].rearrange("p (t h) -> p t h", t=TOK), squares[:, :, :, 0:NOPE],
                                AX.X, ALU.add)
                kp = pairs[at.pair(p + 2)][:].rearrange("p t (h d) -> p t h d", h=2)[:, :, :, 0:NOPE]
                v.tensor_tensor(k_rows[:, :, :, 0:NOPE], kp,
                                gain_k[:, 0:NOPE].unsqueeze(1).unsqueeze(1).broadcast_to([P, TOK, 2, NOPE]),
                                ALU.mult)
                dve.drain().then_inc(evac_done, 1)
                lo(at, p + 2, 4, 6, N)

            dve.wait_ge(mix_ones, 1)
            sub(At("heads_first"), 0, 0, False)
            with dve.Fori(0, (PAIRS - 2) // 2) as i:
                for s in range(2):
                    sub(At("heads", i), 3 * s, i * 2 + (1 + s), True)
            sub(At("heads_last"), 0, PAIRS - 1, True)
            attend_a(PAIRS)
            attend_b(PAIRS)
            attend_c(PAIRS)

            def add_branch(pair, col):
                a = mix[:, :, bass.ds(col + D, N)]
                m = mix[:, :, bass.ds(col, N)]
                v.tensor_tensor(a, a, pairs[pair][:], ALU.mult)
                dve.drain().then_inc(evac_done, 1)
                v.tensor_tensor(m, m, a, ALU.add)
                dve.drain()

            def add_x(at, p, col, pair=None):
                panel_done(at, p)
                xs = xres[:, :, col:col + N]
                ps = pairs[at.pair(p) if pair is None else pair][:]
                v.tensor_tensor(xs, xs, ps, ALU.add)
                dve.drain().then_inc(evac_done, 1)

            at = At("attn_o")
            refill(at, 8)
            dve.sem_inc(side_go, 1)
            for p in range(4):
                if p:
                    lo(at, p, 4, 8)
                lo(at, p, 8, 12)
                panel_done(at, p)
                add_branch(at.pair(p), p * N)
            dve.sem_inc(rows_ready, 8)
            at = At("out")
            fill(2, at, 12, False)
            for p in range(4):
                if p:
                    lo(at, p, 4, 8)
                lo(at, p, 8, 12)
                add_x(at, p, p * N)

            def hid_turn(b):
                for t in range(TOK):
                    dve.wait_ge(hid_hi_ready, b * 2 + t + 1)
                    v.tensor_tensor(low_lo[:, 0:4, t * P:(t + 1) * P],
                                    aux[:, t, :].rearrange("p (c t) -> p c t", c=4),
                                    low_hi[:, 0:4, t * P:(t + 1) * P].bitcast(F32),
                                    ALU.subtract).then_inc(hid_lo_ready, 1)

            def silu_gate(at, p, b):
                dve.wait_ge(act_ready, b + 1)
                v.tensor_tensor(hid, pairs[at.pair(p)][:], act_f, ALU.mult)
                dve.drain().then_inc(evac_done, 1)

            def times_up(at, p):
                panel_done(at, p)
                v.tensor_tensor(hid, hid, pairs[at.pair(p)][:], ALU.mult)
                dve.drain().then_inc(evac_done, 1)
                dve.sem_inc(hid_ready, 1)

            norm(3, 11)
            dve.wait_ge(loaded["gain"], 32)
            at = At("ffn_first")
            fill(3, at, 20, True)
            dve.drain()
            dve.sem_inc(side_go, 1)
            lo(at, 1, 0, 4)
            silu_gate(at, 0, 0)
            lo(at, 1, 4, 8)
            lo(at, 1, 8, 12)
            times_up(at, 1)
            hid_turn(0)
            with dve.Fori(0, NB1 - 1) as i:
                at = At("ffn", i)
                lo(at, 0, 4, 8)
                lo(at, 1, 0, 4)
                silu_gate(at, 0, i + 1)
                lo(at, 1, 4, 8)
                lo(at, 2, 0, 2)
                lo(at, 3, 0, 2)
                times_up(at, 1)
                for j in range(4):
                    lo(at, 2 + j, 4, 6)
                    add_x(at, 2 + j, j * N)
                hid_turn(i + 1)
            at = At("ffn_last")
            for j in range(4):
                lo(at, j, 4, 6)
                add_x(at, j, j * N)

            dve.sem_inc(qk2_sq, 1)
            norm(4, 12)
            dve.wait_ge(loaded["gain"], 48)
            at = At("qk2")
            fill(4, at, 28, True)
            dve.drain()
            dve.sem_inc(side_go, 1)
            dve.wait_ge(loaded["qk2"], 32)
            for p in range(4):
                if p:
                    lo(at, p, 4, 8)
                lo(at, p, 8, 12)
                dve.wait_ge(qk2_sq, 2 * p + 2)
                v.tensor_reduce(ss.rearrange("p (t h) -> p t h", t=TOK),
                                qk_sq.rearrange("p t (h d) -> p t h d", h=4), AX.X, ALU.add)
                dve.drain().then_inc(qk2_sq, 1)
                inverse_root(13 + p, inv, ss, P)
                rows = qk_rows.rearrange("p t (h d) -> p t h d", h=4)
                v.tensor_tensor(rows, pairs[at.pair(p)][:].rearrange("p t (h d) -> p t h d", h=4),
                                inv.rearrange("p (t h) -> p t h", t=TOK).unsqueeze(3).broadcast_to(
                                    [P, TOK, 4, P]), ALU.mult)
                dve.drain().then_inc(evac_done, 1)
                v.tensor_tensor(qk_rows, qk_rows, gain_qk[:, p * N:(p + 1) * N].unsqueeze(1).broadcast_to(
                    [P, TOK, N]), ALU.mult)
                dve.drain().then_inc(qk2_ready, 1)
                dve.wait_ge(qk2_turned, 2 * p + 2)
            with dve.Fori(0, 2) as i:
                at = At("uv2", i)
                for p in range(2):
                    lo(at, p, 4, 12)
                    dve.wait_ge(gelu_done, i * 2 + p + 1)
                    dve.sem_inc(evac_done, 1)

            def layer_norm():
                st = ln_stats.rearrange("p (t c s) -> p t c s", t=TOK, c=2)
                for t in range(TOK):
                    for c in range(2):
                        v.bn_stats(st[:, t, c, :], vs[:, t, c * N:(c + 1) * N])
                dve.drain()
                for t in range(TOK):
                    v.bn_aggr(ln_mv[:, 2 * t:2 * t + 2], st[:, t, :, :])
                dve.drain()
                inverse_root(17, ln_inv, ln_mv.rearrange("p (t s) -> p s t", s=2)[:, 1, :], 1)
                for t in range(TOK):
                    v.tensor_scalar(vs[:, t, :], vs[:, t, :], ln_mv[:, 2 * t:2 * t + 1], ln_inv[:, t:t + 1],
                                    ALU.subtract, ALU.mult)
                dve.drain()

            at = At("v2")
            lo(at, 0, 4, 12)
            layer_norm()
            dve.wait_ge(gelu_done, 5)
            dve.sem_inc(evac_done, 1)
            dve.wait_ge(loaded["ln"], 48)
            v.tensor_tensor(vs, vs, ln_g.unsqueeze(1).broadcast_to([P, TOK, SGU]), ALU.mult)
            dve.drain()
            lo(at, 1, 4, 8)
            v.tensor_tensor(vs, vs, ln_b.unsqueeze(1).broadcast_to([P, TOK, SGU]), ALU.add)
            dve.wait_ge(ws_ready, 1)
            v.memset(ws_t[CHUNK:P, :, 0:CHUNK], 0.0)
            dve.drain().then_inc(ln_done, 1)
            lo(at, 1, 8, 12)
            dve.wait_ge(gelu_done, 6)
            dve.sem_inc(evac_done, 1)
            for g in range(GROUPS):
                dve.wait_ge(sgu_mm, g // 2 + 1)
                c = slice(g * P, (g + 1) * P)
                v.scalar_tensor_tensor(us[:, :, c],
                                       aux[:, g // 2, (g % 2) * S:(g % 2 + 1) * S].rearrange("p (t d) -> p t d", t=TOK),
                                       cols[:, 8 + g:9 + g], us[:, :, c], ALU.add, ALU.mult)
            dve.drain().then_inc(sgu_rows, 1)
            dve.wait_ge(sgu_copied, 1)

            with dve.Fori(0, 4) as i:
                at = At("gates2", i)
                for p in range(2):
                    head = i * 2 + p
                    lo(at, p, 4, 6)
                    dve.wait_ge(z_split, head + 1)
                    z = aux[:, 0, 0:384]
                    v.tensor_scalar(z_pos, z, SB_SCALE, 0.0, ALU.mult, ALU.max)
                    v.tensor_scalar(z_neg, z, SB_SCALE, 0.0, ALU.mult, ALU.min)
                    dve.drain()
                    dve.wait_ge(z_log, head + 1)
                    v.tensor_tensor(z_pos, z_pos, z_abs, ALU.add)
                    v.tensor_tensor(z_neg, z_neg, z_abs, ALU.subtract)
                    dve.drain()
                    for c in (0, 2 * P):
                        v.tensor_tensor(z_pos[:, c:c + P], z_pos[:, c:c + P], past, ALU.mult)
                    dve.drain().then_inc(keep_ready, 1)
                    lo(at, p, 6, 8)
                    dve.wait_ge(tail_done, head + 1)
                    v.tensor_tensor(z_neg, z_neg, aux[:, 1, 0:384], ALU.subtract).then_inc(log_a, 1)
                    dve.wait_ge(a_exp, head + 1)
                    for c in (0, 2 * P):
                        v.tensor_tensor(att[:, c:c + P], att[:, c:c + P], past, ALU.mult)
                    dve.drain().then_inc(a_ready, 1)
                    lo(at, p, 8, 12)
                    panel_done(at, p)
                    v.tensor_copy(gate2_tmp, pairs[at.pair(p)][:])
                    dve.drain().then_inc(evac_done, 1)
                    dve.sem_inc(gate_in, 1)
                    dve.wait_ge(gate_out, head + PAIRS + 1)
                    v.tensor_copy(mix[:, :, bass.ds(head * N, N)], gate2_tmp)
                    dve.drain()
            at = At("mix2")
            dve.wait_ge(av_stored, 2 * PAIRS)

            def mix_turn(at, i):
                m = mix[:, :, bass.ds(i * N, N)]
                panel_done(at, 0)
                v.tensor_tensor(m, m, pairs[at.pair(0)][:], ALU.mult)
                dve.drain().then_inc(evac_done, 1)

            refill(at, 36)
            dve.sem_inc(side_go, 1)
            mix_turn(at, 0)
            lo(at, 0, 8, 12)
            panel_done(at, 1)
            add_branch(at.pair(1), 0)
            with dve.Fori(1, 4) as i:
                at = At("mix2", i)
                lo(at, 0, 4, 8)
                mix_turn(at, i)
                lo(at, 0, 8, 12)
                panel_done(at, 1)
                add_branch(at.pair(1), i * N)
            dve.sem_inc(rows_ready, 8)
            at = At("out2")
            fill(6, at, 40, False)
            for p in range(4):
                if p:
                    lo(at, p, 4, 8)
                lo(at, p, 8, 12)
                add_x(at, p, p * N)

            norm(5, 18)
            dve.wait_ge(loaded["gain"], 64)
            at = At("ffn2_first")
            fill(7, at, 48, True)

            def relu_square(at, b, src):
                dve.wait_ge(act_ready, b + 1)
                v.scalar_tensor_tensor(hid, src, 0.0, act_f, ALU.max, ALU.mult)
                dve.drain().then_inc(evac_done, 1)
                dve.sem_inc(hid_ready, 1)

            lo(at, 0, 8, 12)
            relu_square(at, NB1, pairs[0][:])
            hid_turn(NB1)
            with dve.Fori(0, NB2 - 1) as i:
                at = At("ffn2", i)
                lo(at, 0, 4, 8)
                lo(at, 1, 0, 4)
                relu_square(at, i + (NB1 + 1), third)
                for j in range(4):
                    lo(at, 1 + j, 4, 6)
                    add_x(at, 1 + j, j * N, j % 2)
                hid_turn(i + (NB1 + 1))
            at = At("ffn2_last")
            for j in range(4):
                if j < 2:
                    lo(at, j, 4, 6)
                add_x(at, j, j * N, j % 2)

        @block.tensor
        def _(pe):
            def group(at, p, g, left, c0, ps):
                kch, n = at.panels[p]
                hi_t, lo_t = left
                for h in range(2):
                    k = 2 * g + h
                    pe.wait_ge(lo_ready, at.gran(p, k) + 1 + LO_CREDIT)
                    s = at.slot(p, k)
                    for c in range(2):
                        ch = 2 * k + c
                        for t in range(TOK):
                            tok = slice(t * P, (t + 1) * P)
                            x_hi, x_lo = hi_t[:, c0 + ch, tok], lo_t[:, c0 + ch, tok]
                            nc.tensor.matmul(ps[:, t, 0:n], x_hi, w_hi[:, s, c, 0:n], start=ch == 0, stop=False)
                            nc.tensor.matmul(ps[:, t, 0:n], x_hi, w_lo[:, s, c, 0:n], start=False, stop=False)
                            mm = nc.tensor.matmul(ps[:, t, 0:n], x_lo, w_hi[:, s, c, 0:n], start=False,
                                                  stop=ch == kch - 1)
                    mm.then_inc(gran_used, 1)

            def bank_free(at, p):
                pe.wait_ge(evac_done, at.panel(p) - 1 + EVAC_CREDIT)

            def gemm(at, p, left, c0=0, groups=None, ps=None):
                ps = pairs[at.pair(p)] if ps is None else ps
                kch = at.panels[p][0]
                groups = range(kch // 4) if groups is None else groups
                if groups[0] == 0:
                    bank_free(at, p)
                for g in groups:
                    group(at, p, g, left, c0, ps)

            wide, low = (lhs_hi, lhs_lo), (low_hi, low_lo)

            def turn(dst, src):
                return nc.tensor.transpose(dst, src, ident[0:src.shape[0], :])

            def fill_piece(r, f, p):
                kq, t = p // 2, p % 2
                pe.wait_ge(rows_ready, 8 * r + p + 1)
                if p >= 4:
                    pe.wait_ge(lhs_ready, 8 * f + p - 3)
                for c in range(4):
                    ins = turn(aux[:, p % 4, c * P:(c + 1) * P], mix[:, t, (4 * kq + c) * P:(4 * kq + c + 1) * P])
                ins.then_inc(turned, 1)

            def gemm_filling(at, f, r=None, c0=0, ps=None):
                if r is not None:
                    for p in range(4):
                        fill_piece(r, f, p)
                for g in range(at.panels[0][0] // 4):
                    pe.wait_ge(lhs_ready, 8 * f + 2 * g + 2)
                    gemm(at, 0, wide, c0, [g], ps)
                    if r is not None and g < 2:
                        fill_piece(r, f, 4 + 2 * g)
                        fill_piece(r, f, 5 + 2 * g)

            pe.wait_ge(loaded["con"], 16)
            at = At("in")
            gemm_filling(at, 0, 0)
            for p in range(1, 4):
                gemm(at, p, wide)
            pe.wait_ge(evac_done, 2 + EVAC_CREDIT)
            pe.wait_ge(loaded["pool"], 32)
            for c in range(8):
                dst = aux[:, c // 2, (c % 2) * S:(c % 2 + 1) * S]
                ch = slice(c * P, (c + 1) * P)
                nc.tensor.matmul(dst, u_rows[:, 0, ch], pool_a[:, c // 2, 0:S], start=True, stop=False)
                mm = nc.tensor.matmul(dst[:, P:S], u_rows[:, 1, ch], pool_a[:, c // 2, S:S + P],
                                      start=False, stop=True)
                if c % 2:
                    mm.then_inc(pool_mm, 1)
            gemm(at, 4, wide)
            pe.wait_ge(pool_out, 1)
            for j in range(8):
                dst = aux[:, j // 2, (j % 2) * S:(j % 2 + 1) * S]
                g, d = j // 2, j % 2
                for c in range(2):
                    mm = nc.tensor.matmul(dst, w_grp[:, g, c, d * P:(d + 1) * P], act_t[:, 2 * g + c, :],
                                          start=c == 0, stop=c == 1)
                if j % 2:
                    mm.then_inc(pool_mm, 1)
            pe.wait_ge(low_ready, 8)
            with pe.Fori(0, 2) as i:
                for p in range(2):
                    gemm(At("pool", i), p, low)
            pe.wait_ge(low_rows, 1)
            for q in range(4):
                rows = cq_rows if q < 2 else ckv_rows
                for c in range(4):
                    ins = turn(aux[:, q, c * P:(c + 1) * P], rows[:, q % 2, c * P:(c + 1) * P])
                ins.then_inc(low_turned, 1)

            def turn_qk(u):
                pe.wait_ge(qk_done, u)
                for h in range(2):
                    for t in range(TOK):
                        c = slice(h * S + t * P, h * S + (t + 1) * P)
                        turn(aux[:, 0, c], q_rows[:, t, h, 0:NOPE])
                        turn(aux[:, 1, c], k_rows[:, t, h, 0:NOPE])
                        turn(aux[0:ROPE, 2, c], q_rows[:, t, h, NOPE:QK])
                        ins = turn(aux[0:ROPE, 3, c], k_rows[:, t, h, NOPE:QK])
                ins.then_inc(qk_turned, 1)

            def score(u):
                pe.wait_ge(qk_copied, u)
                for h in range(2):
                    for t in range(TOK):
                        c = slice(0, P) if t == 0 else slice(P, 3 * P)
                        keys = slice(0, (t + 1) * P)
                        tok = slice(t * P, (t + 1) * P)
                        nc.tensor.matmul(aux[:, h, c], q_tn[:, h, tok], k_tn[:, h, keys], start=True, stop=False)
                        mm = nc.tensor.matmul(aux[:, h, c], q_tr[0:ROPE, h, tok], k_tr[0:ROPE, h, keys],
                                              start=False, stop=True)
                mm.then_inc(scored, 1)

            def turn_p(u):
                pe.wait_ge(p_ready, u)
                for h in range(2):
                    for b in range(3):
                        ins = turn(aux[:, 2 + h, b * P:(b + 1) * P], probs[:, h, b * P:(b + 1) * P])
                ins.then_inc(p_turned, 1)

            def values(u):
                pe.wait_ge(p_copied, u)
                for h in range(2):
                    dst = aux[:, 0, h * S:(h + 1) * S]
                    nc.tensor.matmul(dst, v_rows[:, 0, h, :], p_t[:, h, 0:S], start=True, stop=False)
                    mm = nc.tensor.matmul(dst[:, P:S], v_rows[:, 1, h, :], p_t[:, h, S:S + P],
                                          start=False, stop=True)
                mm.then_inc(av_done, 1)

            def sub(at, p, u, has_last):
                gemm(at, p, wide, groups=[0, 1])
                if has_last:
                    turn_qk(u)
                gemm(at, p, wide, groups=[2])
                if has_last:
                    score(u)
                gemm(at, p, wide, groups=[3])
                if has_last:
                    turn_p(u)
                gemm(at, p + 1, low)
                if has_last:
                    values(u)
                gemm(at, p + 2, low, 4)

            pe.wait_ge(low_ready, 12)
            sub(At("heads_first"), 0, 0, False)
            with pe.Fori(0, (PAIRS - 2) // 2) as i:
                for s in range(2):
                    sub(At("heads", i), 3 * s, i * 2 + (1 + s), True)
            sub(At("heads_last"), 0, PAIRS - 1, True)
            turn_qk(PAIRS)
            score(PAIRS)
            turn_p(PAIRS)
            values(PAIRS)

            at = At("attn_o")
            gemm_filling(at, 1)
            for p in range(1, 4):
                gemm(at, p, wide)
            at = At("out")
            gemm_filling(at, 2, 1)
            for p in range(1, 4):
                gemm(at, p, wide)

            def hid_turn(b):
                pe.wait_ge(hid_ready, b + 2)
                for t in range(TOK):
                    for c in range(4):
                        ins = turn(aux[:, t, c * P:(c + 1) * P], hid[:, t, c * P:(c + 1) * P])
                    ins.then_inc(hid_turned, 1)

            at = At("ffn_first")
            gemm_filling(at, 3, 2)
            gemm(at, 1, wide)
            hid_turn(0)
            with pe.Fori(0, NB1 - 1) as i:
                at = At("ffn", i)
                gemm(at, 0, wide)
                gemm(at, 1, wide)
                pe.wait_ge(hid_lo_ready, i * 2 + 2)
                for j in range(4):
                    gemm(at, 2 + j, low)
                hid_turn(i + 1)
            pe.wait_ge(hid_lo_ready, 2 * NB1)
            for j in range(4):
                gemm(At("ffn_last"), j, low)

            at = At("qk2")
            gemm_filling(at, 4, 3)

            def turn_qk2(p):
                pe.wait_ge(qk2_ready, p + 1)
                if p:
                    pe.wait_ge(qk2_copied, 2 * p)
                for t in range(TOK):
                    for c in range(4):
                        ins = turn(aux[:, t, c * P:(c + 1) * P], qk_rows[:, t, c * P:(c + 1) * P])
                    ins.then_inc(qk2_turned, 1)

            for p in range(1, 4):
                gemm(at, p, wide, groups=[0, 1])
                turn_qk2(p - 1)
                gemm(at, p, wide, groups=[2, 3])
            turn_qk2(3)
            with pe.Fori(0, 2) as i:
                for p in range(2):
                    gemm(At("uv2", i), p, wide)
            at = At("v2")
            pe.wait_ge(loaded["ln"], 48)
            pe.wait_ge(qk2_copied, 8)
            for g in range(GROUPS):
                ins = turn(aux[:, g // 4, (g % 4) * P:(g % 4 + 1) * P], ws_raw[:, g, :])
            ins.then_inc(ws_turned, 1)
            gemm(at, 0, wide)
            gemm(at, 1, wide)
            pe.wait_ge(ln_done, 1)
            for g in range(GROUPS):
                mm = nc.tensor.matmul(aux[:, g // 2, (g % 2) * S:(g % 2 + 1) * S].rearrange("p (t d) -> p t d", t=TOK),
                                      ws_t[:, g, :], vs[:, :, g * P:(g + 1) * P], start=True, stop=True)
                if g % 2:
                    mm.then_inc(sgu_mm, 1)
            pe.wait_ge(sgu_rows, 1)
            for c in range(8):
                for t in range(TOK):
                    ins = turn(aux[:, c // 2, (c % 2) * S + t * P:(c % 2) * S + (t + 1) * P],
                               us[:, t, c * P:(c + 1) * P])
                if c % 2:
                    ins.then_inc(sgu_turned, 1)
            pe.wait_ge(sgu_copied, 1)

            with pe.Fori(0, 4) as i:
                at = At("gates2", i)
                for p in range(2):
                    head = i * 2 + p
                    gemm(at, p, wide, groups=[0])
                    pe.wait_ge(head_copied, head + 1)
                    q_head = qk_t[:, bass.ds(head, 1), :].rearrange("p a t -> p (a t)")
                    nc.tensor.matmul(aux[:, 0, 0:S], k_head[:, 0:P], q_head, start=True, stop=True)
                    nc.tensor.matmul(aux[:, 0, S:S + P], k_head[:, P:S],
                                     qk_t[:, bass.ds(head, 1), P:S].rearrange("p a t -> p (a t)"),
                                     start=True, stop=True).then_inc(z_done, 1)
                    gemm(at, p, wide, groups=[1])
                    pe.wait_ge(keep_ready, head + 1)
                    nc.tensor.matmul(aux[:, 1, 0:384], after, z_pos, start=True, stop=False)
                    nc.tensor.matmul(aux[:, 1, P:S], ones, z_pos[:, S:S + P], start=False, stop=True
                                     ).then_inc(tail_done, 1)
                    gemm(at, p, wide, groups=[2])
                    pe.wait_ge(a_ready, head + 1)
                    nc.tensor.matmul(aux[:, 2, 0:S], v_head[:, 0, :], att[:, 0:S], start=True, stop=False)
                    nc.tensor.matmul(aux[:, 2, P:S], v_head[:, 1, :], att[:, S:S + P], start=False, stop=True
                                     ).then_inc(av_done, 1)
                    gemm(at, p, wide, groups=[3])
            at = At("mix2")
            for g in range(2):
                pe.wait_ge(lhs_ready, 8 * 5 + 2 * g + 2)
                gemm(at, 0, wide, 0, [g])
            for g in range(2):
                pe.wait_ge(lhs_ready, 8 * 5 + 2 * g + 6)
                gemm(at, 1, wide, 8, [g])
            with pe.Fori(1, 4) as i:
                gemm(At("mix2", i), 0, wide)
                gemm(At("mix2", i), 1, wide, 8)
            at = At("out2")
            gemm_filling(at, 6, 4)
            for p in range(1, 4):
                gemm(at, p, wide)

            at = At("ffn2_first")
            gemm_filling(at, 7, 5, ps=pairs[0])
            hid_turn(NB1)
            with pe.Fori(0, NB2 - 1) as i:
                at = At("ffn2", i)
                gemm(at, 0, wide, ps=third)
                pe.wait_ge(hid_lo_ready, i * 2 + (2 * NB1 + 2))
                for j in range(4):
                    gemm(at, 1 + j, low, ps=pairs[j % 2])
                hid_turn(i + (NB1 + 1))
            pe.wait_ge(hid_lo_ready, 2 * (NB1 + NB2))
            for j in range(4):
                gemm(At("ffn2_last"), j, low, ps=pairs[j % 2])


_INS = ["x", "positions", "attn_norm_g", "w_in", "b_gate", "q_a_norm_g", "w_q_b", "kv_a_norm_g",
        "w_kv_b", "q_norm_g", "k_norm_g", "w_attn_o", "w_pool_grp", "pool_scale", "w_pool_o", "w_out",
        "ffn_norm_g", "w_ffn_gate", "w_ffn_up", "w_ffn_down", "g_mix_2", "w_in_2", "g_q_2", "g_k_2",
        "sgu_ln_g_2", "sgu_ln_b_2", "w_spatial_2", "b_spatial_2", "w_oa_2", "w_ob_2", "w_out_2",
        "g_ff_2", "w_ff1_2", "w_ff2_2"]


def shape_constants():
    r = np.arange(P)
    con = np.zeros((P, C_END), np.float32)
    con[:, C_ID:C_ID + P] = np.eye(P)
    for b in (0, 2):
        con[:, C_CAUSAL + b * P:C_CAUSAL + (b + 1) * P] = np.where(r[None, :] <= r[:, None], 0.0, -3e38)
    con[:, C_AFTER:C_AFTER + P] = r[:, None] > r[None, :]
    con[:, C_ONES:C_ONES + P] = 1.0
    con[:, C_PAST:C_PAST + P] = r[:, None] < r[None, :]
    half = np.arange(HALF, dtype=np.float32)
    con[:, C_FREQ:C_FREQ + HALF] = (np.float32(10000.0) ** (-half / np.float32(HALF)))[None, :]
    mats = np.zeros((P, 4, 384), np.float32)
    src = np.arange(S)[:, None]
    dst = np.arange(S)[None, :]
    for g, w in enumerate(POOL_WINDOWS):
        lo = np.maximum(dst + 1 - w, 0)
        a = np.where((src >= lo) & (src <= dst), 1.0 / (dst + 1 - lo), 0.0) - (src == dst)
        mats[:, g, 0:S] = a[0:P, :]
        mats[:, g, S:S + P] = a[P:S, P:S]
    return con, mats


def kernel(**inputs):
    import concourse.bacc as bacc
    from concourse.bass_utils import run_bass_kernel_spmd

    nc = bacc.Bacc("TRN2", target_bir_lowering=False, num_devices=1)
    arrays, args = {}, []
    con, mats = shape_constants()
    named = [(n, np.ascontiguousarray(inputs[n])) for n in _INS] + [("consts", con), ("pool_mats", mats)]
    for name, a in named:
        arrays[f"in_{name}"] = a
        args.append(nc.dram_tensor(f"in_{name}", a.shape, mybir.dt.from_np(a.dtype), kind="ExternalInput").ap())
    args.append(nc.dram_tensor("out_x", (1, S, D), F32, kind="ExternalOutput").ap())
    two_blocks(nc, *args)
    r = run_bass_kernel_spmd(nc, [arrays], core_ids=[0])
    return r.results[0]["out_x"]
```

```python
import numpy as np

import concourse.bass as bass
from concourse import mybir

F32 = mybir.dt.float32
F32R = mybir.dt.float32r
I32 = mybir.dt.int32
ALU = mybir.AluOpType
ACT = mybir.ActivationFunctionType
AX = mybir.AxisListType

P = 128
TOK = 2
S = TOK * P
D = 2048
KC = D // P
N = 512
EPS = 1e-6

Q_RANK, KV_RANK, ROPE, POOL = 512, 512, 64, 1024
NOPE, VDIM, HEADS = 128, 128, 16
QK = NOPE + ROPE
HALF = ROPE // 2
POOL_WINDOWS = (2, 4, 8, 16)
D_FF = 5632
COL_KV = Q_RANK
COL_KR = COL_KV + KV_RANK
COL_POOL = COL_KR + ROPE
COL_GATE = COL_POOL + POOL
PAIRS = HEADS // 2
SM_SCALE = QK ** -0.5

SB = 1024
SB_HEADS = 8
SGU = 1024
GROUPS = 8
CHUNK = 64
D_FF2 = 8192
COL_U = 3 * SB
COL_VS = COL_U + SGU
COL_GATE2 = COL_VS + SGU
SB_SCALE = 128 ** -0.5

RAW = 4
SPLIT = 4
LEAD = 4
LO_CREDIT = 2 * RAW
EVAC_CREDIT = 2

NB1 = D_FF // N
NB2 = D_FF2 // N

C_ID, C_CAUSAL, C_AFTER, C_ONES, C_PAST, C_FREQ = 0, 128, 512, 640, 768, 896
C_END = 928
TWO_PI = 2 * np.pi
PI_1 = 6.28125
PI_2 = float(np.float32(np.round((TWO_PI - PI_1) * 2 ** 21) / 2 ** 21))
PI_3 = float(TWO_PI - PI_1 - PI_2)
MAGIC = 1.5 * 2 ** 23
PI_MAX = 3.1415925


FULL = (KC, N)
SHORT = (4, N)
SUB = [FULL, (4, 2 * QK), SHORT]
PLAN = [
    ("in", 1, [FULL, FULL, (KC, ROPE), FULL, FULL]),
    ("pool", 2, [(8, N), (8, N)]),
    ("heads_first", 1, SUB),
    ("heads", (PAIRS - 2) // 2, SUB + SUB),
    ("heads_last", 1, SUB),
    ("attn_o", 1, [(KC - 4, N)] * 2 + [SHORT] * 2 + [FULL] * 2),
    ("out", 1, [FULL] * 4),
    ("ffn_first", 1, [FULL, FULL]),
    ("ffn", NB1 - 1, [FULL, FULL] + [SHORT] * 4),
    ("ffn_last", 1, [SHORT] * 4),
    ("qk2", 1, [FULL] * 4),
    ("uv2", 2, [FULL] * 2),
    ("v2", 1, [FULL] * 2),
    ("gates2", 4, [FULL] * 2),
    ("mix2", 4, [(8, N), (8, N)]),
    ("out2", 1, [FULL] * 4),
    ("ffn2_first", 1, [FULL]),
    ("ffn2", NB2 - 1, [FULL] + [SHORT] * 4),
    ("ffn2_last", 1, [SHORT] * 4),
]


class At:

    def __init__(self, name, i=0):
        gran = panel = 0
        for stage, turns, panels in PLAN:
            sizes = [k // 2 for k, _ in panels]
            if stage == name:
                break
            gran += turns * sum(sizes)
            panel += turns * len(panels)
        self.i, self.panels = i, panels
        self.gran0, self.panel0 = gran, panel
        self.starts = [sum(sizes[:p]) for p in range(len(sizes) + 1)]
        self.per = self.starts[-1]
        assert turns == 1 or self.per % (2 * RAW) == 0

    def gran(self, p, k=0):
        return self.i * self.per + (self.gran0 + self.starts[p] + k)

    def slot(self, p, k=0):
        return (self.gran0 + self.starts[p] + k) % SPLIT

    def raw_slot(self, p, k=0):
        return (self.gran0 + self.starts[p] + k) // 2 % RAW

    def loads(self, p, k=0):
        return self.i * (16 * self.per // (2 * RAW)) + 16 * ((self.gran0 + self.starts[p] + k) // (2 * RAW) + 1)

    def end(self, p):
        return self.gran(p, self.panels[p][0] // 2)

    def panel(self, p):
        return self.i * len(self.panels) + (self.panel0 + p)

    def pair(self, p):
        return (self.panel0 + p) % 2


def two_blocks(nc, x, positions, attn_norm_g, w_in, b_gate, q_a_norm_g, w_q_b, kv_a_norm_g, w_kv_b,
               q_norm_g, k_norm_g, w_attn_o, w_pool_grp, pool_scale, w_pool_o, w_out, ffn_norm_g,
               w_ffn_gate, w_ffn_up, w_ffn_down, g_mix_2, w_in_2, g_q_2, g_k_2, sgu_ln_g_2,
               sgu_ln_b_2, w_spatial_2, b_spatial_2, w_oa_2, w_ob_2, w_out_2, g_ff_2, w_ff1_2,
               w_ff2_2, consts, pool_mats, out):
    at_byte = [(nc.sbuf_base + 31) // 32 * 32]

    def place(name, shape, dtype=F32, offset=None):
        size = 4 * int(np.prod(shape[1:]))
        if offset is None:
            offset = at_byte[0]
            at_byte[0] += (size + 31) // 32 * 32
        return nc.alloc_sbuf_tensor_at(name, shape, dtype, offset=offset)

    xres = place("xres", [P, TOK, D])
    lhs_hi = place("lhs_hi", [P, KC, S], F32R)
    lhs_lo = place("lhs_lo", [P, KC, S], F32R)
    raw = place("raw", [P, RAW, 4, N])
    w_hi = place("w_hi", [P, SPLIT, 2, N], F32R)
    w_lo = place("w_lo", [P, SPLIT, 2, N], F32R)
    mix = place("mix", [P, TOK, 2 * D])
    act_t = place("act_t", [P, KC, S])
    low_at = at_byte[0]
    low_hi = place("low_hi", [P, 8, S], F32R)
    low_lo = place("low_lo", [P, 8, S], F32R)
    qk_t = place("qk_t", [P, 16, S], offset=low_at)
    con = place("con", [P, C_END])
    cols = place("cols", [P, 16])
    small = place("small", [P, 96])
    cosd = place("cosd", [P, TOK, ROPE])
    sind = place("sind", [P, TOK, ROPE])
    krr = place("krr", [P, TOK, ROPE])
    pos_i = place("pos_i", [P, TOK], I32)
    arena_at = at_byte[0]
    arena = place("arena", [P, 6144])
    assert at_byte[0] <= nc.sbuf_base + nc.sbuf_bytes_remaining, at_byte[0]

    def part(start, *shape):
        size = int(np.prod(shape))
        ap = arena[:, start:start + size]
        if len(shape) == 2:
            return ap.rearrange("p (a b) -> p a b", a=shape[0])
        if len(shape) == 3:
            return ap.rearrange("p (a b c) -> p a b c", a=shape[0], b=shape[1])
        return ap

    gain = part(0, D)
    pool_a = part(2048, 4, 384)
    gain_cq = part(3584, N)
    gain_ckv = part(4096, N)
    junk = part(4608, N)
    q_rows = part(0, TOK, 2, QK)
    k_rows = part(768, TOK, 2, QK)
    v_rows = part(1536, TOK, 2, VDIM)
    q_tn = part(2048, 2, S)
    k_tn = part(2560, 2, S)
    p_t = part(2048, 2, 384)
    q_tr = part(3072, 2, S)
    k_tr = part(3584, 2, S)
    gate_tmp = part(3072, TOK, N)
    probs = part(4096, 2, 384)
    squares = part(4096, TOK, 2, QK)
    rope_a = part(4096, TOK, 2, ROPE)
    rope_b = part(4352, TOK, 2, ROPE)
    gain_q = part(5120, QK)
    gain_k = part(5312, QK)
    bias = part(5504, N)
    act_f = part(2048, TOK, N)
    hid = part(3072, TOK, N)
    vs = part(0, TOK, SGU)
    us = part(2048, TOK, SGU)
    vb = part(4096, TOK, SB)
    z_neg = part(0, 384)
    z_pos = part(384, 384)
    z_abs = part(768, 384)
    att = part(1152, 384)
    k_head = part(1536, S)
    v_head = part(1792, TOK, P)
    gain_qk = mix[:, 0, D:2 * D]
    qk_rows = mix[:, 1, D:D + 1024].rearrange("p (a b) -> p a b", a=TOK)
    qk_sq = mix[:, 1, D + 1024:2 * D].rearrange("p (a b) -> p a b", a=TOK)
    ln_g, ln_b = mix[:, 0, 0:SGU], mix[:, 0, SGU:2 * SGU]
    ws_raw = mix[:, 1, 0:1024].rearrange("p (g j) -> p g j", g=GROUPS)
    ws_t = mix[:, 1, 1024:2048].rearrange("p (g i) -> p g i", g=GROUPS)
    w_grp = act_t[:, 8:16, :].rearrange("p (g c) d -> p g c d", g=4)
    cq_rows = mix[:, :, D:D + N]
    ckv_rows = mix[:, :, D + N:D + 2 * N]
    u_rows = mix[:, :, D + 2 * N:2 * D]

    ident = con[:, C_ID:C_ID + P]
    causal = con[:, C_CAUSAL:C_CAUSAL + 384]
    after = con[:, C_AFTER:C_AFTER + P]
    ones = con[:, C_ONES:C_ONES + P]
    past = con[:, C_PAST:C_PAST + P]
    freq = con[:, C_FREQ:C_FREQ + HALF]
    ss, inv = small[:, 0:8], small[:, 8:16]
    x_inv = small[:, 72:74]
    x_ss = small[:, 74:82].rearrange("p (t b) -> p t b", t=TOK)
    inv_x = small[:, 82:90]
    kr_ss, cq_ss, cq_inv = small[:, 16:18], small[:, 18:20], small[:, 20:22]
    row_max, row_sum, row_inv = small[:, 24:28], small[:, 28:32], small[:, 32:36]
    pos_f = small[:, 36:38]
    ln_mv, ln_inv = small[:, 40:44], small[:, 44:46]
    ln_stats = small[:, 48:72]

    pairs = [nc.alloc_psum_tensor(f"pair{i}", [P, TOK, N], F32) for i in range(2)]
    aux = nc.alloc_psum_tensor("aux", [P, 4, N], F32)
    third = aux[:, 2:4, :]

    sem = nc.alloc_semaphore
    raw_loaded = [sem(f"raw_loaded{r}") for r in range(RAW)]
    hi_ready = sem("hi_ready")
    lo_ready = sem("lo_ready")
    gran_used = sem("gran_used")
    evac_done = sem("evac_done")
    ident_loaded = sem("ident_loaded")
    x_loaded = [sem(f"x_loaded{b}") for b in range(4)]
    x_inv_ready = sem("x_inv_ready")
    loaded = {n: sem("loaded_" + n) for n in (
        "con", "pos", "cols", "cq", "pool", "qk", "bias", "gain", "qk2", "ln")}
    side_go = sem("side_go")
    bias_used = sem("bias_used")
    sumsq = sem("sumsq")
    ms_ready = sem("ms_ready")
    rms_ready = sem("rms_ready")
    rows_ready = sem("rows_ready")
    turned = sem("turned")
    lhs_hi_ready = sem("lhs_hi_ready")
    lhs_ready = sem("lhs_ready")
    angles = sem("angles")
    sines = sem("sines")
    pool_rows = sem("pool_rows")
    pool_mm = sem("pool_mm")
    pool_out = sem("pool_out")
    low_rows = sem("low_rows")
    low_turned = sem("low_turned")
    low_hi_ready = sem("low_hi_ready")
    low_ready = sem("low_ready")
    mix_ones = sem("mix_ones")
    kr_sq = sem("kr_sq")
    gate_in = sem("gate_in")
    gate_out = sem("gate_out")
    q_sq = sem("q_sq")
    kv_sq = sem("kv_sq")
    qk_done = sem("qk_done")
    qk_turned = sem("qk_turned")
    qk_copied = sem("qk_copied")
    scored = sem("scored")
    max_ready = sem("max_ready")
    exp_done = sem("exp_done")
    p_ready = sem("p_ready")
    p_turned = sem("p_turned")
    p_copied = sem("p_copied")
    av_done = sem("av_done")
    av_stored = sem("av_stored")
    act_ready = sem("act_ready")
    hid_ready = sem("hid_ready")
    hid_turned = sem("hid_turned")
    hid_hi_ready = sem("hid_hi_ready")
    hid_lo_ready = sem("hid_lo_ready")
    qk2_sq = sem("qk2_sq")
    qk2_ready = sem("qk2_ready")
    qk2_turned = sem("qk2_turned")
    qk2_copied = sem("qk2_copied")
    gelu_done = sem("gelu_done")
    ln_done = sem("ln_done")
    ws_turned = sem("ws_turned")
    ws_ready = sem("ws_ready")
    sgu_mm = sem("sgu_mm")
    sgu_rows = sem("sgu_rows")
    sgu_turned = sem("sgu_turned")
    sgu_copied = sem("sgu_copied")
    head_copied = sem("head_copied")
    z_done = sem("z_done")
    z_split = sem("z_split")
    z_log = sem("z_log")
    keep_ready = sem("keep_ready")
    tail_done = sem("tail_done")
    log_a = sem("log_a")
    a_exp = sem("a_exp")
    a_ready = sem("a_ready")
    out_done = sem("out_done")

    def token_rows(ap):
        return ap.rearrange("(t p) n -> p t n", p=P)

    block = nc.Block()
    with block:
        @block.sync
        def _(sp):
            def load(at, p, w, col, row0=0, groups=None):
                kch, n = at.panels[p]
                for g in range(kch // 4) if groups is None else groups:
                    k = 2 * g
                    sp.wait_ge(lo_ready, at.gran(p, k) + 2)
                    rows = w[bass.ds(row0 + g * 4 * P, 4 * P), bass.ds(col, n)]
                    sp.dma_start(raw[:, at.raw_slot(p, k), :, 0:n],
                                 rows.rearrange("(c p) n -> p c n", p=P)
                                 ).then_inc(raw_loaded[at.raw_slot(p, k)], 16)

            w1, w2 = w_in[0], w_in_2[0]
            at = At("in")
            sp.dma_start(ident, consts[:, C_ID:C_ID + P]).then_inc(ident_loaded, 16)
            for b in range(4):
                blk = slice(b * N, (b + 1) * N)
                sp.dma_start(xres[:, :, blk], token_rows(x[0])[:, :, blk]).then_inc(x_loaded[b], 16)
                sp.dma_start(gain[:, blk], attn_norm_g[0, blk].partition_broadcast(P)).then_inc(x_loaded[b], 16)
                load(at, 0, w1, COL_POOL, groups=[b])
            for p, col in enumerate((COL_POOL + N, COL_KR, 0, COL_KV)):
                load(at, p + 1, w1, col)
            with sp.Fori(0, 2) as i:
                for p in range(2):
                    load(At("pool", i), p, w_pool_o[0], i * (2 * N) + p * N)

            def sub(at, p, u):
                load(at, p, w1, u * N + COL_GATE)
                load(at, p + 1, w_q_b[0], u * (2 * QK))
                load(at, p + 2, w_kv_b[0], (u * P) * 4)

            sub(At("heads_first"), 0, 0)
            with sp.Fori(0, (PAIRS - 2) // 2) as i:
                for s in range(2):
                    sub(At("heads", i), 3 * s, i * 2 + (1 + s))
            sub(At("heads_last"), 0, PAIRS - 1)
            at = At("attn_o")
            for p in range(2):
                load(at, p, w_attn_o[0], p * N)
            for p in range(2):
                load(at, 2 + p, w_attn_o[0], p * N, (KC - 4) * P)
            for p in range(2, 4):
                load(at, 2 + p, w_attn_o[0], p * N)
            for p in range(4):
                load(At("out"), p, w_out[0], p * N)
            at = At("ffn_first")
            load(at, 0, w_ffn_gate[0], 0)
            load(at, 1, w_ffn_up[0], 0)
            with sp.Fori(0, NB1 - 1) as i:
                at = At("ffn", i)
                load(at, 0, w_ffn_gate[0], i * N + N)
                load(at, 1, w_ffn_up[0], i * N + N)
                for j in range(4):
                    load(at, 2 + j, w_ffn_down[0], j * N, i * N)
            for j in range(4):
                load(At("ffn_last"), j, w_ffn_down[0], j * N, (NB1 - 1) * N)

            for p in range(4):
                load(At("qk2"), p, w2, p * N)
            with sp.Fori(0, 2) as i:
                for p in range(2):
                    load(At("uv2", i), p, w2, i * (-SGU) + (COL_VS + p * N))
            for p in range(2):
                load(At("v2"), p, w2, 2 * SB + p * N)
            with sp.Fori(0, 4) as i:
                for p in range(2):
                    load(At("gates2", i), p, w2, i * (2 * N) + (COL_GATE2 + p * N))
            with sp.Fori(0, 4) as i:
                load(At("mix2", i), 0, w_oa_2[0], i * N)
                load(At("mix2", i), 1, w_ob_2[0], i * N)
            for p in range(4):
                load(At("out2"), p, w_out_2[0], p * N)
            load(At("ffn2_first"), 0, w_ff1_2[0], 0)
            with sp.Fori(0, NB2 - 1) as i:
                at = At("ffn2", i)
                load(at, 0, w_ff1_2[0], i * N + N)
                for j in range(4):
                    load(at, 1 + j, w_ff2_2[0], j * N, i * N)
            for j in range(4):
                load(At("ffn2_last"), j, w_ff2_2[0], j * N, (NB2 - 1) * N)
            last = At("ffn2_last")
            for j in range(4):
                sp.wait_ge(evac_done, last.panel(j) + 1 + EVAC_CREDIT)
                sp.dma_start(token_rows(out[0])[:, :, j * N:(j + 1) * N],
                             xres[:, :, j * N:(j + 1) * N]).then_inc(out_done, 16)
            sp.wait_ge(out_done, 4 * 16)

        @block.gpsimd
        def _(pool):
            def to_all(dst, row, what):
                pool.dma_start(dst, row.partition_broadcast(P)).then_inc(loaded[what], 16)

            pool.dma_start(con[:, P:C_END], consts[:, P:C_END]).then_inc(loaded["con"], 16)
            with nc.allow_non_contiguous_dma("a few columns"):
                pool.dma_start(pos_i[:], positions[0].rearrange("(t p) -> p t", p=P)).then_inc(loaded["pos"], 16)
                pool.dma_start(cols[:, 0:8], pool_scale[0].rearrange("g (c p) -> p (g c)", p=P)
                               ).then_inc(loaded["cols"], 16)
                pool.dma_start(cols[:, 8:16], b_spatial_2[0].rearrange("g p -> p g")).then_inc(loaded["cols"], 16)
            to_all(gain_k, k_norm_g[0], "qk")
            to_all(gain_q, q_norm_g[0], "qk")
            to_all(gain_cq, q_a_norm_g[0], "cq")
            to_all(gain_ckv, kv_a_norm_g[0], "cq")
            pool.dma_start(pool_a, pool_mats).then_inc(loaded["pool"], 16)
            pool.dma_start(w_grp, w_pool_grp[0].rearrange("g (c p) d -> p g c d", p=P)
                           ).then_inc(loaded["pool"], 16)
            pool.wait_ge(low_turned, 4)
            nc.gpsimd.memset(mix[:, :, D:2 * D], 1.0).then_inc(mix_ones, 1)
            to_all(bias, b_gate[0, 0:N], "bias")
            with pool.Fori(1, PAIRS) as u:
                pool.wait_ge(bias_used, u)
                to_all(bias, b_gate[0, bass.ds(u * N, N)], "bias")
            pool.wait_ge(side_go, 1)
            to_all(gain, ffn_norm_g[0], "gain")
            pool.wait_ge(side_go, 2)
            to_all(gain, g_mix_2[0], "gain")
            to_all(gain_qk[:, 0:SB], g_q_2[0].rearrange("h d -> (h d)"), "qk2")
            to_all(gain_qk[:, SB:2 * SB], g_k_2[0].rearrange("h d -> (h d)"), "qk2")
            pool.wait_ge(side_go, 3)
            to_all(ln_g, sgu_ln_g_2[0], "ln")
            to_all(ln_b, sgu_ln_b_2[0], "ln")
            pool.dma_start(ws_raw, w_spatial_2[0].rearrange("g i j -> i g j")).then_inc(loaded["ln"], 16)
            pool.wait_ge(side_go, 4)
            to_all(gain, g_ff_2[0], "gain")

        @block.scalar
        def _(act):
            def hi(at, p, k0, k1, after_panel=None):
                for k in range(k0, k1):
                    width = at.panels[p][1] if after_panel is None else after_panel
                    act.wait_ge(raw_loaded[at.raw_slot(p, k)], at.loads(p, k))
                    act.wait_ge(gran_used, at.gran(p, k) + 1)
                    h = (at.gran0 + at.starts[p] + k) % 2
                    nc.scalar.activation(w_hi[:, at.slot(p, k), :, 0:width],
                                         raw[:, at.raw_slot(p, k), 2 * h:2 * h + 2, 0:width],
                                         ACT.Copy).then_inc(hi_ready, 1)

            def panel_done(at, p):
                act.wait_ge(gran_used, at.end(p) + SPLIT)

            def root(n_before, dst, src):
                act.wait_ge(ms_ready, n_before + 1)
                nc.scalar.activation(dst, src, ACT.Sqrt).then_inc(rms_ready, 1)

            def squares_of(b, at=None, p=None):
                if at is not None:
                    act.wait_ge(evac_done, at.panel(p) + 1 + EVAC_CREDIT)
                for t in range(TOK):
                    nc.scalar.activation(mix[:, 1, 2 * D - N:2 * D], xres[:, t, b * N:(b + 1) * N],
                                         ACT.Square, accum_out=x_ss[:, t, b:b + 1])
                    act.drain()
                if b == 3:
                    act.sem_inc(sumsq, 1)

            def x_norm(n_roots):
                root(n_roots, x_inv, x_inv)

            def piece(r, p, free=None):
                act.wait_ge(turned, 8 * r + p + 1)
                if free is not None:
                    act.wait_ge(gran_used, free)
                kq, t = p // 2, p % 2
                nc.scalar.activation(lhs_hi[:, 4 * kq:4 * kq + 4, t * P:(t + 1) * P],
                                     aux[:, p % 4, :].rearrange("p (c t) -> p c t", c=4),
                                     ACT.Copy).then_inc(lhs_hi_ready, 1)

            def pieces(r, kq, free=None):
                piece(r, 2 * kq, free)
                piece(r, 2 * kq + 1, free)

            def refill(kq):
                nc.scalar.activation(lhs_hi[:, 4 * kq:4 * kq + 4, :], act_t[:, 4 * kq:4 * kq + 4, :],
                                     ACT.Copy).then_inc(lhs_hi_ready, 1)

            def bridge(r, at, p, nxt, between=None):
                for kq in range(3):
                    hi(at, p, 4 + 2 * kq, 6 + 2 * kq)
                    pieces(r, kq, at.gran(p, 2 * kq + 2) + SPLIT)
                hi(at, p, 10, 12)
                if between is not None:
                    between()
                hi(nxt, 0, 4, 6)
                pieces(r, 3, at.gran(p, 8) + SPLIT)
                hi(nxt, 0, 6, 8)

            act.sem_inc(gran_used, SPLIT)
            at = At("in")
            for kq in range(4):
                hi(at, 0, 2 * kq, 2 * kq + 2)
                pieces(0, kq)
            for b in range(4):
                act.wait_ge(x_loaded[b], 32)
                squares_of(b)
            x_norm(0)
            hi(at, 1, 0, 4)
            act.wait_ge(angles, 1)
            nc.scalar.activation(cosd[:, :, 0:HALF], cosd[:, :, HALF:ROPE], ACT.Sin)
            nc.scalar.activation(sind[:, :, HALF:ROPE], sind[:, :, 0:HALF], ACT.Sin)
            act.drain().then_inc(sines, 1)
            hi(at, 1, 4, 8)
            act.wait_ge(x_inv_ready, 1)

            def low_squares(p):
                panel_done(at, p)
                for t in range(TOK):
                    nc.scalar.activation(junk, pairs[at.pair(p)][:, t, :], ACT.Square,
                                         scale=x_inv[:, t:t + 1], accum_out=cq_ss[:, t:t + 1])
                    act.drain()
                act.sem_inc(sumsq, 1)

            for p in range(2, 5):
                hi(at, p, 0, 4)
                if p == 4:
                    low_squares(3)
                    root(1, cq_inv, cq_inv)
                if p == 3:
                    panel_done(at, 2)
                    for t in range(TOK):
                        nc.scalar.activation(junk[:, 0:ROPE], pairs[at.pair(2)][:, t, 0:ROPE], ACT.Square,
                                             scale=x_inv[:, t:t + 1], accum_out=kr_ss[:, t:t + 1])
                        act.drain()
                    act.sem_inc(kr_sq, 1)
                hi(at, p, 4, 8)
                if p == 4:
                    for b in range(4):
                        act.wait_ge(pool_mm, b + 1)
                        nc.scalar.activation(act_t[:, 2 * b:2 * b + 2, :],
                                             aux[:, b, :].rearrange("p (c t) -> p c t", c=2), ACT.Copy)
                    act.drain().then_inc(pool_out, 1)
            nxt = At("pool")
            hi(nxt, 0, 0, 4)
            low_squares(4)
            root(2, cq_inv, cq_inv)
            for j in range(8):
                act.wait_ge(pool_mm, 4 + j // 2 + 1)
                act.wait_ge(loaded["cols"], 32)
                nc.scalar.activation(low_hi[:, j, :], aux[:, j // 2, (j % 2) * S:(j % 2 + 1) * S], ACT.Copy,
                                     scale=cols[:, j:j + 1]).then_inc(low_hi_ready, 1)
            with act.Fori(0, 2) as i:
                at = At("pool", i)
                for p in range(2):
                    hi(at, p, 4, 8)
            for q in range(4):
                act.wait_ge(low_turned, q + 1)
                c0, t = 4 * (q // 2), q % 2
                nc.scalar.activation(low_hi[:, c0:c0 + 4, t * P:(t + 1) * P],
                                     aux[:, q, :].rearrange("p (c t) -> p c t", c=4),
                                     ACT.Copy).then_inc(low_hi_ready, 1)

            def attend_a(u):
                root(u + 2, inv, inv)

            def attend_b(u):
                act.wait_ge(qk_turned, u)
                nc.scalar.activation(q_tn, aux[:, 0, :].rearrange("p (h t) -> p h t", h=2), ACT.Copy)
                nc.scalar.activation(k_tn, aux[:, 1, :].rearrange("p (h t) -> p h t", h=2), ACT.Copy)
                nc.scalar.activation(q_tr[0:ROPE], aux[0:ROPE, 2, :].rearrange("p (h t) -> p h t", h=2), ACT.Copy)
                nc.scalar.activation(k_tr[0:ROPE], aux[0:ROPE, 3, :].rearrange("p (h t) -> p h t", h=2), ACT.Copy)
                act.drain().then_inc(qk_copied, 1)

            def attend_c(u):
                act.wait_ge(max_ready, u)
                for h in range(2):
                    for t in range(TOK):
                        c = slice(0, P) if t == 0 else slice(P, 3 * P)
                        nc.scalar.activation(probs[:, h, c], probs[:, h, c], ACT.Exp,
                                             bias=row_max[:, 2 * t + h:2 * t + h + 1],
                                             accum_out=row_sum[:, 2 * t + h:2 * t + h + 1])
                act.drain().then_inc(exp_done, 1)

            def attend_d(u):
                act.wait_ge(p_turned, u)
                nc.scalar.activation(p_t, aux[:, 2:4, 0:384], ACT.Copy).then_inc(p_copied, 1)

            def attend_e(u):
                act.wait_ge(av_done, u)
                nc.scalar.activation(act_t[:, bass.ds(u * 2 - 2, 2), :],
                                     aux[:, 0, :].rearrange("p (h t) -> p h t", h=2), ACT.Copy
                                     ).then_inc(av_stored, 1)

            def rows_q(at, p, u):
                panel_done(at, p)
                nc.scalar.activation(squares, pairs[at.pair(p)][:, :, 0:2 * QK].rearrange(
                    "p t (h d) -> p t h d", h=2), ACT.Square).then_inc(q_sq, 1)

            def rows_kv(at, p, u):
                panel_done(at, p)
                kv = pairs[at.pair(p)][:].rearrange("p t (h d) -> p t h d", h=2)
                act.wait_ge(q_sq, u * 2 + 2)
                nc.scalar.activation(squares[:, :, :, 0:NOPE], kv[:, :, :, 0:NOPE], ACT.Square)
                nc.scalar.activation(v_rows, kv[:, :, :, NOPE:NOPE + VDIM], ACT.Copy)
                act.drain().then_inc(kv_sq, 1)

            def sub(at, p, u, has_last, last=False):
                if has_last:
                    attend_a(u)
                hi(at, p, 4, 6)
                hi(at, p, 6, 8)
                if has_last:
                    attend_b(u)
                hi(at, p + 1, 0, 2)
                if has_last:
                    attend_c(u)
                hi(at, p + 2, 0, 2)
                if has_last:
                    attend_d(u)
                act.wait_ge(gate_in, u + 1)
                nc.scalar.activation(gate_tmp, gate_tmp, ACT.Sigmoid).then_inc(gate_out, 1)
                rows_q(at, p + 1, u)
                if has_last:
                    attend_e(u)
                hi(at, p + 2, 2, 4, N)
                if last:
                    act.drain()
                    refill(0)
                rows_kv(at, p + 2, u)
                hi(at, p + 2, 4, 6, N)
                if last:
                    refill(1)
                    refill(2)

            sub(At("heads_first"), 0, 0, False)
            with act.Fori(0, (PAIRS - 2) // 2) as i:
                for s in range(2):
                    sub(At("heads", i), 3 * s, i * 2 + (1 + s), True)
            sub(At("heads_last"), 0, PAIRS - 1, True, True)

            at = At("attn_o")
            attend_a(PAIRS)
            hi(at, 0, 4, 8)
            attend_b(PAIRS)
            hi(at, 0, 8, 10)
            attend_c(PAIRS)
            hi(at, 0, 10, 12)
            attend_d(PAIRS)
            hi(at, 0, 12, 14)
            attend_e(PAIRS)
            act.drain()
            refill(3)
            hi(at, 0, 14, 24)
            hi(at, 0, 24, 28)
            bridge(1, at, 5, At("out"))
            at, nxt = At("out"), At("ffn_first")
            for p in range(3):
                if p:
                    hi(at, p, 4, 8)
                    squares_of(p - 1, at, p - 1)
                hi(at, p, 8, 12)
            bridge(2, at, 3, nxt, lambda: squares_of(2, at, 2))
            squares_of(3, at, 3)

            def hid_turn(b):
                for t in range(TOK):
                    act.wait_ge(hid_turned, b * 2 + t + 1)
                    nc.scalar.activation(low_hi[:, 0:4, t * P:(t + 1) * P],
                                         aux[:, t, :].rearrange("p (c t) -> p c t", c=4),
                                         ACT.Copy).then_inc(hid_hi_ready, 1)

            def gate_function(at, p, b, func, src):
                panel_done(at, p)
                act.wait_ge(hid_ready, b + 1)
                for t in range(TOK):
                    nc.scalar.activation(act_f[:, t, :], src[:, t, :], func, scale=x_inv[:, t:t + 1])
                act.drain().then_inc(act_ready, 1)

            act.sem_inc(hid_ready, 1)
            at = At("ffn_first")
            hi(at, 1, 0, 4)
            x_norm(11)
            act.wait_ge(x_inv_ready, 2)
            gate_function(at, 0, 0, ACT.Sigmoid, pairs[at.pair(0)][:])
            hi(at, 1, 4, 8)
            hi(at, 1, 8, 12)
            hid_turn(0)
            with act.Fori(0, NB1 - 1) as i:
                at = At("ffn", i)
                hi(at, 0, 4, 8)
                hi(at, 1, 0, 4)
                gate_function(at, 0, i + 1, ACT.Sigmoid, pairs[at.pair(0)][:])
                hi(at, 1, 4, 8)
                for j in range(4):
                    hi(at, 2 + j, 0, 2)
                hi(at, 5, 2, 6)
                hid_turn(i + 1)
            at, nxt = At("ffn_last"), At("qk2")
            hi(at, 0, 4, 8)
            squares_of(0, at, 0)
            pieces(3, 0)
            hi(at, 0, 8, 10)
            squares_of(1, at, 1)
            pieces(3, 1)
            hi(at, 0, 10, 12)
            squares_of(2, at, 2)
            pieces(3, 2)
            hi(nxt, 0, 4, 6)
            squares_of(3, at, 3)
            pieces(3, 3)
            hi(nxt, 0, 6, 8)

            at = At("qk2")
            for p in range(4):
                if p:
                    hi(at, p, 4, 8)
                hi(at, p, 8, 12)
                if p == 0:
                    x_norm(12)
                    act.wait_ge(x_inv_ready, 3)
                panel_done(at, p)
                act.wait_ge(qk2_sq, 2 * p + 1)
                for t in range(TOK):
                    nc.scalar.activation(qk_sq[:, t, :], pairs[at.pair(p)][:, t, :], ACT.Square,
                                         scale=x_inv[:, t:t + 1])
                act.drain().then_inc(qk2_sq, 1)
                root(13 + p, inv, inv)
                for t in range(TOK):
                    act.wait_ge(qk2_turned, 2 * p + t + 1)
                    nc.scalar.activation(qk_t[:, 4 * p:4 * p + 4, t * P:(t + 1) * P],
                                         aux[:, t, :].rearrange("p (c t) -> p c t", c=4),
                                         ACT.Copy).then_inc(qk2_copied, 1)
            with act.Fori(0, 2) as i:
                at = At("uv2", i)
                for p in range(2):
                    hi(at, p, 4, 12)
                    panel_done(at, p)
                    for t in range(TOK):
                        nc.scalar.activation(arena[:, bass.ds(i * 2048 + (t * SGU + p * N), N)],
                                             pairs[at.pair(p)][:, t, :], ACT.Gelu, scale=x_inv[:, t:t + 1])
                    act.drain().then_inc(gelu_done, 1)
            at = At("v2")
            for p in range(2):
                hi(at, p, 4, 12)
                if p == 0:
                    root(17, ln_inv, ln_inv)
                panel_done(at, p)
                for t in range(TOK):
                    nc.scalar.activation(vb[:, t, p * N:(p + 1) * N], pairs[at.pair(p)][:, t, :],
                                         ACT.Copy, scale=x_inv[:, t:t + 1])
                act.drain().then_inc(gelu_done, 1)
                if p == 0:
                    act.wait_ge(ws_turned, 1)
                    for b in range(2):
                        nc.scalar.activation(ws_t[:, 4 * b:4 * b + 4, :],
                                             aux[:, b, :].rearrange("p (g i) -> p g i", g=4), ACT.Copy)
                    act.drain().then_inc(ws_ready, 1)
            for b in range(4):
                act.wait_ge(sgu_turned, b + 1)
                nc.scalar.activation(act_t[:, 8 + 2 * b:10 + 2 * b, :],
                                     aux[:, b, :].rearrange("p (c t) -> p c t", c=2), ACT.Copy)
            act.drain().then_inc(sgu_copied, 1)

            with act.Fori(0, 4) as i:
                at = At("gates2", i)
                for p in range(2):
                    head = i * 2 + p
                    act.wait_ge(av_stored, head + PAIRS)
                    nc.scalar.activation(k_head, qk_t[:, bass.ds(head + 8, 1), :].rearrange("p a t -> p (a t)"), ACT.Copy)
                    nc.scalar.activation(v_head, vb[:, :, bass.ds(head * P, P)], ACT.Copy)
                    act.drain().then_inc(head_copied, 1)
                    hi(at, p, 4, 6)
                    act.wait_ge(z_done, head + 1)
                    nc.scalar.activation(z_abs, aux[:, 0, 0:384], ACT.Abs, scale=SB_SCALE)
                    act.drain().then_inc(z_split, 1)
                    nc.scalar.activation(z_abs, z_abs, ACT.Exp, scale=-1.0)
                    act.drain()
                    nc.scalar.activation(z_abs, z_abs, ACT.Ln, bias=1.0).then_inc(z_log, 1)
                    hi(at, p, 6, 8)
                    act.wait_ge(log_a, head + 1)
                    nc.scalar.activation(att, z_neg, ACT.Exp).then_inc(a_exp, 1)
                    hi(at, p, 8, 10)
                    act.wait_ge(av_done, head + PAIRS + 1)
                    nc.scalar.activation(act_t[:, bass.ds(head, 1), :].rearrange("p a t -> p (a t)"),
                                         aux[:, 2, 0:S], ACT.Copy).then_inc(av_stored, 1)
                    hi(at, p, 10, 12)
                    panel_done(at, p)
                    for t in range(TOK):
                        nc.scalar.activation(mix[:, t, bass.ds(head * N, N)], pairs[at.pair(p)][:, t, :],
                                             ACT.Sigmoid, scale=x_inv[:, t:t + 1])
                    act.drain().then_inc(gate_out, 1)
            at = At("mix2")
            refill(0)
            refill(1)
            hi(at, 0, 4, 6)
            refill(2)
            hi(at, 0, 6, 8)
            refill(3)
            hi(at, 0, 8, 12)
            with act.Fori(1, 3) as i:
                hi(At("mix2", i), 0, 4, 12)
            bridge(4, At("mix2", 3), 0, At("out2"))
            at, nxt = At("out2"), At("ffn2_first")
            for p in range(3):
                if p:
                    hi(at, p, 4, 8)
                    squares_of(p - 1, at, p - 1)
                hi(at, p, 8, 12)
            bridge(5, at, 3, nxt, lambda: squares_of(2, at, 2))
            squares_of(3, at, 3)
            at = At("ffn2_first")
            hi(at, 0, 8, 12)
            x_norm(18)
            act.wait_ge(x_inv_ready, 4)
            gate_function(at, 0, NB1, ACT.Relu, pairs[at.pair(0)][:])
            hid_turn(NB1)
            with act.Fori(0, NB2 - 1) as i:
                at = At("ffn2", i)
                hi(at, 0, 4, 8)
                hi(at, 1, 0, 4)
                gate_function(at, 0, i + (NB1 + 1), ACT.Relu, third)
                hi(at, 1, 4, 8)
                hi(at, 4, 2, 6)
                hid_turn(i + (NB1 + 1))
            at = At("ffn2_last")
            hi(at, 0, 4, 8)

        @block.vector
        def _(dve):
            v = nc.vector

            def lo(at, p, k0, k1, width=None):
                for k in range(k0, k1):
                    n = at.panels[p][1] if width is None else width
                    h = (at.gran0 + at.starts[p] + k) % 2
                    dve.wait_ge(hi_ready, at.gran(p, k) + 1)
                    v.tensor_tensor(w_lo[:, at.slot(p, k), :, 0:n],
                                    raw[:, at.raw_slot(p, k), 2 * h:2 * h + 2, 0:n],
                                    w_hi[:, at.slot(p, k), :, 0:n].bitcast(F32),
                                    ALU.subtract).then_inc(lo_ready, 1)

            def panel_done(at, p):
                dve.wait_ge(gran_used, at.end(p) + SPLIT)

            def inverse_root(n_roots, dst, src, count):
                v.tensor_scalar(dst, src, 1.0 / count, EPS, ALU.mult, ALU.add).then_inc(ms_ready, 1)
                dve.wait_ge(rms_ready, n_roots + 1)
                v.reciprocal(dst, dst)
                dve.drain()

            def x_norm(n_sums, n_roots):
                dve.wait_ge(sumsq, n_sums + 1)
                v.tensor_reduce(ss[:, 0:2], x_ss, AX.X, ALU.add)
                dve.drain()
                inverse_root(n_roots, x_inv, ss[:, 0:2], D)
                dve.sem_inc(x_inv_ready, 1)

            def gained(b):
                c = slice(b * N, (b + 1) * N)
                v.tensor_tensor(mix[:, :, c], xres[:, :, c],
                                gain[:, c].unsqueeze(1).broadcast_to([P, TOK, N]), ALU.mult
                                ).then_inc(rows_ready, 2)

            def pieces(n_hi, kq):
                for p in (2 * kq, 2 * kq + 1):
                    dst = slice(p % 2 * P, (p % 2 + 1) * P)
                    dve.wait_ge(lhs_hi_ready, n_hi + p + 1)
                    v.tensor_tensor(lhs_lo[:, 4 * kq:4 * kq + 4, dst],
                                    aux[:, p % 4, :].rearrange("p (c t) -> p c t", c=4),
                                    lhs_hi[:, 4 * kq:4 * kq + 4, dst].bitcast(F32),
                                    ALU.subtract).then_inc(lhs_ready, 1)

            def refill(n_hi, kq):
                dve.wait_ge(lhs_hi_ready, n_hi + kq + 1)
                c = slice(4 * kq, 4 * kq + 4)
                v.tensor_tensor(lhs_lo[:, c, :], act_t[:, c, :], lhs_hi[:, c, :].bitcast(F32),
                                ALU.subtract).then_inc(lhs_ready, 2)

            def bridge(n_hi, at, p, nxt, last_rows, between=None):
                lo(at, p, 4, 6)
                pieces(n_hi, 0)
                lo(at, p, 6, 8)
                if between is not None:
                    between()
                pieces(n_hi, 1)
                lo(at, p, 8, 10)
                pieces(n_hi, 2)
                lo(at, p, 10, 12)
                last_rows()
                lo(nxt, 0, 4, 6)
                pieces(n_hi, 3)
                lo(nxt, 0, 6, 8)

            def rope(dst, src, tmp_a, tmp_b, heads):
                def table(t):
                    return t if heads is None else t.unsqueeze(2).broadcast_to([P, TOK, heads, ROPE])
                def halves(ap):
                    if heads is None:
                        return ap[:, :, 0:HALF], ap[:, :, HALF:ROPE]
                    return ap[:, :, :, 0:HALF], ap[:, :, :, HALF:ROPE]
                c, s = table(cosd[:]), table(sind[:])
                v.tensor_tensor(tmp_a, src, c, ALU.mult)
                v.tensor_tensor(halves(tmp_b)[0], halves(src)[1], halves(s)[0], ALU.mult)
                v.tensor_tensor(halves(tmp_b)[1], halves(src)[0], halves(s)[1], ALU.mult)
                dve.drain()
                v.tensor_tensor(dst, tmp_a, tmp_b, ALU.add)
                dve.drain()

            dve.sem_inc(lo_ready, LO_CREDIT)
            dve.sem_inc(evac_done, EVAC_CREDIT)
            def rope_angles():
                dve.wait_ge(loaded["con"], 16)
                dve.wait_ge(loaded["pos"], 16)
                v.tensor_copy(pos_f, pos_i[:])
                dve.drain()
                ang, turns = junk[:, 0:64].rearrange("p (t f) -> p t f", t=TOK), junk[:, 64:128].rearrange(
                    "p (t f) -> p t f", t=TOK)
                for t in range(TOK):
                    v.tensor_scalar(ang[:, t, :], freq, pos_f[:, t:t + 1], None, ALU.mult)
                dve.drain()
                v.tensor_scalar(turns, ang, float(1 / TWO_PI), MAGIC, ALU.mult, ALU.add)
                dve.drain()
                v.tensor_scalar(turns, turns, -MAGIC, None, ALU.add)
                dve.drain()
                for c in (PI_1, PI_2, PI_3):
                    v.scalar_tensor_tensor(ang, turns, -float(c), ang, ALU.mult, ALU.add)
                    dve.drain()
                v.tensor_scalar(sind[:, :, 0:HALF], ang, PI_MAX, -PI_MAX, ALU.min, ALU.max)
                v.tensor_scalar(ang, ang, float(TWO_PI / 4), None, ALU.add)
                dve.drain()
                v.tensor_scalar(turns, ang, float(TWO_PI / 2), -float(TWO_PI), ALU.is_gt, ALU.mult)
                dve.drain()
                v.tensor_tensor(ang, ang, turns, ALU.add)
                dve.drain()
                v.tensor_scalar(cosd[:, :, HALF:ROPE], ang, PI_MAX, -PI_MAX, ALU.min, ALU.max)
                dve.drain().then_inc(angles, 1)

            def rope_tables():
                dve.wait_ge(sines, 1)
                v.tensor_copy(cosd[:, :, HALF:ROPE], cosd[:, :, 0:HALF])
                v.tensor_scalar(sind[:, :, 0:HALF], sind[:, :, HALF:ROPE], -1.0, None, ALU.mult)

            at = At("in")
            for b in range(4):
                dve.wait_ge(x_loaded[b], 32)
                gained(b)
                lo(at, 0, 2 * b, 2 * b + 2)
                pieces(0, b)
            x_norm(0, 0)
            rope_angles()

            def low_norm(p, n_sums, n_roots, gains, rows):
                dve.wait_ge(sumsq, n_sums + 1)
                inverse_root(n_roots, cq_inv, cq_ss, Q_RANK)
                v.tensor_tensor(cq_inv, cq_inv, x_inv, ALU.mult)
                dve.drain()
                for t in range(TOK):
                    ins = v.scalar_tensor_tensor(rows[:, t, :], pairs[at.pair(p)][:, t, :],
                                                 cq_inv[:, t:t + 1], gains, ALU.mult, ALU.mult)
                dve.drain().then_inc(evac_done, 1)

            for p in range(1, 5):
                lo(at, p, 0, 4)
                panel_done(at, p - 1)
                if p <= 2:
                    for t in range(TOK):
                        v.tensor_scalar(u_rows[:, t, (p - 1) * N:p * N], pairs[at.pair(p - 1)][:, t, :],
                                        x_inv[:, t:t + 1], None, ALU.mult)
                    dve.drain().then_inc(evac_done, 1)
                if p == 2:
                    rope_tables()
                if p == 3:
                    dve.wait_ge(loaded["qk"], 32)
                    dve.wait_ge(kr_sq, 1)
                    for t in range(TOK):
                        v.scalar_tensor_tensor(krr[:, t, :], pairs[at.pair(2)][:, t, 0:ROPE],
                                               x_inv[:, t:t + 1], gain_k[:, NOPE:QK], ALU.mult, ALU.mult)
                    dve.drain().then_inc(evac_done, 1)
                    ta = junk[:, 128:256].rearrange("p (t f) -> p t f", t=TOK)
                    tb = junk[:, 256:384].rearrange("p (t f) -> p t f", t=TOK)
                    rope(krr[:], krr[:], ta, tb, None)
                if p == 4:
                    dve.wait_ge(loaded["cq"], 32)
                    low_norm(3, 1, 1, gain_cq, cq_rows)
                lo(at, p, 4, 8)
            nxt = At("pool")
            lo(nxt, 0, 0, 4)
            panel_done(at, 4)
            low_norm(4, 2, 2, gain_ckv, ckv_rows)
            dve.sem_inc(low_rows, 1)
            for j in range(8):
                dve.wait_ge(low_hi_ready, j // 2 * 2 + 2)
                v.scalar_tensor_tensor(low_lo[:, j, :], aux[:, j // 2, (j % 2) * S:(j % 2 + 1) * S],
                                       cols[:, j:j + 1], low_hi[:, j, :].bitcast(F32),
                                       ALU.mult, ALU.subtract).then_inc(low_ready, 1)
            with dve.Fori(0, 2) as i:
                at = At("pool", i)
                for p in range(2):
                    lo(at, p, 4, 8)
                    panel_done(at, p)
                    v.tensor_copy(mix[:, :, bass.ds(i * (2 * N) + p * N, N)], pairs[at.pair(p)][:]
                                  ).then_inc(evac_done, 1)
            for q in range(4):
                dve.wait_ge(low_hi_ready, 8 + q + 1)
                c0, t = 4 * (q // 2), q % 2
                v.tensor_tensor(low_lo[:, c0:c0 + 4, t * P:(t + 1) * P],
                                aux[:, q, :].rearrange("p (c t) -> p c t", c=4),
                                low_hi[:, c0:c0 + 4, t * P:(t + 1) * P].bitcast(F32),
                                ALU.subtract).then_inc(low_ready, 1)

            def per_head(scales, first, n):
                return scales[:, first:first + 4].rearrange("p (t h) -> p t h", t=TOK).unsqueeze(3).broadcast_to(
                    [P, TOK, 2, n])

            def attend_a(u):
                v.tensor_tensor(ss[:, 4:8].rearrange("p (t h) -> p t h", t=TOK),
                                ss[:, 4:8].rearrange("p (t h) -> p t h", t=TOK),
                                kr_ss.unsqueeze(2).broadcast_to([P, TOK, 2]), ALU.add)
                dve.drain()
                inverse_root(u + 2, inv, ss, QK)
                v.tensor_tensor(q_rows, q_rows, per_head(inv, 0, QK), ALU.mult)
                v.tensor_tensor(k_rows[:, :, :, 0:NOPE], k_rows[:, :, :, 0:NOPE], per_head(inv, 4, NOPE),
                                ALU.mult)
                v.tensor_tensor(k_rows[:, :, :, NOPE:QK], krr[:].unsqueeze(2).broadcast_to([P, TOK, 2, ROPE]),
                                per_head(inv, 4, ROPE), ALU.mult)
                dve.drain()

            def attend_b(u):
                qr = q_rows[:, :, :, NOPE:QK]
                rope(qr, qr, rope_a, rope_b, 2)
                dve.sem_inc(qk_done, 1)

            def attend_c(u):
                dve.wait_ge(scored, u)
                v.scalar_tensor_tensor(probs, aux[:, 0:2, 0:384], SM_SCALE,
                                       causal.unsqueeze(1).broadcast_to([P, 2, 384]), ALU.mult, ALU.add)
                dve.drain()
                v.tensor_reduce(row_max[:, 0:2], probs[:, :, 0:P], AX.X, ALU.max)
                v.tensor_reduce(row_max[:, 2:4], probs[:, :, P:3 * P], AX.X, ALU.max)
                dve.drain()
                v.tensor_scalar(row_max, row_max, -1.0, None, ALU.mult).then_inc(max_ready, 1)
                dve.wait_ge(exp_done, u)
                v.reciprocal(row_inv, row_sum)
                dve.drain()
                v.tensor_tensor(probs[:, :, 0:P], probs[:, :, 0:P],
                                row_inv[:, 0:2].unsqueeze(2).broadcast_to([P, 2, P]), ALU.mult)
                v.tensor_tensor(probs[:, :, P:3 * P], probs[:, :, P:3 * P],
                                row_inv[:, 2:4].unsqueeze(2).broadcast_to([P, 2, 2 * P]), ALU.mult)
                dve.drain().then_inc(p_ready, 1)

            def sub(at, p, u, has_last, last=False):
                if has_last:
                    attend_a(u)
                lo(at, p, 4, 6)
                if has_last:
                    attend_b(u)
                lo(at, p, 6, 8)
                lo(at, p + 1, 0, 2)
                if has_last:
                    attend_c(u)
                lo(at, p + 2, 0, 2)
                panel_done(at, p)
                dve.wait_ge(loaded["bias"], u * 16 + 16)
                for t in range(TOK):
                    v.scalar_tensor_tensor(gate_tmp[:, t, :], pairs[at.pair(p)][:, t, :], x_inv[:, t:t + 1],
                                           bias, ALU.mult, ALU.add)
                dve.drain().then_inc(evac_done, 1)
                dve.sem_inc(gate_in, 1)
                dve.sem_inc(bias_used, 1)
                dve.wait_ge(q_sq, u * 2 + 1)
                v.tensor_reduce(ss[:, 0:4].rearrange("p (t h) -> p t h", t=TOK), squares, AX.X, ALU.add)
                dve.drain().then_inc(q_sq, 1)
                qp = pairs[at.pair(p + 1)][:, :, 0:2 * QK].rearrange("p t (h d) -> p t h d", h=2)
                v.tensor_tensor(q_rows, qp, gain_q.unsqueeze(1).unsqueeze(1).broadcast_to([P, TOK, 2, QK]),
                                ALU.mult)
                dve.drain().then_inc(evac_done, 1)
                lo(at, p + 2, 2, 4, N)
                if last:
                    dve.wait_ge(av_stored, PAIRS - 2)
                    refill(8, 0)
                dve.wait_ge(gate_out, u + 1)
                m = mix[:, :, bass.ds(u * N, N)]
                v.tensor_tensor(m, m, gate_tmp, ALU.mult)
                dve.wait_ge(kv_sq, u + 1)
                v.tensor_reduce(ss[:, 4:8].rearrange("p (t h) -> p t h", t=TOK), squares[:, :, :, 0:NOPE],
                                AX.X, ALU.add)
                kp = pairs[at.pair(p + 2)][:].rearrange("p t (h d) -> p t h d", h=2)[:, :, :, 0:NOPE]
                v.tensor_tensor(k_rows[:, :, :, 0:NOPE], kp,
                                gain_k[:, 0:NOPE].unsqueeze(1).unsqueeze(1).broadcast_to([P, TOK, 2, NOPE]),
                                ALU.mult)
                dve.drain().then_inc(evac_done, 1)
                lo(at, p + 2, 4, 6, N)
                if last:
                    refill(8, 1)
                    refill(8, 2)

            dve.wait_ge(mix_ones, 1)
            sub(At("heads_first"), 0, 0, False)
            with dve.Fori(0, (PAIRS - 2) // 2) as i:
                for s in range(2):
                    sub(At("heads", i), 3 * s, i * 2 + (1 + s), True)
            sub(At("heads_last"), 0, PAIRS - 1, True, True)

            def add_branch(pair, col):
                a = mix[:, :, bass.ds(col + D, N)]
                m = mix[:, :, bass.ds(col, N)]
                v.tensor_tensor(a, a, pairs[pair][:], ALU.mult)
                dve.drain().then_inc(evac_done, 1)
                v.tensor_tensor(m, m, a, ALU.add)
                dve.drain().then_inc(rows_ready, 2)

            def add_x(at, p, col, pair=None):
                panel_done(at, p)
                xs = xres[:, :, col:col + N]
                ps = pairs[at.pair(p) if pair is None else pair][:]
                v.tensor_tensor(xs, xs, ps, ALU.add)
                dve.drain().then_inc(evac_done, 1)

            at = At("attn_o")
            attend_a(PAIRS)
            lo(at, 0, 4, 6)
            attend_b(PAIRS)
            lo(at, 0, 6, 10)
            attend_c(PAIRS)
            lo(at, 0, 10, 14)
            dve.sem_inc(evac_done, 2)
            dve.wait_ge(av_stored, PAIRS)
            refill(8, 3)
            dve.sem_inc(side_go, 1)
            lo(at, 0, 14, 18)
            panel_done(at, 2)
            add_branch(at.pair(2), 0)
            lo(at, 0, 18, 20)
            panel_done(at, 3)
            add_branch(at.pair(3), N)
            lo(at, 0, 20, 28)
            panel_done(at, 4)
            add_branch(at.pair(4), 2 * N)

            def last_branch():
                panel_done(at, 5)
                add_branch(at.pair(5), 3 * N)

            bridge(12, at, 5, At("out"), last_branch)

            def out_panels(at, nxt, n_hi, n_gains):
                lo(at, 0, 8, 12)
                add_x(at, 0, 0)
                dve.wait_ge(loaded["gain"], 16 * n_gains)
                gained(0)
                for p in range(1, 3):
                    lo(at, p, 4, 12)
                    add_x(at, p, p * N)
                    gained(p)

                def last_block():
                    add_x(at, 3, 3 * N)
                    gained(3)

                bridge(n_hi, at, 3, nxt, last_block)

            out_panels(At("out"), At("ffn_first"), 20, 1)

            def hid_turn(b):
                for t in range(TOK):
                    dve.wait_ge(hid_hi_ready, b * 2 + t + 1)
                    v.tensor_tensor(low_lo[:, 0:4, t * P:(t + 1) * P],
                                    aux[:, t, :].rearrange("p (c t) -> p c t", c=4),
                                    low_hi[:, 0:4, t * P:(t + 1) * P].bitcast(F32),
                                    ALU.subtract).then_inc(hid_lo_ready, 1)

            def silu_gate(at, p, b):
                dve.wait_ge(act_ready, b + 1)
                for t in range(TOK):
                    v.scalar_tensor_tensor(hid[:, t, :], pairs[at.pair(p)][:, t, :], x_inv[:, t:t + 1],
                                           act_f[:, t, :], ALU.mult, ALU.mult)
                dve.drain().then_inc(evac_done, 1)

            def times_up(at, p):
                panel_done(at, p)
                for t in range(TOK):
                    v.scalar_tensor_tensor(hid[:, t, :], pairs[at.pair(p)][:, t, :], x_inv[:, t:t + 1],
                                           hid[:, t, :], ALU.mult, ALU.mult)
                dve.drain().then_inc(evac_done, 1)
                dve.sem_inc(hid_ready, 1)

            dve.drain()
            dve.sem_inc(side_go, 1)
            at = At("ffn_first")
            lo(at, 1, 0, 4)
            x_norm(3, 11)
            silu_gate(at, 0, 0)
            lo(at, 1, 4, 8)
            lo(at, 1, 8, 12)
            times_up(at, 1)
            hid_turn(0)
            with dve.Fori(0, NB1 - 1) as i:
                at = At("ffn", i)
                lo(at, 0, 4, 8)
                lo(at, 1, 0, 4)
                silu_gate(at, 0, i + 1)
                lo(at, 1, 4, 8)
                lo(at, 2, 0, 2)
                lo(at, 3, 0, 2)
                times_up(at, 1)
                for j in range(4):
                    lo(at, 2 + j, 4, 6)
                    add_x(at, 2 + j, j * N)
                hid_turn(i + 1)
            at, nxt = At("ffn_last"), At("qk2")
            dve.wait_ge(loaded["gain"], 32)
            for j in range(4):
                lo(at, j, 4, 6)
                add_x(at, j, j * N)
                gained(j)
                if j:
                    pieces(28, j - 1)
            lo(nxt, 0, 4, 6)
            pieces(28, 3)
            lo(nxt, 0, 6, 8)

            dve.sem_inc(qk2_sq, 1)
            at = At("qk2")
            dve.drain()
            dve.sem_inc(side_go, 1)
            dve.wait_ge(loaded["qk2"], 32)
            for p in range(4):
                if p:
                    lo(at, p, 4, 8)
                lo(at, p, 8, 12)
                if p == 0:
                    x_norm(4, 12)
                dve.wait_ge(qk2_sq, 2 * p + 2)
                v.tensor_reduce(ss.rearrange("p (t h) -> p t h", t=TOK),
                                qk_sq.rearrange("p t (h d) -> p t h d", h=4), AX.X, ALU.add)
                dve.drain().then_inc(qk2_sq, 1)
                inverse_root(13 + p, inv, ss, P)
                v.tensor_tensor(inv_x.rearrange("p (t h) -> p t h", t=TOK),
                                inv.rearrange("p (t h) -> p t h", t=TOK),
                                x_inv.unsqueeze(2).broadcast_to([P, TOK, 4]), ALU.mult)
                dve.drain()
                rows = qk_rows.rearrange("p t (h d) -> p t h d", h=4)
                v.tensor_tensor(rows, pairs[at.pair(p)][:].rearrange("p t (h d) -> p t h d", h=4),
                                inv_x.rearrange("p (t h) -> p t h", t=TOK).unsqueeze(3).broadcast_to(
                                    [P, TOK, 4, P]), ALU.mult)
                dve.drain().then_inc(evac_done, 1)
                v.tensor_tensor(qk_rows, qk_rows, gain_qk[:, p * N:(p + 1) * N].unsqueeze(1).broadcast_to(
                    [P, TOK, N]), ALU.mult)
                dve.drain().then_inc(qk2_ready, 1)
                dve.wait_ge(qk2_turned, 2 * p + 2)
            with dve.Fori(0, 2) as i:
                at = At("uv2", i)
                for p in range(2):
                    lo(at, p, 4, 12)
                    dve.wait_ge(gelu_done, i * 2 + p + 1)
                    dve.sem_inc(evac_done, 1)

            def layer_norm():
                st = ln_stats.rearrange("p (t c s) -> p t c s", t=TOK, c=2)
                for t in range(TOK):
                    for c in range(2):
                        v.bn_stats(st[:, t, c, :], vs[:, t, c * N:(c + 1) * N])
                dve.drain()
                for t in range(TOK):
                    v.bn_aggr(ln_mv[:, 2 * t:2 * t + 2], st[:, t, :, :])
                dve.drain()
                inverse_root(17, ln_inv, ln_mv.rearrange("p (t s) -> p s t", s=2)[:, 1, :], 1)
                for t in range(TOK):
                    v.tensor_scalar(vs[:, t, :], vs[:, t, :], ln_mv[:, 2 * t:2 * t + 1], ln_inv[:, t:t + 1],
                                    ALU.subtract, ALU.mult)
                dve.drain()

            at = At("v2")
            lo(at, 0, 4, 12)
            layer_norm()
            dve.wait_ge(gelu_done, 5)
            dve.sem_inc(evac_done, 1)
            dve.wait_ge(loaded["ln"], 48)
            v.tensor_tensor(vs, vs, ln_g.unsqueeze(1).broadcast_to([P, TOK, SGU]), ALU.mult)
            dve.drain()
            lo(at, 1, 4, 8)
            v.tensor_tensor(vs, vs, ln_b.unsqueeze(1).broadcast_to([P, TOK, SGU]), ALU.add)
            dve.wait_ge(ws_ready, 1)
            v.memset(ws_t[CHUNK:P, :, 0:CHUNK], 0.0)
            dve.drain().then_inc(ln_done, 1)
            lo(at, 1, 8, 12)
            dve.wait_ge(gelu_done, 6)
            dve.sem_inc(evac_done, 1)
            for g in range(GROUPS):
                dve.wait_ge(sgu_mm, g // 2 + 1)
                c = slice(g * P, (g + 1) * P)
                v.scalar_tensor_tensor(us[:, :, c],
                                       aux[:, g // 2, (g % 2) * S:(g % 2 + 1) * S].rearrange("p (t d) -> p t d", t=TOK),
                                       cols[:, 8 + g:9 + g], us[:, :, c], ALU.add, ALU.mult)
            dve.drain().then_inc(sgu_rows, 1)
            dve.wait_ge(sgu_copied, 1)

            with dve.Fori(0, 4) as i:
                at = At("gates2", i)
                for p in range(2):
                    head = i * 2 + p
                    lo(at, p, 4, 6)
                    dve.wait_ge(z_split, head + 1)
                    z = aux[:, 0, 0:384]
                    v.tensor_scalar(z_pos, z, SB_SCALE, 0.0, ALU.mult, ALU.max)
                    v.tensor_scalar(z_neg, z, SB_SCALE, 0.0, ALU.mult, ALU.min)
                    dve.drain()
                    dve.wait_ge(z_log, head + 1)
                    v.tensor_tensor(z_pos, z_pos, z_abs, ALU.add)
                    v.tensor_tensor(z_neg, z_neg, z_abs, ALU.subtract)
                    dve.drain()
                    for c in (0, 2 * P):
                        v.tensor_tensor(z_pos[:, c:c + P], z_pos[:, c:c + P], past, ALU.mult)
                    dve.drain().then_inc(keep_ready, 1)
                    lo(at, p, 6, 8)
                    dve.wait_ge(tail_done, head + 1)
                    v.tensor_tensor(z_neg, z_neg, aux[:, 1, 0:384], ALU.subtract).then_inc(log_a, 1)
                    dve.wait_ge(a_exp, head + 1)
                    for c in (0, 2 * P):
                        v.tensor_tensor(att[:, c:c + P], att[:, c:c + P], past, ALU.mult)
                    dve.drain().then_inc(a_ready, 1)
                    lo(at, p, 8, 12)
                    dve.wait_ge(gate_out, head + PAIRS + 1)
                    dve.sem_inc(evac_done, 1)
            at = At("mix2")
            dve.wait_ge(av_stored, 2 * PAIRS)

            def mix_turn(at, i):
                m = mix[:, :, bass.ds(i * N, N)]
                panel_done(at, 0)
                v.tensor_tensor(m, m, pairs[at.pair(0)][:], ALU.mult)
                dve.drain().then_inc(evac_done, 1)

            dve.sem_inc(side_go, 1)
            refill(36, 0)
            refill(36, 1)
            lo(at, 0, 4, 6)
            refill(36, 2)
            lo(at, 0, 6, 8)
            refill(36, 3)
            mix_turn(at, 0)
            lo(at, 0, 8, 12)
            panel_done(at, 1)
            add_branch(at.pair(1), 0)
            with dve.Fori(1, 3) as i:
                at = At("mix2", i)
                lo(at, 0, 4, 8)
                mix_turn(at, i)
                lo(at, 0, 8, 12)
                panel_done(at, 1)
                add_branch(at.pair(1), i * N)
            at = At("mix2", 3)

            def last_mix():
                panel_done(at, 1)
                add_branch(at.pair(1), 3 * N)

            bridge(40, at, 0, At("out2"), last_mix, lambda: mix_turn(at, 3))
            out_panels(At("out2"), At("ffn2_first"), 48, 3)
            at = At("ffn2_first")

            def relu_square(at, b, src):
                dve.wait_ge(act_ready, b + 1)
                for t in range(TOK):
                    v.scalar_tensor_tensor(hid[:, t, :], src[:, t, :], x_inv[:, t:t + 1], act_f[:, t, :],
                                           ALU.mult, ALU.mult)
                dve.drain().then_inc(evac_done, 1)
                dve.sem_inc(hid_ready, 1)

            lo(at, 0, 8, 12)
            x_norm(5, 18)
            relu_square(at, NB1, pairs[at.pair(0)][:])
            hid_turn(NB1)
            with dve.Fori(0, NB2 - 1) as i:
                at = At("ffn2", i)
                lo(at, 0, 4, 8)
                lo(at, 1, 0, 4)
                relu_square(at, i + (NB1 + 1), third)
                for j in range(4):
                    lo(at, 1 + j, 4, 6)
                    add_x(at, 1 + j, j * N, j % 2)
                hid_turn(i + (NB1 + 1))
            at = At("ffn2_last")
            for j in range(4):
                if j < 2:
                    lo(at, j, 4, 6)
                add_x(at, j, j * N, j % 2)

        @block.tensor
        def _(pe):
            def group(at, p, g, left, c0, ps, start, stop):
                kch, n = at.panels[p]
                hi_t, lo_t = left
                for h in range(2):
                    k = 2 * g + h
                    pe.wait_ge(lo_ready, at.gran(p, k) + 1 + LO_CREDIT)
                    s = at.slot(p, k)
                    for c in range(2):
                        ch = 2 * k + c
                        for t in range(TOK):
                            tok = slice(t * P, (t + 1) * P)
                            x_hi, x_lo = hi_t[:, c0 + ch, tok], lo_t[:, c0 + ch, tok]
                            nc.tensor.matmul(ps[:, t, 0:n], x_hi, w_hi[:, s, c, 0:n],
                                             start=start and ch == 0, stop=False)
                            nc.tensor.matmul(ps[:, t, 0:n], x_hi, w_lo[:, s, c, 0:n], start=False, stop=False)
                            mm = nc.tensor.matmul(ps[:, t, 0:n], x_lo, w_hi[:, s, c, 0:n], start=False,
                                                  stop=stop and ch == kch - 1)
                    mm.then_inc(gran_used, 1)

            def bank_free(at, p):
                pe.wait_ge(evac_done, at.panel(p) - 1 + EVAC_CREDIT)

            def gemm(at, p, left, c0=0, groups=None, ps=None, start=True, stop=True):
                ps = pairs[at.pair(p)] if ps is None else ps
                kch = at.panels[p][0]
                groups = range(kch // 4) if groups is None else groups
                if groups[0] == 0:
                    bank_free(at, p)
                for g in groups:
                    group(at, p, g, left, c0, ps, start, stop)

            wide, low = (lhs_hi, lhs_lo), (low_hi, low_lo)

            def turn(dst, src):
                return nc.tensor.transpose(dst, src, ident[0:src.shape[0], :])

            def pieces(r, f, kq):
                pe.wait_ge(rows_ready, 8 * r + 2 * kq + 2)
                for p in (2 * kq, 2 * kq + 1):
                    if p >= 4:
                        pe.wait_ge(lhs_ready, 8 * f + p - 3)
                    for c in range(4):
                        ins = turn(aux[:, p % 4, c * P:(c + 1) * P],
                                   mix[:, p % 2, (4 * kq + c) * P:(4 * kq + c + 1) * P])
                    ins.then_inc(turned, 1)

            def gemm_after(at, f, left, c0=0, r=None, ps=None):
                for g in range(4):
                    pe.wait_ge(lhs_ready, 8 * f + 2 * g + 2)
                    gemm(at, 0, left, c0, [g], ps)
                    if g == 1:
                        pieces(r, f, 3)

            def last_panel(at, p, r, f):
                for g in range(4):
                    gemm(at, p, wide, groups=[g])
                    if g < 3:
                        pieces(r, f, g)

            pe.wait_ge(ident_loaded, 16)
            at = At("in")
            pieces(0, 0, 0)
            for g in range(4):
                if g < 3:
                    pieces(0, 0, g + 1)
                pe.wait_ge(lhs_ready, 2 * g + 2)
                gemm(at, 0, wide, groups=[g])
            for p in range(1, 4):
                gemm(at, p, wide)
            pe.wait_ge(evac_done, 2 + EVAC_CREDIT)
            pe.wait_ge(loaded["pool"], 32)
            for c in range(8):
                dst = aux[:, c // 2, (c % 2) * S:(c % 2 + 1) * S]
                ch = slice(c * P, (c + 1) * P)
                nc.tensor.matmul(dst, u_rows[:, 0, ch], pool_a[:, c // 2, 0:S], start=True, stop=False)
                mm = nc.tensor.matmul(dst[:, P:S], u_rows[:, 1, ch], pool_a[:, c // 2, S:S + P],
                                      start=False, stop=True)
                if c % 2:
                    mm.then_inc(pool_mm, 1)
            gemm(at, 4, wide)
            pe.wait_ge(pool_out, 1)
            for j in range(8):
                dst = aux[:, j // 2, (j % 2) * S:(j % 2 + 1) * S]
                g, d = j // 2, j % 2
                for c in range(2):
                    mm = nc.tensor.matmul(dst, w_grp[:, g, c, d * P:(d + 1) * P], act_t[:, 2 * g + c, :],
                                          start=c == 0, stop=c == 1)
                if j % 2:
                    mm.then_inc(pool_mm, 1)
            pe.wait_ge(low_ready, 8)
            with pe.Fori(0, 2) as i:
                for p in range(2):
                    gemm(At("pool", i), p, low)
            pe.wait_ge(low_rows, 1)
            for q in range(4):
                rows = cq_rows if q < 2 else ckv_rows
                for c in range(4):
                    ins = turn(aux[:, q, c * P:(c + 1) * P], rows[:, q % 2, c * P:(c + 1) * P])
                ins.then_inc(low_turned, 1)

            def turn_qk(u):
                pe.wait_ge(qk_done, u)
                for h in range(2):
                    for t in range(TOK):
                        c = slice(h * S + t * P, h * S + (t + 1) * P)
                        turn(aux[:, 0, c], q_rows[:, t, h, 0:NOPE])
                        turn(aux[:, 1, c], k_rows[:, t, h, 0:NOPE])
                        turn(aux[0:ROPE, 2, c], q_rows[:, t, h, NOPE:QK])
                        ins = turn(aux[0:ROPE, 3, c], k_rows[:, t, h, NOPE:QK])
                ins.then_inc(qk_turned, 1)

            def score(u):
                pe.wait_ge(qk_copied, u)
                for h in range(2):
                    for t in range(TOK):
                        c = slice(0, P) if t == 0 else slice(P, 3 * P)
                        keys = slice(0, (t + 1) * P)
                        tok = slice(t * P, (t + 1) * P)
                        nc.tensor.matmul(aux[:, h, c], q_tn[:, h, tok], k_tn[:, h, keys], start=True, stop=False)
                        mm = nc.tensor.matmul(aux[:, h, c], q_tr[0:ROPE, h, tok], k_tr[0:ROPE, h, keys],
                                              start=False, stop=True)
                mm.then_inc(scored, 1)

            def turn_p(u):
                pe.wait_ge(p_ready, u)
                for h in range(2):
                    for b in range(3):
                        ins = turn(aux[:, 2 + h, b * P:(b + 1) * P], probs[:, h, b * P:(b + 1) * P])
                ins.then_inc(p_turned, 1)

            def values(u):
                pe.wait_ge(p_copied, u)
                for h in range(2):
                    dst = aux[:, 0, h * S:(h + 1) * S]
                    nc.tensor.matmul(dst, v_rows[:, 0, h, :], p_t[:, h, 0:S], start=True, stop=False)
                    mm = nc.tensor.matmul(dst[:, P:S], v_rows[:, 1, h, :], p_t[:, h, S:S + P],
                                          start=False, stop=True)
                mm.then_inc(av_done, 1)

            def sub(at, p, u, has_last):
                gemm(at, p, wide, groups=[0, 1])
                if has_last:
                    turn_qk(u)
                gemm(at, p, wide, groups=[2])
                if has_last:
                    score(u)
                gemm(at, p, wide, groups=[3])
                if has_last:
                    turn_p(u)
                gemm(at, p + 1, low)
                if has_last:
                    values(u)
                gemm(at, p + 2, low, 4)

            pe.wait_ge(low_ready, 12)
            sub(At("heads_first"), 0, 0, False)
            with pe.Fori(0, (PAIRS - 2) // 2) as i:
                for s in range(2):
                    sub(At("heads", i), 3 * s, i * 2 + (1 + s), True)
            sub(At("heads_last"), 0, PAIRS - 1, True)
            at = At("attn_o")
            pe.wait_ge(lhs_ready, 10)
            gemm(at, 0, wide, groups=[0], stop=False)
            pe.wait_ge(lhs_ready, 12)
            gemm(at, 0, wide, groups=[1], stop=False)
            turn_qk(PAIRS)
            pe.wait_ge(lhs_ready, 14)
            gemm(at, 0, wide, groups=[2], stop=False)
            score(PAIRS)
            gemm(at, 1, wide, groups=[0], stop=False)
            turn_p(PAIRS)
            gemm(at, 1, wide, groups=[1], stop=False)
            values(PAIRS)
            gemm(at, 1, wide, groups=[2], stop=False)
            pe.wait_ge(lhs_ready, 16)
            for p in range(2):
                gemm(at, 2 + p, wide, KC - 4, start=False)
            gemm(at, 4, wide)
            last_panel(at, 5, 1, 2)
            at = At("out")
            gemm_after(at, 2, wide, 0, 1)
            for p in range(1, 3):
                gemm(at, p, wide)
            last_panel(at, 3, 2, 3)

            def hid_turn(b):
                pe.wait_ge(hid_ready, b + 2)
                for t in range(TOK):
                    for c in range(4):
                        ins = turn(aux[:, t, c * P:(c + 1) * P], hid[:, t, c * P:(c + 1) * P])
                    ins.then_inc(hid_turned, 1)

            at = At("ffn_first")
            gemm_after(at, 3, wide, 0, 2)
            gemm(at, 1, wide)
            hid_turn(0)
            with pe.Fori(0, NB1 - 1) as i:
                at = At("ffn", i)
                gemm(at, 0, wide)
                gemm(at, 1, wide)
                pe.wait_ge(hid_lo_ready, i * 2 + 2)
                for j in range(4):
                    gemm(at, 2 + j, low)
                hid_turn(i + 1)
            pe.wait_ge(hid_lo_ready, 2 * NB1)
            for j in range(4):
                gemm(At("ffn_last"), j, low)
                if j:
                    pieces(3, 4, j - 1)

            at = At("qk2")
            gemm_after(at, 4, wide, 0, 3)

            def turn_qk2(p):
                pe.wait_ge(qk2_ready, p + 1)
                if p:
                    pe.wait_ge(qk2_copied, 2 * p)
                for t in range(TOK):
                    for c in range(4):
                        ins = turn(aux[:, t, c * P:(c + 1) * P], qk_rows[:, t, c * P:(c + 1) * P])
                    ins.then_inc(qk2_turned, 1)

            for p in range(1, 4):
                gemm(at, p, wide, groups=[0, 1])
                turn_qk2(p - 1)
                gemm(at, p, wide, groups=[2, 3])
            turn_qk2(3)
            with pe.Fori(0, 2) as i:
                for p in range(2):
                    gemm(At("uv2", i), p, wide)
            at = At("v2")
            pe.wait_ge(loaded["ln"], 48)
            pe.wait_ge(qk2_copied, 8)
            for g in range(GROUPS):
                ins = turn(aux[:, g // 4, (g % 4) * P:(g % 4 + 1) * P], ws_raw[:, g, :])
            ins.then_inc(ws_turned, 1)
            gemm(at, 0, wide)
            gemm(at, 1, wide)
            pe.wait_ge(ln_done, 1)
            for g in range(GROUPS):
                mm = nc.tensor.matmul(aux[:, g // 2, (g % 2) * S:(g % 2 + 1) * S].rearrange("p (t d) -> p t d", t=TOK),
                                      ws_t[:, g, :], vs[:, :, g * P:(g + 1) * P], start=True, stop=True)
                if g % 2:
                    mm.then_inc(sgu_mm, 1)
            pe.wait_ge(sgu_rows, 1)
            for c in range(8):
                for t in range(TOK):
                    ins = turn(aux[:, c // 2, (c % 2) * S + t * P:(c % 2) * S + (t + 1) * P],
                               us[:, t, c * P:(c + 1) * P])
                if c % 2:
                    ins.then_inc(sgu_turned, 1)
            pe.wait_ge(sgu_copied, 1)

            with pe.Fori(0, 4) as i:
                at = At("gates2", i)
                for p in range(2):
                    head = i * 2 + p
                    gemm(at, p, wide, groups=[0])
                    pe.wait_ge(head_copied, head + 1)
                    q_head = qk_t[:, bass.ds(head, 1), :].rearrange("p a t -> p (a t)")
                    nc.tensor.matmul(aux[:, 0, 0:S], k_head[:, 0:P], q_head, start=True, stop=True)
                    nc.tensor.matmul(aux[:, 0, S:S + P], k_head[:, P:S],
                                     qk_t[:, bass.ds(head, 1), P:S].rearrange("p a t -> p (a t)"),
                                     start=True, stop=True).then_inc(z_done, 1)
                    gemm(at, p, wide, groups=[1])
                    pe.wait_ge(keep_ready, head + 1)
                    nc.tensor.matmul(aux[:, 1, 0:384], after, z_pos, start=True, stop=False)
                    nc.tensor.matmul(aux[:, 1, P:S], ones, z_pos[:, S:S + P], start=False, stop=True
                                     ).then_inc(tail_done, 1)
                    gemm(at, p, wide, groups=[2])
                    pe.wait_ge(a_ready, head + 1)
                    nc.tensor.matmul(aux[:, 2, 0:S], v_head[:, 0, :], att[:, 0:S], start=True, stop=False)
                    nc.tensor.matmul(aux[:, 2, P:S], v_head[:, 1, :], att[:, S:S + P], start=False, stop=True
                                     ).then_inc(av_done, 1)
                    gemm(at, p, wide, groups=[3])
            at = At("mix2")
            for g in range(2):
                pe.wait_ge(lhs_ready, 8 * 5 + 2 * g + 2)
                gemm(at, 0, wide, 0, [g])
            for g in range(2):
                pe.wait_ge(lhs_ready, 8 * 5 + 2 * g + 6)
                gemm(at, 1, wide, 8, [g])
            with pe.Fori(1, 3) as i:
                gemm(At("mix2", i), 0, wide)
                gemm(At("mix2", i), 1, wide, 8)
            at = At("mix2", 3)
            for kq in range(4):
                gemm(at, kq // 2, wide, kq // 2 * 8, [kq % 2])
                if kq < 3:
                    pieces(4, 6, kq)
            at = At("out2")
            gemm_after(at, 6, wide, 0, 4)
            for p in range(1, 3):
                gemm(at, p, wide)
            last_panel(at, 3, 5, 7)

            at = At("ffn2_first")
            gemm_after(at, 7, wide, 0, 5)
            hid_turn(NB1)
            with pe.Fori(0, NB2 - 1) as i:
                at = At("ffn2", i)
                gemm(at, 0, wide, ps=third)
                pe.wait_ge(hid_lo_ready, i * 2 + (2 * NB1 + 2))
                for j in range(4):
                    gemm(at, 1 + j, low, ps=pairs[j % 2])
                hid_turn(i + (NB1 + 1))
            pe.wait_ge(hid_lo_ready, 2 * (NB1 + NB2))
            for j in range(4):
                gemm(At("ffn2_last"), j, low, ps=pairs[j % 2])


_INS = ["x", "positions", "attn_norm_g", "w_in", "b_gate", "q_a_norm_g", "w_q_b", "kv_a_norm_g",
        "w_kv_b", "q_norm_g", "k_norm_g", "w_attn_o", "w_pool_grp", "pool_scale", "w_pool_o", "w_out",
        "ffn_norm_g", "w_ffn_gate", "w_ffn_up", "w_ffn_down", "g_mix_2", "w_in_2", "g_q_2", "g_k_2",
        "sgu_ln_g_2", "sgu_ln_b_2", "w_spatial_2", "b_spatial_2", "w_oa_2", "w_ob_2", "w_out_2",
        "g_ff_2", "w_ff1_2", "w_ff2_2"]


def shape_constants():
    r = np.arange(P)
    con = np.zeros((P, C_END), np.float32)
    con[:, C_ID:C_ID + P] = np.eye(P)
    for b in (0, 2):
        con[:, C_CAUSAL + b * P:C_CAUSAL + (b + 1) * P] = np.where(r[None, :] <= r[:, None], 0.0, -3e38)
    con[:, C_AFTER:C_AFTER + P] = r[:, None] > r[None, :]
    con[:, C_ONES:C_ONES + P] = 1.0
    con[:, C_PAST:C_PAST + P] = r[:, None] < r[None, :]
    half = np.arange(HALF, dtype=np.float32)
    con[:, C_FREQ:C_FREQ + HALF] = (np.float32(10000.0) ** (-half / np.float32(HALF)))[None, :]
    mats = np.zeros((P, 4, 384), np.float32)
    src = np.arange(S)[:, None]
    dst = np.arange(S)[None, :]
    for g, w in enumerate(POOL_WINDOWS):
        lo = np.maximum(dst + 1 - w, 0)
        a = np.where((src >= lo) & (src <= dst), 1.0 / (dst + 1 - lo), 0.0) - (src == dst)
        mats[:, g, 0:S] = a[0:P, :]
        mats[:, g, S:S + P] = a[P:S, P:S]
    return con, mats


def kernel(**inputs):
    import concourse.bacc as bacc
    from concourse.bass_utils import run_bass_kernel_spmd

    nc = bacc.Bacc("TRN2", target_bir_lowering=False, num_devices=1)
    arrays, args = {}, []
    con, mats = shape_constants()
    named = [(n, np.ascontiguousarray(inputs[n])) for n in _INS] + [("consts", con), ("pool_mats", mats)]
    for name, a in named:
        arrays[f"in_{name}"] = a
        args.append(nc.dram_tensor(f"in_{name}", a.shape, mybir.dt.from_np(a.dtype), kind="ExternalInput").ap())
    args.append(nc.dram_tensor("out_x", (1, S, D), F32, kind="ExternalOutput").ap())
    two_blocks(nc, *args)
    r = run_bass_kernel_spmd(nc, [arrays], core_ids=[0])
    return r.results[0]["out_x"]
```

```python
import numpy as np

import concourse.bass as bass
from concourse import mybir

F32 = mybir.dt.float32
F32R = mybir.dt.float32r
I32 = mybir.dt.int32
ALU = mybir.AluOpType
ACT = mybir.ActivationFunctionType
AX = mybir.AxisListType

P = 128
TOK = 2
S = TOK * P
D = 2048
KC = D // P
N = 512
EPS = 1e-6

Q_RANK, KV_RANK, ROPE, POOL = 512, 512, 64, 1024
NOPE, VDIM, HEADS = 128, 128, 16
QK = NOPE + ROPE
HALF = ROPE // 2
POOL_WINDOWS = (2, 4, 8, 16)
D_FF = 5632
COL_KV = Q_RANK
COL_KR = COL_KV + KV_RANK
COL_POOL = COL_KR + ROPE
COL_GATE = COL_POOL + POOL
PAIRS = HEADS // 2
SM_SCALE = QK ** -0.5

SB = 1024
SB_HEADS = 8
SGU = 1024
GROUPS = 8
CHUNK = 64
D_FF2 = 8192
COL_U = 3 * SB
COL_VS = COL_U + SGU
COL_GATE2 = COL_VS + SGU
SB_SCALE = 128 ** -0.5

RAW = 4
SPLIT = 4
LEAD = 4
LO_CREDIT = 2 * RAW
EVAC_CREDIT = 2

NB1 = D_FF // N
NB2 = D_FF2 // N

C_ID, C_CAUSAL, C_AFTER, C_ONES, C_PAST, C_FREQ = 0, 128, 512, 640, 768, 896
C_END = 928
TWO_PI = 2 * np.pi
PI_1 = 6.28125
PI_2 = float(np.float32(np.round((TWO_PI - PI_1) * 2 ** 21) / 2 ** 21))
PI_3 = float(TWO_PI - PI_1 - PI_2)
MAGIC = 1.5 * 2 ** 23
PI_MAX = 3.1415925


FULL = (KC, N)
SHORT = (4, N)
SUB = [FULL, (4, 2 * QK), SHORT]
PLAN = [
    ("in", 1, [FULL, FULL, (KC, ROPE), FULL, FULL]),
    ("pool", 2, [(8, N), (8, N)]),
    ("heads_first", 1, SUB),
    ("heads", (PAIRS - 2) // 2, SUB + SUB),
    ("heads_last", 1, SUB),
    ("attn_o", 1, [(KC - 4, N)] * 2 + [SHORT] * 2 + [FULL] * 2),
    ("out", 1, [FULL] * 4),
    ("ffn_first", 1, [FULL, FULL]),
    ("ffn", NB1 - 2, [FULL, FULL] + [SHORT] * 4),
    ("ffn_last", 1, [FULL, FULL] + [SHORT] * 8),
    ("in2", 1, [FULL] * 10),
    ("gates2", SB_HEADS // 2 - 1, [FULL] * 2),
    ("gates2_last", 1, [FULL] * 2),
    ("mix2", 4, [(8, N), (8, N)]),
    ("out2", 1, [FULL] * 4),
    ("ffn2_first", 1, [FULL]),
    ("ffn2", NB2 - 2, [FULL] + [SHORT] * 4),
    ("ffn2_last", 1, [FULL] + [SHORT] * 8),
]


class At:

    def __init__(self, name, i=0):
        gran = panel = 0
        for stage, turns, panels in PLAN:
            sizes = [k // 2 for k, _ in panels]
            if stage == name:
                break
            gran += turns * sum(sizes)
            panel += turns * len(panels)
        self.i, self.panels = i, panels
        self.gran0, self.panel0 = gran, panel
        self.starts = [sum(sizes[:p]) for p in range(len(sizes) + 1)]
        self.per = self.starts[-1]
        assert turns == 1 or self.per % (2 * RAW) == 0

    def gran(self, p, k=0):
        return self.i * self.per + (self.gran0 + self.starts[p] + k)

    def slot(self, p, k=0):
        return (self.gran0 + self.starts[p] + k) % SPLIT

    def raw_slot(self, p, k=0):
        return (self.gran0 + self.starts[p] + k) // 2 % RAW

    def loads(self, p, k=0):
        return self.i * (16 * self.per // (2 * RAW)) + 16 * ((self.gran0 + self.starts[p] + k) // (2 * RAW) + 1)

    def end(self, p):
        return self.gran(p, self.panels[p][0] // 2)

    def panel(self, p):
        return self.i * len(self.panels) + (self.panel0 + p)

    def pair(self, p):
        return (self.panel0 + p) % 2


def two_blocks(nc, x, positions, attn_norm_g, w_in, b_gate, q_a_norm_g, w_q_b, kv_a_norm_g, w_kv_b,
               q_norm_g, k_norm_g, w_attn_o, w_pool_grp, pool_scale, w_pool_o, w_out, ffn_norm_g,
               w_ffn_gate, w_ffn_up, w_ffn_down, g_mix_2, w_in_2, g_q_2, g_k_2, sgu_ln_g_2,
               sgu_ln_b_2, w_spatial_2, b_spatial_2, w_oa_2, w_ob_2, w_out_2, g_ff_2, w_ff1_2,
               w_ff2_2, consts, pool_mats, out):
    at_byte = [(nc.sbuf_base + 31) // 32 * 32]

    def place(name, shape, dtype=F32, offset=None):
        size = 4 * int(np.prod(shape[1:]))
        if offset is None:
            offset = at_byte[0]
            at_byte[0] += (size + 31) // 32 * 32
        return nc.alloc_sbuf_tensor_at(name, shape, dtype, offset=offset)

    xres = place("xres", [P, TOK, D])
    lhs_hi = place("lhs_hi", [P, KC, S], F32R)
    lhs_lo = place("lhs_lo", [P, KC, S], F32R)
    raw = place("raw", [P, RAW, 4, N])
    w_hi = place("w_hi", [P, SPLIT, 2, N], F32R)
    w_lo = place("w_lo", [P, SPLIT, 2, N], F32R)
    mix = place("mix", [P, TOK, 2 * D])
    act_t = place("act_t", [P, KC, S])
    low_at = at_byte[0]
    low_hi = place("low_hi", [P, 8, S], F32R)
    low_lo = place("low_lo", [P, 8, S], F32R)
    qk_t = place("qk_t", [P, 16, S], offset=low_at)
    con = place("con", [P, C_END])
    cols = place("cols", [P, 16])
    small = place("small", [P, 96])
    cosd = place("cosd", [P, TOK, ROPE])
    sind = place("sind", [P, TOK, ROPE])
    krr = place("krr", [P, TOK, ROPE])
    pos_i = place("pos_i", [P, TOK], I32)
    arena = place("arena", [P, 6144])
    assert at_byte[0] <= nc.sbuf_base + nc.sbuf_bytes_remaining, at_byte[0]

    def part(start, *shape):
        size = int(np.prod(shape))
        ap = arena[:, start:start + size]
        if len(shape) == 2:
            return ap.rearrange("p (a b) -> p a b", a=shape[0])
        if len(shape) == 3:
            return ap.rearrange("p (a b c) -> p a b c", a=shape[0], b=shape[1])
        return ap

    gain = part(0, D)
    pool_a = part(2048, 4, 384)
    gain_cq = part(3584, N)
    gain_ckv = part(4096, N)
    junk = part(4608, N)
    q_rows = part(0, TOK, 2, QK)
    k_rows = part(768, TOK, 2, QK)
    v_rows = part(1536, TOK, 2, VDIM)
    q_tn = part(2048, 2, S)
    k_tn = part(2560, 2, S)
    p_t = part(2048, 2, 384)
    q_tr = part(3072, 2, S)
    k_tr = part(3584, 2, S)
    gate_tmp = part(3072, TOK, N)
    probs = part(4096, 2, 384)
    squares = part(4096, TOK, 2, QK)
    rope_a = part(4096, TOK, 2, ROPE)
    rope_b = part(4352, TOK, 2, ROPE)
    gain_q = part(5120, QK)
    gain_k = part(5312, QK)
    bias = part(5504, N)
    act_f = part(2048, TOK, N)
    hid = part(3072, TOK, N)
    vs = part(0, TOK, SGU)
    us = part(2048, TOK, SGU)
    vb = part(4096, TOK, SB)
    z_neg = part(0, 384)
    z_pos = part(384, 384)
    z_abs = part(768, 384)
    att = part(1152, 384)
    k_head = part(1536, S)
    v_head = part(1792, TOK, P)
    gain_qk = mix[:, 0, D:2 * D]
    qk_rows = mix[:, 1, D:D + 1024].rearrange("p (a b) -> p a b", a=TOK)
    qk_sq = mix[:, 1, D + 1024:2 * D].rearrange("p (a b) -> p a b", a=TOK)
    ln_g, ln_b = mix[:, 0, 0:SGU], mix[:, 0, SGU:2 * SGU]
    ws_raw = mix[:, 1, 0:1024].rearrange("p (g j) -> p g j", g=GROUPS)
    ws_t = mix[:, 1, 1024:2048].rearrange("p (g i) -> p g i", g=GROUPS)
    w_grp = act_t[:, 8:16, :].rearrange("p (g c) d -> p g c d", g=4)
    cq_rows = mix[:, :, D:D + N]
    ckv_rows = mix[:, :, D + N:D + 2 * N]
    u_rows = mix[:, :, D + 2 * N:2 * D]

    ident = con[:, C_ID:C_ID + P]
    causal = con[:, C_CAUSAL:C_CAUSAL + 384]
    after = con[:, C_AFTER:C_AFTER + P]
    ones = con[:, C_ONES:C_ONES + P]
    past = con[:, C_PAST:C_PAST + P]
    freq = con[:, C_FREQ:C_FREQ + HALF]
    ss, inv = small[:, 0:8], small[:, 8:16]
    x_inv = small[:, 72:74]
    x_ss = small[:, 74:82].rearrange("p (t b) -> p t b", t=TOK)
    inv_x = small[:, 82:90]
    kr_ss, cq_ss, cq_inv = small[:, 16:18], small[:, 18:20], small[:, 20:22]
    row_max, row_sum, row_inv = small[:, 24:28], small[:, 28:32], small[:, 32:36]
    pos_f = small[:, 36:38]
    ln_mv, ln_inv = small[:, 40:44], small[:, 44:46]
    ln_stats = small[:, 48:72]

    pairs = [nc.alloc_psum_tensor(f"pair{i}", [P, TOK, N], F32) for i in range(2)]
    aux = nc.alloc_psum_tensor("aux", [P, 4, N], F32)
    third = aux[:, 2:4, :]

    sem = nc.alloc_semaphore
    raw_loaded = [sem(f"raw_loaded{r}") for r in range(RAW)]
    hi_ready = sem("hi_ready")
    lo_ready = sem("lo_ready")
    gran_used = sem("gran_used")
    evac_done = sem("evac_done")
    ident_loaded = sem("ident_loaded")
    x_loaded = [sem(f"x_loaded{b}") for b in range(4)]
    x_inv_ready = sem("x_inv_ready")
    loaded = {n: sem("loaded_" + n) for n in (
        "con", "pos", "cols", "cq", "pool", "qk", "bias", "gain", "qk2", "ln")}
    side_go = sem("side_go")
    bias_used = sem("bias_used")
    sumsq = sem("sumsq")
    ms_ready = sem("ms_ready")
    rms_ready = sem("rms_ready")
    rows_ready = sem("rows_ready")
    turned = sem("turned")
    lhs_hi_ready = sem("lhs_hi_ready")
    lhs_ready = sem("lhs_ready")
    angles = sem("angles")
    sines = sem("sines")
    pool_mm = sem("pool_mm")
    pool_out = sem("pool_out")
    low_rows = sem("low_rows")
    low_turned = sem("low_turned")
    low_hi_ready = sem("low_hi_ready")
    low_ready = sem("low_ready")
    mix_ones = sem("mix_ones")
    kr_sq = sem("kr_sq")
    gate_in = sem("gate_in")
    gate_out = sem("gate_out")
    q_sq = sem("q_sq")
    kv_sq = sem("kv_sq")
    qk_done = sem("qk_done")
    qk_turned = sem("qk_turned")
    qk_copied = sem("qk_copied")
    scored = sem("scored")
    max_ready = sem("max_ready")
    exp_done = sem("exp_done")
    p_ready = sem("p_ready")
    p_turned = sem("p_turned")
    p_copied = sem("p_copied")
    av_done = sem("av_done")
    av_stored = sem("av_stored")
    act_ready = sem("act_ready")
    hid_ready = sem("hid_ready")
    hid_turned = sem("hid_turned")
    hid_hi_ready = sem("hid_hi_ready")
    hid_lo_ready = sem("hid_lo_ready")
    qk2_sq = sem("qk2_sq")
    qk2_ready = sem("qk2_ready")
    qk2_turned = sem("qk2_turned")
    qk2_copied = sem("qk2_copied")
    gelu_done = sem("gelu_done")
    ln_done = sem("ln_done")
    ws_turned = sem("ws_turned")
    ws_ready = sem("ws_ready")
    sgu_mm = sem("sgu_mm")
    sgu_rows = sem("sgu_rows")
    sgu_turned = sem("sgu_turned")
    keys_copied = sem("keys_copied")
    values_copied = sem("values_copied")
    z_done = sem("z_done")
    z_split = sem("z_split")
    z_log = sem("z_log")
    keep_ready = sem("keep_ready")
    tail_done = sem("tail_done")
    log_a = sem("log_a")
    a_exp = sem("a_exp")
    a_ready = sem("a_ready")
    out_done = sem("out_done")

    def token_rows(ap):
        return ap.rearrange("(t p) n -> p t n", p=P)

    block = nc.Block()
    with block:
        @block.sync
        def _(sp):
            def load(at, p, w, col, row0=0, groups=None):
                kch, n = at.panels[p]
                for g in range(kch // 4) if groups is None else groups:
                    k = 2 * g
                    sp.wait_ge(lo_ready, at.gran(p, k) + 2)
                    rows = w[bass.ds(row0 + g * 4 * P, 4 * P), bass.ds(col, n)]
                    sp.dma_start(raw[:, at.raw_slot(p, k), :, 0:n],
                                 rows.rearrange("(c p) n -> p c n", p=P)
                                 ).then_inc(raw_loaded[at.raw_slot(p, k)], 16)

            w1, w2 = w_in[0], w_in_2[0]
            at = At("in")
            sp.dma_start(ident, consts[:, C_ID:C_ID + P]).then_inc(ident_loaded, 16)
            for b in range(4):
                blk = slice(b * N, (b + 1) * N)
                sp.dma_start(xres[:, :, blk], token_rows(x[0])[:, :, blk]).then_inc(x_loaded[b], 16)
                sp.dma_start(gain[:, blk], attn_norm_g[0, blk].partition_broadcast(P)).then_inc(x_loaded[b], 16)
                load(at, 0, w1, COL_POOL, groups=[b])
            for p, col in enumerate((COL_POOL + N, COL_KR, 0, COL_KV)):
                load(at, p + 1, w1, col)
            with sp.Fori(0, 2) as i:
                for p in range(2):
                    load(At("pool", i), p, w_pool_o[0], i * (2 * N) + p * N)

            def sub(at, p, u):
                load(at, p, w1, u * N + COL_GATE)
                load(at, p + 1, w_q_b[0], u * (2 * QK))
                load(at, p + 2, w_kv_b[0], (u * P) * 4)

            sub(At("heads_first"), 0, 0)
            with sp.Fori(0, (PAIRS - 2) // 2) as i:
                for s in range(2):
                    sub(At("heads", i), 3 * s, i * 2 + (1 + s))
            sub(At("heads_last"), 0, PAIRS - 1)
            at = At("attn_o")
            for p in range(2):
                load(at, p, w_attn_o[0], p * N)
            for p in range(2):
                load(at, 2 + p, w_attn_o[0], p * N, (KC - 4) * P)
            for p in range(2, 4):
                load(at, 2 + p, w_attn_o[0], p * N)
            for p in range(4):
                load(At("out"), p, w_out[0], p * N)
            at = At("ffn_first")
            load(at, 0, w_ffn_gate[0], 0)
            load(at, 1, w_ffn_up[0], 0)

            def ffn_block(at, i):
                load(at, 0, w_ffn_gate[0], i * N + N)
                load(at, 1, w_ffn_up[0], i * N + N)
                for j in range(4):
                    load(at, 2 + j, w_ffn_down[0], j * N, i * N)

            with sp.Fori(0, NB1 - 2) as i:
                ffn_block(At("ffn", i), i)
            ffn_block(At("ffn_last"), NB1 - 2)
            for j in range(4):
                load(At("ffn_last"), 6 + j, w_ffn_down[0], j * N, (NB1 - 1) * N)

            starts = (0, SB, COL_VS, COL_U, 2 * SB)
            for p in range(10):
                load(At("in2"), p, w2, starts[p // 2] + p % 2 * N)
            with sp.Fori(0, 2) as i:
                for p in range(2):
                    load(At("gates2", i), p, w2, i * (2 * N) + (COL_GATE2 + D + p * N))
            for p in range(2):
                load(At("gates2", 2), p, w2, COL_GATE2 + p * N)
            for p in range(2):
                load(At("gates2_last"), p, w2, COL_GATE2 + (2 + p) * N)
            with sp.Fori(0, 4) as i:
                load(At("mix2", i), 0, w_ob_2[0], i * N)
                load(At("mix2", i), 1, w_oa_2[0], i * N)
            for p in range(4):
                load(At("out2"), p, w_out_2[0], p * N)
            load(At("ffn2_first"), 0, w_ff1_2[0], 0)

            def ffn2_block(at, i):
                load(at, 0, w_ff1_2[0], i * N + N)
                for j in range(4):
                    load(at, 1 + j, w_ff2_2[0], j * N, i * N)

            with sp.Fori(0, NB2 - 2) as i:
                ffn2_block(At("ffn2", i), i)
            ffn2_block(At("ffn2_last"), NB2 - 2)
            for j in range(4):
                load(At("ffn2_last"), 5 + j, w_ff2_2[0], j * N, (NB2 - 1) * N)
            last = At("ffn2_last")
            for j in range(4):
                sp.wait_ge(evac_done, last.panel(5 + j) + 1 + EVAC_CREDIT)
                sp.dma_start(token_rows(out[0])[:, :, j * N:(j + 1) * N],
                             xres[:, :, j * N:(j + 1) * N]).then_inc(out_done, 16)
            sp.wait_ge(out_done, 4 * 16)

        @block.gpsimd
        def _(pool):
            def to_all(dst, row, what):
                pool.dma_start(dst, row.partition_broadcast(P)).then_inc(loaded[what], 16)

            pool.dma_start(con[:, P:C_END], consts[:, P:C_END]).then_inc(loaded["con"], 16)
            with nc.allow_non_contiguous_dma("a few columns"):
                pool.dma_start(pos_i[:], positions[0].rearrange("(t p) -> p t", p=P)).then_inc(loaded["pos"], 16)
                pool.dma_start(cols[:, 0:8], pool_scale[0].rearrange("g (c p) -> p (g c)", p=P)
                               ).then_inc(loaded["cols"], 16)
                pool.dma_start(cols[:, 8:16], b_spatial_2[0].rearrange("g p -> p g")).then_inc(loaded["cols"], 16)
            to_all(gain_k, k_norm_g[0], "qk")
            to_all(gain_q, q_norm_g[0], "qk")
            to_all(gain_cq, q_a_norm_g[0], "cq")
            to_all(gain_ckv, kv_a_norm_g[0], "cq")
            pool.dma_start(pool_a, pool_mats).then_inc(loaded["pool"], 16)
            pool.dma_start(w_grp, w_pool_grp[0].rearrange("g (c p) d -> p g c d", p=P)
                           ).then_inc(loaded["pool"], 16)
            pool.wait_ge(low_turned, 4)
            nc.gpsimd.memset(mix[:, :, D:2 * D], 1.0).then_inc(mix_ones, 1)
            to_all(bias, b_gate[0, 0:N], "bias")
            with pool.Fori(1, PAIRS) as u:
                pool.wait_ge(bias_used, u)
                to_all(bias, b_gate[0, bass.ds(u * N, N)], "bias")
            pool.wait_ge(side_go, 1)
            to_all(gain, ffn_norm_g[0], "gain")
            pool.wait_ge(side_go, 2)
            to_all(gain, g_mix_2[0], "gain")
            to_all(gain_qk[:, 0:SB], g_q_2[0].rearrange("h d -> (h d)"), "qk2")
            to_all(gain_qk[:, SB:2 * SB], g_k_2[0].rearrange("h d -> (h d)"), "qk2")
            pool.wait_ge(side_go, 3)
            to_all(ln_g, sgu_ln_g_2[0], "ln")
            to_all(ln_b, sgu_ln_b_2[0], "ln")
            pool.dma_start(ws_raw, w_spatial_2[0].rearrange("g i j -> i g j")).then_inc(loaded["ln"], 16)
            pool.wait_ge(side_go, 4)
            to_all(gain, g_ff_2[0], "gain")

        @block.scalar
        def _(act):
            def hi(at, p, k0, k1, after_panel=None):
                for k in range(k0, k1):
                    width = at.panels[p][1] if after_panel is None else after_panel
                    act.wait_ge(raw_loaded[at.raw_slot(p, k)], at.loads(p, k))
                    act.wait_ge(gran_used, at.gran(p, k) + 1)
                    h = (at.gran0 + at.starts[p] + k) % 2
                    nc.scalar.activation(w_hi[:, at.slot(p, k), :, 0:width],
                                         raw[:, at.raw_slot(p, k), 2 * h:2 * h + 2, 0:width],
                                         ACT.Copy).then_inc(hi_ready, 1)

            def panel_done(at, p):
                act.wait_ge(gran_used, at.end(p) + SPLIT)

            def root(n_before, dst, src):
                act.wait_ge(ms_ready, n_before + 1)
                nc.scalar.activation(dst, src, ACT.Sqrt).then_inc(rms_ready, 1)

            def squares_of(b, at=None, p=None):
                if at is not None:
                    act.wait_ge(evac_done, at.panel(p) + 1 + EVAC_CREDIT)
                for t in range(TOK):
                    nc.scalar.activation(mix[:, 1, 2 * D - N:2 * D], xres[:, t, b * N:(b + 1) * N],
                                         ACT.Square, accum_out=x_ss[:, t, b:b + 1])
                    act.drain()
                if b == 3:
                    act.sem_inc(sumsq, 1)

            def x_norm(n_roots):
                root(n_roots, x_inv, x_inv)

            def piece(r, p, free=None):
                act.wait_ge(turned, 8 * r + p + 1)
                if free is not None:
                    act.wait_ge(gran_used, free)
                kq, t = p // 2, p % 2
                nc.scalar.activation(lhs_hi[:, 4 * kq:4 * kq + 4, t * P:(t + 1) * P],
                                     aux[:, p % 4, :].rearrange("p (c t) -> p c t", c=4),
                                     ACT.Copy).then_inc(lhs_hi_ready, 1)

            def pieces(r, kq, free=None):
                piece(r, 2 * kq, free)
                piece(r, 2 * kq + 1, free)

            def refill(kq):
                nc.scalar.activation(lhs_hi[:, 4 * kq:4 * kq + 4, :], act_t[:, 4 * kq:4 * kq + 4, :],
                                     ACT.Copy).then_inc(lhs_hi_ready, 1)

            def bridge(r, at, p, nxt, between=None):
                for kq in range(3):
                    hi(at, p, 4 + 2 * kq, 6 + 2 * kq)
                    pieces(r, kq, at.gran(p, 2 * kq + 2) + SPLIT)
                hi(at, p, 10, 12)
                if between is not None:
                    between()
                hi(nxt, 0, 4, 6)
                pieces(r, 3, at.gran(p, 8) + SPLIT)
                hi(nxt, 0, 6, 8)

            act.sem_inc(gran_used, SPLIT)
            at = At("in")
            for b in range(4):
                pieces(0, b)
                hi(at, 0, 2 * b, 2 * b + 2)
                if b:
                    squares_of(b - 1)
            squares_of(3)
            hi(at, 1, 0, 2)
            x_norm(0)
            hi(at, 1, 2, 8)
            act.wait_ge(angles, 1)
            nc.scalar.activation(cosd[:, :, 0:HALF], cosd[:, :, HALF:ROPE], ACT.Sin)
            nc.scalar.activation(sind[:, :, HALF:ROPE], sind[:, :, 0:HALF], ACT.Sin)
            act.drain().then_inc(sines, 1)
            act.wait_ge(x_inv_ready, 1)

            def low_squares(p):
                panel_done(at, p)
                for t in range(TOK):
                    nc.scalar.activation(junk, pairs[at.pair(p)][:, t, :], ACT.Square,
                                         scale=x_inv[:, t:t + 1], accum_out=cq_ss[:, t:t + 1])
                    act.drain()
                act.sem_inc(sumsq, 1)

            for p in range(2, 5):
                hi(at, p, 0, 4)
                if p == 4:
                    low_squares(3)
                    root(1, cq_inv, cq_inv)
                if p == 3:
                    panel_done(at, 2)
                    for t in range(TOK):
                        nc.scalar.activation(junk[:, 0:ROPE], pairs[at.pair(2)][:, t, 0:ROPE], ACT.Square,
                                             scale=x_inv[:, t:t + 1], accum_out=kr_ss[:, t:t + 1])
                        act.drain()
                    act.sem_inc(kr_sq, 1)
                hi(at, p, 4, 8)
                if p == 4:
                    for b in range(4):
                        act.wait_ge(pool_mm, b + 1)
                        nc.scalar.activation(act_t[:, 2 * b:2 * b + 2, :],
                                             aux[:, b, :].rearrange("p (c t) -> p c t", c=2), ACT.Copy)
                    act.drain().then_inc(pool_out, 1)
            nxt = At("pool")
            hi(nxt, 0, 0, 4)
            for j in range(8):
                act.wait_ge(pool_mm, 4 + j // 2 + 1)
                act.wait_ge(loaded["cols"], 32)
                nc.scalar.activation(low_hi[:, j, :], aux[:, j // 2, (j % 2) * S:(j % 2 + 1) * S], ACT.Copy,
                                     scale=cols[:, j:j + 1]).then_inc(low_hi_ready, 1)
            low_squares(4)
            root(2, cq_inv, cq_inv)
            with act.Fori(0, 2) as i:
                at = At("pool", i)
                for p in range(2):
                    hi(at, p, 4, 8)

            def turned_low():
                for q in range(4):
                    act.wait_ge(low_turned, q + 1)
                    c0, t = 4 * (q // 2), q % 2
                    nc.scalar.activation(low_hi[:, c0:c0 + 4, t * P:(t + 1) * P],
                                         aux[:, q, :].rearrange("p (c t) -> p c t", c=4),
                                         ACT.Copy).then_inc(low_hi_ready, 1)

            def attend_a(u):
                root(u + 2, inv, inv)

            def attend_b(u):
                act.wait_ge(qk_turned, u)
                nc.scalar.activation(q_tn, aux[:, 0, :].rearrange("p (h t) -> p h t", h=2), ACT.Copy)
                nc.scalar.activation(k_tn, aux[:, 1, :].rearrange("p (h t) -> p h t", h=2), ACT.Copy)
                nc.scalar.activation(q_tr[0:ROPE], aux[0:ROPE, 2, :].rearrange("p (h t) -> p h t", h=2),
                                     ACT.Copy)
                nc.scalar.activation(k_tr[0:ROPE], aux[0:ROPE, 3, :].rearrange("p (h t) -> p h t", h=2),
                                     ACT.Copy)
                act.drain().then_inc(qk_copied, 1)

            def attend_c(u):
                act.wait_ge(max_ready, u)
                for h in range(2):
                    for t in range(TOK):
                        c = slice(0, P) if t == 0 else slice(P, 3 * P)
                        nc.scalar.activation(probs[:, h, c], probs[:, h, c], ACT.Exp,
                                             bias=row_max[:, 2 * t + h:2 * t + h + 1],
                                             accum_out=row_sum[:, 2 * t + h:2 * t + h + 1])
                act.drain().then_inc(exp_done, 1)

            def attend_d(u):
                act.wait_ge(p_turned, u)
                nc.scalar.activation(p_t, aux[:, 2:4, 0:384], ACT.Copy).then_inc(p_copied, 1)

            def attend_e(u):
                act.wait_ge(av_done, u)
                nc.scalar.activation(act_t[:, bass.ds(u * 2 - 2, 2), :],
                                     aux[:, 0, :].rearrange("p (h t) -> p h t", h=2), ACT.Copy
                                     ).then_inc(av_stored, 1)

            def rows_q(at, p, u):
                panel_done(at, p)
                nc.scalar.activation(squares, pairs[at.pair(p)][:, :, 0:2 * QK].rearrange(
                    "p t (h d) -> p t h d", h=2), ACT.Square).then_inc(q_sq, 1)

            def rows_kv(at, p, u):
                panel_done(at, p)
                kv = pairs[at.pair(p)][:].rearrange("p t (h d) -> p t h d", h=2)
                act.wait_ge(q_sq, u * 2 + 2)
                nc.scalar.activation(squares[:, :, :, 0:NOPE], kv[:, :, :, 0:NOPE], ACT.Square)
                nc.scalar.activation(v_rows, kv[:, :, :, NOPE:NOPE + VDIM], ACT.Copy)
                act.drain().then_inc(kv_sq, 1)

            def sub(at, p, u, has_last, last=False):
                if has_last:
                    attend_a(u)
                hi(at, p, 4, 6)
                hi(at, p, 6, 8)
                if has_last:
                    attend_b(u)
                else:
                    turned_low()
                hi(at, p + 1, 0, 2)
                if has_last:
                    attend_c(u)
                hi(at, p + 2, 0, 2)
                if has_last:
                    attend_d(u)
                act.wait_ge(gate_in, u + 1)
                nc.scalar.activation(gate_tmp, gate_tmp, ACT.Sigmoid).then_inc(gate_out, 1)
                rows_q(at, p + 1, u)
                if has_last:
                    attend_e(u)
                hi(at, p + 2, 2, 4, N)
                if last:
                    act.drain()
                    refill(0)
                rows_kv(at, p + 2, u)
                hi(at, p + 2, 4, 6, N)
                if last:
                    refill(1)
                    refill(2)

            sub(At("heads_first"), 0, 0, False)
            with act.Fori(0, (PAIRS - 2) // 2) as i:
                for s in range(2):
                    sub(At("heads", i), 3 * s, i * 2 + (1 + s), True)
            sub(At("heads_last"), 0, PAIRS - 1, True, True)

            at = At("attn_o")
            attend_a(PAIRS)
            hi(at, 0, 4, 8)
            attend_b(PAIRS)
            hi(at, 0, 8, 10)
            attend_c(PAIRS)
            hi(at, 0, 10, 12)
            attend_d(PAIRS)
            hi(at, 0, 12, 14)
            attend_e(PAIRS)
            act.drain()
            refill(3)
            hi(at, 0, 14, 24)
            hi(at, 0, 24, 28)
            bridge(1, at, 5, At("out"))
            at, nxt = At("out"), At("ffn_first")
            for p in range(3):
                if p:
                    hi(at, p, 4, 8)
                    squares_of(p - 1, at, p - 1)
                hi(at, p, 8, 12)
            bridge(2, at, 3, nxt, lambda: squares_of(2, at, 2))
            squares_of(3, at, 3)

            def hid_turn(b, c0=0):
                for t in range(TOK):
                    act.wait_ge(hid_turned, b * 2 + t + 1)
                    nc.scalar.activation(low_hi[:, c0:c0 + 4, t * P:(t + 1) * P],
                                         aux[:, t, :].rearrange("p (c t) -> p c t", c=4),
                                         ACT.Copy).then_inc(hid_hi_ready, 1)

            def gate_function(at, p, b, func, src):
                panel_done(at, p)
                act.wait_ge(hid_ready, b + 1)
                for t in range(TOK):
                    nc.scalar.activation(act_f[:, t, :], src[:, t, :], func, scale=x_inv[:, t:t + 1])
                act.drain().then_inc(act_ready, 1)

            act.sem_inc(hid_ready, 1)
            at = At("ffn_first")
            hi(at, 1, 0, 4)
            x_norm(11)
            act.wait_ge(x_inv_ready, 2)
            gate_function(at, 0, 0, ACT.Sigmoid, pairs[at.pair(0)][:])
            hi(at, 1, 4, 8)
            hi(at, 1, 8, 12)

            def block(at, i, last=False):
                hi(at, 0, 4, 8)
                hid_turn(i)
                hi(at, 1, 0, 4)
                gate_function(at, 0, i + 1, ACT.Sigmoid, pairs[at.pair(0)][:])
                hi(at, 1, 4, 8)
                for j in range(4):
                    hi(at, 2 + j, 0, 2)
                    if last and j == 2:
                        hid_turn(NB1 - 1, 4)
                hi(at, 5, 2, 6)

            with act.Fori(0, NB1 - 2) as i:
                block(At("ffn", i), i)
            at, nxt = At("ffn_last"), At("in2")
            block(at, NB1 - 2, True)
            hi(at, 6, 4, 8)
            squares_of(0, at, 6)
            pieces(3, 0)
            hi(at, 6, 8, 10)
            squares_of(1, at, 7)
            pieces(3, 1)
            hi(at, 6, 10, 12)
            squares_of(2, at, 8)
            pieces(3, 2)
            hi(nxt, 0, 4, 6)
            squares_of(3, at, 9)
            pieces(3, 3)
            hi(nxt, 0, 6, 8)

            at = At("in2")

            def values2(at, p):
                panel_done(at, p)
                for t in range(TOK):
                    nc.scalar.activation(vb[:, t, (p - 8) * N:(p - 7) * N], pairs[at.pair(p)][:, t, :],
                                         ACT.Copy, scale=x_inv[:, t:t + 1])
                act.drain().then_inc(gelu_done, 1)

            def next_key(head):
                nc.scalar.activation(k_head, qk_t[:, bass.ds(head + 8, 1), :].rearrange("p a t -> p (a t)"),
                                     ACT.Copy)
                act.drain().then_inc(keys_copied, 1)

            x_norm(12)
            hi(at, 0, 8, 12)
            act.wait_ge(x_inv_ready, 3)
            for p in range(1, 10):
                panel_done(at, p - 1)
                src = pairs[at.pair(p - 1)]
                if p <= 4:
                    act.wait_ge(qk2_sq, 2 * p - 1)
                    for t in range(TOK):
                        nc.scalar.activation(qk_sq[:, t, :], src[:, t, :], ACT.Square,
                                             scale=x_inv[:, t:t + 1])
                    act.drain().then_inc(qk2_sq, 1)
                    hi(at, p, 4, 5)
                    root(12 + p, inv, inv)
                    hi(at, p, 5, 10)
                    for t in range(TOK):
                        act.wait_ge(qk2_turned, 2 * p + t - 1)
                        nc.scalar.activation(qk_t[:, 4 * p - 4:4 * p, t * P:(t + 1) * P],
                                             aux[:, t, :].rearrange("p (c t) -> p c t", c=4),
                                             ACT.Copy).then_inc(qk2_copied, 1)
                    hi(at, p, 10, 12)
                elif p <= 8:
                    dst = vs if p <= 6 else us
                    for t in range(TOK):
                        nc.scalar.activation(dst[:, t, (p - 1) % 2 * N:((p - 1) % 2 + 1) * N], src[:, t, :],
                                             ACT.Gelu, scale=x_inv[:, t:t + 1])
                    act.drain().then_inc(gelu_done, 1)
                    if p == 6:
                        act.wait_ge(ws_turned, 1)
                        for b in range(2):
                            nc.scalar.activation(ws_t[:, 4 * b:4 * b + 4, :],
                                                 aux[:, b, :].rearrange("p (g i) -> p g i", g=4), ACT.Copy)
                        act.drain().then_inc(ws_ready, 1)
                        root(17, ln_inv, ln_inv)
                    hi(at, p, 4, 12)
                else:
                    values2(at, 8)
                    hi(at, 9, 4, 6)
                    for b in range(4):
                        act.wait_ge(sgu_turned, b + 1)
                        nc.scalar.activation(act_t[:, 2 * b:2 * b + 2, :],
                                             aux[:, b, :].rearrange("p (c t) -> p c t", c=2), ACT.Copy)
                    next_key(0)
                    hi(at, 9, 6, 12)
            values2(at, 9)

            def head2(at, p, head, last=False):
                act.wait_ge(z_done, head + 1)
                nc.scalar.activation(z_abs, aux[:, 0, 0:384], ACT.Abs, scale=SB_SCALE)
                act.drain().then_inc(z_split, 1)
                nc.scalar.activation(z_abs, z_abs, ACT.Exp, scale=-1.0)
                act.drain()
                nc.scalar.activation(z_abs, z_abs, ACT.Ln, bias=1.0).then_inc(z_log, 1)
                nc.scalar.activation(v_head, vb[:, :, bass.ds(head * P, P)], ACT.Copy)
                act.drain().then_inc(values_copied, 1)
                hi(at, p, 4, 6)
                if not last:
                    next_key(head + 1)
                hi(at, p, 6, 8)
                act.wait_ge(log_a, head + 1)
                nc.scalar.activation(att, z_neg, ACT.Exp).then_inc(a_exp, 1)
                if last:
                    for kq in range(3):
                        act.wait_ge(gran_used, at.gran(p, 2 * kq + 2) + SPLIT)
                        refill(kq)
                        if kq:
                            hi(at, p, 6 + 2 * kq, 8 + 2 * kq)
                else:
                    hi(at, p, 8, 12)
                panel_done(at, p)
                for t in range(TOK):
                    nc.scalar.activation(mix[:, t, bass.ds(head * N, N)], pairs[at.pair(p)][:, t, :],
                                         ACT.Sigmoid, scale=x_inv[:, t:t + 1])
                act.drain().then_inc(gate_out, 1)
                act.wait_ge(av_done, head + PAIRS + 1)
                nc.scalar.activation(act_t[:, bass.ds(head + 8, 1), :].rearrange("p a t -> p (a t)"),
                                     aux[:, 2, 0:S], ACT.Copy)
                act.drain().then_inc(av_stored, 1)

            with act.Fori(0, SB_HEADS // 2 - 1) as i:
                for p in range(2):
                    head2(At("gates2", i), p, i * 2 + p)
            for p in range(2):
                head2(At("gates2_last"), p, SB_HEADS - 2 + p, p == 1)
            refill(3)
            hi(At("mix2"), 0, 4, 12)
            with act.Fori(1, 3) as i:
                hi(At("mix2", i), 0, 4, 12)
            bridge(4, At("mix2", 3), 0, At("out2"))
            at, nxt = At("out2"), At("ffn2_first")
            for p in range(3):
                if p:
                    hi(at, p, 4, 8)
                    squares_of(p - 1, at, p - 1)
                hi(at, p, 8, 12)
            bridge(5, at, 3, nxt, lambda: squares_of(2, at, 2))
            squares_of(3, at, 3)
            at = At("ffn2_first")
            hi(at, 0, 8, 12)
            x_norm(18)
            act.wait_ge(x_inv_ready, 4)
            gate_function(at, 0, NB1, ACT.Relu, pairs[at.pair(0)][:])

            def block2(at, i, last=False):
                hi(at, 0, 4, 8)
                hid_turn(i + NB1)
                hi(at, 1, 0, 4)
                gate_function(at, 0, i + (NB1 + 1), ACT.Relu, third)
                hi(at, 1, 4, 8)
                if last:
                    hid_turn(NB1 + NB2 - 1, 4)
                hi(at, 4, 2, 6)

            with act.Fori(0, NB2 - 2) as i:
                block2(At("ffn2", i), i)
            at = At("ffn2_last")
            block2(at, NB2 - 2, True)
            hi(at, 5, 4, 8)

        @block.vector
        def _(dve):
            v = nc.vector

            def lo(at, p, k0, k1, width=None):
                for k in range(k0, k1):
                    n = at.panels[p][1] if width is None else width
                    h = (at.gran0 + at.starts[p] + k) % 2
                    dve.wait_ge(hi_ready, at.gran(p, k) + 1)
                    v.tensor_tensor(w_lo[:, at.slot(p, k), :, 0:n],
                                    raw[:, at.raw_slot(p, k), 2 * h:2 * h + 2, 0:n],
                                    w_hi[:, at.slot(p, k), :, 0:n].bitcast(F32),
                                    ALU.subtract).then_inc(lo_ready, 1)

            def panel_done(at, p):
                dve.wait_ge(gran_used, at.end(p) + SPLIT)

            def inverse_root(n_roots, dst, src, count, between=None):
                v.tensor_scalar(dst, src, 1.0 / count, EPS, ALU.mult, ALU.add).then_inc(ms_ready, 1)
                if between is not None:
                    between()
                dve.wait_ge(rms_ready, n_roots + 1)
                v.reciprocal(dst, dst)
                dve.drain()

            def x_norm(n_sums, n_roots):
                dve.wait_ge(sumsq, n_sums + 1)
                v.tensor_reduce(ss[:, 0:2], x_ss, AX.X, ALU.add)
                dve.drain()
                inverse_root(n_roots, x_inv, ss[:, 0:2], D)
                dve.sem_inc(x_inv_ready, 1)

            def gained(b):
                c = slice(b * N, (b + 1) * N)
                v.tensor_tensor(mix[:, :, c], xres[:, :, c],
                                gain[:, c].unsqueeze(1).broadcast_to([P, TOK, N]), ALU.mult
                                ).then_inc(rows_ready, 2)

            def pieces(n_hi, kq):
                for p in (2 * kq, 2 * kq + 1):
                    dst = slice(p % 2 * P, (p % 2 + 1) * P)
                    dve.wait_ge(lhs_hi_ready, n_hi + p + 1)
                    v.tensor_tensor(lhs_lo[:, 4 * kq:4 * kq + 4, dst],
                                    aux[:, p % 4, :].rearrange("p (c t) -> p c t", c=4),
                                    lhs_hi[:, 4 * kq:4 * kq + 4, dst].bitcast(F32),
                                    ALU.subtract).then_inc(lhs_ready, 1)

            def refill(n_hi, kq):
                dve.wait_ge(lhs_hi_ready, n_hi + kq + 1)
                c = slice(4 * kq, 4 * kq + 4)
                v.tensor_tensor(lhs_lo[:, c, :], act_t[:, c, :], lhs_hi[:, c, :].bitcast(F32),
                                ALU.subtract).then_inc(lhs_ready, 2)

            def bridge(n_hi, at, p, nxt, last_rows, between=None):
                lo(at, p, 4, 6)
                pieces(n_hi, 0)
                lo(at, p, 6, 8)
                if between is not None:
                    between()
                pieces(n_hi, 1)
                lo(at, p, 8, 10)
                pieces(n_hi, 2)
                lo(at, p, 10, 12)
                last_rows()
                lo(nxt, 0, 4, 6)
                pieces(n_hi, 3)
                lo(nxt, 0, 6, 8)

            def rope(dst, src, tmp_a, tmp_b, heads):
                def table(t):
                    return t if heads is None else t.unsqueeze(2).broadcast_to([P, TOK, heads, ROPE])
                def halves(ap):
                    if heads is None:
                        return ap[:, :, 0:HALF], ap[:, :, HALF:ROPE]
                    return ap[:, :, :, 0:HALF], ap[:, :, :, HALF:ROPE]
                c, s = table(cosd[:]), table(sind[:])
                v.tensor_tensor(tmp_a, src, c, ALU.mult)
                v.tensor_tensor(halves(tmp_b)[0], halves(src)[1], halves(s)[0], ALU.mult)
                v.tensor_tensor(halves(tmp_b)[1], halves(src)[0], halves(s)[1], ALU.mult)
                dve.drain()
                v.tensor_tensor(dst, tmp_a, tmp_b, ALU.add)
                dve.drain()

            def rope_angles():
                dve.wait_ge(loaded["con"], 16)
                dve.wait_ge(loaded["pos"], 16)
                v.tensor_copy(pos_f, pos_i[:])
                dve.drain()
                ang, turns = junk[:, 0:64].rearrange("p (t f) -> p t f", t=TOK), junk[:, 64:128].rearrange(
                    "p (t f) -> p t f", t=TOK)
                for t in range(TOK):
                    v.tensor_scalar(ang[:, t, :], freq, pos_f[:, t:t + 1], None, ALU.mult)
                dve.drain()
                v.tensor_scalar(turns, ang, float(1 / TWO_PI), MAGIC, ALU.mult, ALU.add)
                dve.drain()
                v.tensor_scalar(turns, turns, -MAGIC, None, ALU.add)
                dve.drain()
                for c in (PI_1, PI_2, PI_3):
                    v.scalar_tensor_tensor(ang, turns, -float(c), ang, ALU.mult, ALU.add)
                    dve.drain()
                v.tensor_scalar(sind[:, :, 0:HALF], ang, PI_MAX, -PI_MAX, ALU.min, ALU.max)
                v.tensor_scalar(ang, ang, float(TWO_PI / 4), None, ALU.add)
                dve.drain()
                v.tensor_scalar(turns, ang, float(TWO_PI / 2), -float(TWO_PI), ALU.is_gt, ALU.mult)
                dve.drain()
                v.tensor_tensor(ang, ang, turns, ALU.add)
                dve.drain()
                v.tensor_scalar(cosd[:, :, HALF:ROPE], ang, PI_MAX, -PI_MAX, ALU.min, ALU.max)
                dve.drain().then_inc(angles, 1)

            def rope_tables():
                dve.wait_ge(sines, 1)
                v.tensor_copy(cosd[:, :, HALF:ROPE], cosd[:, :, 0:HALF])
                v.tensor_scalar(sind[:, :, 0:HALF], sind[:, :, HALF:ROPE], -1.0, None, ALU.mult)

            dve.sem_inc(lo_ready, LO_CREDIT)
            dve.sem_inc(evac_done, EVAC_CREDIT)
            at = At("in")
            for b in range(4):
                dve.wait_ge(x_loaded[b], 32)
                gained(b)
                pieces(0, b)
                lo(at, 0, 2 * b, 2 * b + 2)
            lo(at, 1, 0, 2)
            x_norm(0, 0)
            lo(at, 1, 2, 4)

            def low_norm(p, n_sums, n_roots, gains, rows):
                dve.wait_ge(sumsq, n_sums + 1)
                inverse_root(n_roots, cq_inv, cq_ss, Q_RANK)
                v.tensor_tensor(cq_inv, cq_inv, x_inv, ALU.mult)
                dve.drain()
                for t in range(TOK):
                    ins = v.scalar_tensor_tensor(rows[:, t, :], pairs[at.pair(p)][:, t, :],
                                                 cq_inv[:, t:t + 1], gains, ALU.mult, ALU.mult)
                dve.drain().then_inc(evac_done, 1)

            for p in range(1, 5):
                if p > 1:
                    lo(at, p, 0, 4)
                panel_done(at, p - 1)
                if p <= 2:
                    for t in range(TOK):
                        v.tensor_scalar(u_rows[:, t, (p - 1) * N:p * N], pairs[at.pair(p - 1)][:, t, :],
                                        x_inv[:, t:t + 1], None, ALU.mult)
                    dve.drain().then_inc(evac_done, 1)
                if p == 2:
                    rope_tables()
                if p == 3:
                    dve.wait_ge(loaded["qk"], 32)
                    dve.wait_ge(kr_sq, 1)
                    for t in range(TOK):
                        v.scalar_tensor_tensor(krr[:, t, :], pairs[at.pair(2)][:, t, 0:ROPE],
                                               x_inv[:, t:t + 1], gain_k[:, NOPE:QK], ALU.mult, ALU.mult)
                    dve.drain().then_inc(evac_done, 1)
                    ta = junk[:, 128:256].rearrange("p (t f) -> p t f", t=TOK)
                    tb = junk[:, 256:384].rearrange("p (t f) -> p t f", t=TOK)
                    rope(krr[:], krr[:], ta, tb, None)
                if p == 4:
                    dve.wait_ge(loaded["cq"], 32)
                    low_norm(3, 1, 1, gain_cq, cq_rows)
                lo(at, p, 4, 8)
                if p == 1:
                    rope_angles()
            nxt = At("pool")
            lo(nxt, 0, 0, 4)
            for j in range(8):
                dve.wait_ge(low_hi_ready, j // 2 * 2 + 2)
                v.scalar_tensor_tensor(low_lo[:, j, :], aux[:, j // 2, (j % 2) * S:(j % 2 + 1) * S],
                                       cols[:, j:j + 1], low_hi[:, j, :].bitcast(F32),
                                       ALU.mult, ALU.subtract).then_inc(low_ready, 1)
            panel_done(at, 4)
            low_norm(4, 2, 2, gain_ckv, ckv_rows)
            dve.sem_inc(low_rows, 1)
            with dve.Fori(0, 2) as i:
                at = At("pool", i)
                for p in range(2):
                    lo(at, p, 4, 8)
                    panel_done(at, p)
                    v.tensor_copy(mix[:, :, bass.ds(i * (2 * N) + p * N, N)], pairs[at.pair(p)][:]
                                  ).then_inc(evac_done, 1)

            def turned_low():
                for q in range(4):
                    dve.wait_ge(low_hi_ready, 8 + q + 1)
                    c0, t = 4 * (q // 2), q % 2
                    v.tensor_tensor(low_lo[:, c0:c0 + 4, t * P:(t + 1) * P],
                                    aux[:, q, :].rearrange("p (c t) -> p c t", c=4),
                                    low_hi[:, c0:c0 + 4, t * P:(t + 1) * P].bitcast(F32),
                                    ALU.subtract).then_inc(low_ready, 1)

            def per_head(scales, first, n):
                return scales[:, first:first + 4].rearrange("p (t h) -> p t h", t=TOK).unsqueeze(3).broadcast_to(
                    [P, TOK, 2, n])

            def attend_a(u):
                v.tensor_tensor(ss[:, 4:8].rearrange("p (t h) -> p t h", t=TOK),
                                ss[:, 4:8].rearrange("p (t h) -> p t h", t=TOK),
                                kr_ss.unsqueeze(2).broadcast_to([P, TOK, 2]), ALU.add)
                dve.drain()
                inverse_root(u + 2, inv, ss, QK)
                v.tensor_tensor(q_rows, q_rows, per_head(inv, 0, QK), ALU.mult)
                v.tensor_tensor(k_rows[:, :, :, 0:NOPE], k_rows[:, :, :, 0:NOPE], per_head(inv, 4, NOPE),
                                ALU.mult)
                v.tensor_tensor(k_rows[:, :, :, NOPE:QK], krr[:].unsqueeze(2).broadcast_to([P, TOK, 2, ROPE]),
                                per_head(inv, 4, ROPE), ALU.mult)
                dve.drain()

            def attend_b(u):
                qr = q_rows[:, :, :, NOPE:QK]
                rope(qr, qr, rope_a, rope_b, 2)
                dve.sem_inc(qk_done, 1)

            def attend_c(u):
                dve.wait_ge(scored, u)
                v.scalar_tensor_tensor(probs, aux[:, 0:2, 0:384], SM_SCALE,
                                       causal.unsqueeze(1).broadcast_to([P, 2, 384]), ALU.mult, ALU.add)
                dve.drain()
                v.tensor_reduce(row_max[:, 0:2], probs[:, :, 0:P], AX.X, ALU.max)
                v.tensor_reduce(row_max[:, 2:4], probs[:, :, P:3 * P], AX.X, ALU.max)
                dve.drain()
                v.tensor_scalar(row_max, row_max, -1.0, None, ALU.mult).then_inc(max_ready, 1)
                dve.wait_ge(exp_done, u)
                v.reciprocal(row_inv, row_sum)
                dve.drain()
                v.tensor_tensor(probs[:, :, 0:P], probs[:, :, 0:P],
                                row_inv[:, 0:2].unsqueeze(2).broadcast_to([P, 2, P]), ALU.mult)
                v.tensor_tensor(probs[:, :, P:3 * P], probs[:, :, P:3 * P],
                                row_inv[:, 2:4].unsqueeze(2).broadcast_to([P, 2, 2 * P]), ALU.mult)
                dve.drain().then_inc(p_ready, 1)

            def sub(at, p, u, has_last, last=False):
                if has_last:
                    attend_a(u)
                    attend_b(u)
                lo(at, p, 4, 8)
                if not has_last:
                    turned_low()
                lo(at, p + 1, 0, 2)
                if has_last:
                    attend_c(u)
                lo(at, p + 2, 0, 2)
                panel_done(at, p)
                dve.wait_ge(loaded["bias"], u * 16 + 16)
                for t in range(TOK):
                    v.scalar_tensor_tensor(gate_tmp[:, t, :], pairs[at.pair(p)][:, t, :], x_inv[:, t:t + 1],
                                           bias, ALU.mult, ALU.add)
                dve.drain().then_inc(evac_done, 1)
                dve.sem_inc(gate_in, 1)
                dve.sem_inc(bias_used, 1)
                dve.wait_ge(q_sq, u * 2 + 1)
                v.tensor_reduce(ss[:, 0:4].rearrange("p (t h) -> p t h", t=TOK), squares, AX.X, ALU.add)
                dve.drain().then_inc(q_sq, 1)
                qp = pairs[at.pair(p + 1)][:, :, 0:2 * QK].rearrange("p t (h d) -> p t h d", h=2)
                v.tensor_tensor(q_rows, qp, gain_q.unsqueeze(1).unsqueeze(1).broadcast_to([P, TOK, 2, QK]),
                                ALU.mult)
                dve.drain().then_inc(evac_done, 1)
                lo(at, p + 2, 2, 4, N)
                if last:
                    dve.wait_ge(av_stored, PAIRS - 2)
                    refill(8, 0)
                dve.wait_ge(gate_out, u + 1)
                m = mix[:, :, bass.ds(u * N, N)]
                v.tensor_tensor(m, m, gate_tmp, ALU.mult)
                dve.wait_ge(kv_sq, u + 1)
                v.tensor_reduce(ss[:, 4:8].rearrange("p (t h) -> p t h", t=TOK), squares[:, :, :, 0:NOPE],
                                AX.X, ALU.add)
                kp = pairs[at.pair(p + 2)][:].rearrange("p t (h d) -> p t h d", h=2)[:, :, :, 0:NOPE]
                v.tensor_tensor(k_rows[:, :, :, 0:NOPE], kp,
                                gain_k[:, 0:NOPE].unsqueeze(1).unsqueeze(1).broadcast_to([P, TOK, 2, NOPE]),
                                ALU.mult)
                dve.drain().then_inc(evac_done, 1)
                lo(at, p + 2, 4, 6, N)
                if last:
                    refill(8, 1)
                    refill(8, 2)

            sub(At("heads_first"), 0, 0, False)
            dve.wait_ge(mix_ones, 1)
            with dve.Fori(0, (PAIRS - 2) // 2) as i:
                for s in range(2):
                    sub(At("heads", i), 3 * s, i * 2 + (1 + s), True)
            sub(At("heads_last"), 0, PAIRS - 1, True, True)

            def add_branch(pair, col):
                a = mix[:, :, bass.ds(col + D, N)]
                m = mix[:, :, bass.ds(col, N)]
                v.tensor_tensor(a, a, pairs[pair][:], ALU.mult)
                dve.drain().then_inc(evac_done, 1)
                v.tensor_tensor(m, m, a, ALU.add)
                dve.drain().then_inc(rows_ready, 2)

            def add_x(at, p, col, pair=None):
                panel_done(at, p)
                xs = xres[:, :, col:col + N]
                ps = pairs[at.pair(p) if pair is None else pair][:]
                v.tensor_tensor(xs, xs, ps, ALU.add)
                dve.drain().then_inc(evac_done, 1)

            at = At("attn_o")
            attend_a(PAIRS)
            attend_b(PAIRS)
            lo(at, 0, 4, 10)
            attend_c(PAIRS)
            lo(at, 0, 10, 14)
            dve.sem_inc(evac_done, 2)
            dve.wait_ge(av_stored, PAIRS)
            refill(8, 3)
            dve.sem_inc(side_go, 1)
            lo(at, 0, 14, 18)
            panel_done(at, 2)
            add_branch(at.pair(2), 0)
            lo(at, 0, 18, 20)
            panel_done(at, 3)
            add_branch(at.pair(3), N)
            lo(at, 0, 20, 28)
            panel_done(at, 4)
            add_branch(at.pair(4), 2 * N)

            def last_branch():
                panel_done(at, 5)
                add_branch(at.pair(5), 3 * N)

            bridge(12, at, 5, At("out"), last_branch)

            def out_panels(at, nxt, n_hi, n_gains):
                lo(at, 0, 8, 12)
                add_x(at, 0, 0)
                dve.wait_ge(loaded["gain"], 16 * n_gains)
                gained(0)
                for p in range(1, 3):
                    lo(at, p, 4, 12)
                    add_x(at, p, p * N)
                    gained(p)

                def last_block():
                    add_x(at, 3, 3 * N)
                    gained(3)

                bridge(n_hi, at, 3, nxt, last_block)

            out_panels(At("out"), At("ffn_first"), 20, 1)

            def hid_turn(b, c0=0):
                for t in range(TOK):
                    dve.wait_ge(hid_hi_ready, b * 2 + t + 1)
                    v.tensor_tensor(low_lo[:, c0:c0 + 4, t * P:(t + 1) * P],
                                    aux[:, t, :].rearrange("p (c t) -> p c t", c=4),
                                    low_hi[:, c0:c0 + 4, t * P:(t + 1) * P].bitcast(F32),
                                    ALU.subtract).then_inc(hid_lo_ready, 1)

            def silu_gate(at, p, b):
                dve.wait_ge(act_ready, b + 1)
                for t in range(TOK):
                    v.scalar_tensor_tensor(hid[:, t, :], pairs[at.pair(p)][:, t, :], x_inv[:, t:t + 1],
                                           act_f[:, t, :], ALU.mult, ALU.mult)
                dve.drain().then_inc(evac_done, 1)

            def times_up(at, p):
                panel_done(at, p)
                for t in range(TOK):
                    v.scalar_tensor_tensor(hid[:, t, :], pairs[at.pair(p)][:, t, :], x_inv[:, t:t + 1],
                                           hid[:, t, :], ALU.mult, ALU.mult)
                dve.drain().then_inc(evac_done, 1)
                dve.sem_inc(hid_ready, 1)

            dve.drain()
            dve.sem_inc(side_go, 1)
            at = At("ffn_first")
            lo(at, 1, 0, 4)
            x_norm(3, 11)
            silu_gate(at, 0, 0)
            lo(at, 1, 4, 8)
            lo(at, 1, 8, 12)
            times_up(at, 1)

            def block(at, i, last=False):
                lo(at, 0, 4, 8)
                hid_turn(i)
                lo(at, 1, 0, 4)
                silu_gate(at, 0, i + 1)
                lo(at, 1, 4, 8)
                lo(at, 2, 0, 2)
                lo(at, 3, 0, 2)
                times_up(at, 1)
                for j in range(4):
                    lo(at, 2 + j, 4, 6)
                    if last and j == 1:
                        hid_turn(NB1 - 1, 4)
                    add_x(at, 2 + j, j * N)

            with dve.Fori(0, NB1 - 2) as i:
                block(At("ffn", i), i)
            at, nxt = At("ffn_last"), At("in2")
            block(at, NB1 - 2, True)
            dve.wait_ge(loaded["gain"], 32)
            for j in range(4):
                lo(at, 6 + j, 4, 6)
                add_x(at, 6 + j, j * N)
                gained(j)
                if j:
                    pieces(28, j - 1)
            lo(nxt, 0, 4, 6)
            pieces(28, 3)
            lo(nxt, 0, 6, 8)

            dve.sem_inc(qk2_sq, 1)
            at = At("in2")
            dve.drain()
            dve.sem_inc(side_go, 1)
            x_norm(4, 12)
            lo(at, 0, 8, 12)
            dve.wait_ge(loaded["qk2"], 32)

            def qk_norm(p):
                dve.wait_ge(qk2_sq, 2 * p + 2)
                v.tensor_reduce(ss.rearrange("p (t h) -> p t h", t=TOK),
                                qk_sq.rearrange("p t (h d) -> p t h d", h=4), AX.X, ALU.add)
                dve.drain().then_inc(qk2_sq, 1)
                inverse_root(13 + p, inv, ss, P, lambda: lo(at, p + 1, 4, 5))
                v.tensor_tensor(inv_x.rearrange("p (t h) -> p t h", t=TOK),
                                inv.rearrange("p (t h) -> p t h", t=TOK),
                                x_inv.unsqueeze(2).broadcast_to([P, TOK, 4]), ALU.mult)
                dve.drain()
                rows = qk_rows.rearrange("p t (h d) -> p t h d", h=4)
                v.tensor_tensor(rows, pairs[at.pair(p)][:].rearrange("p t (h d) -> p t h d", h=4),
                                inv_x.rearrange("p (t h) -> p t h", t=TOK).unsqueeze(3).broadcast_to(
                                    [P, TOK, 4, P]), ALU.mult)
                dve.drain().then_inc(evac_done, 1)
                v.tensor_tensor(qk_rows, qk_rows, gain_qk[:, p * N:(p + 1) * N].unsqueeze(1).broadcast_to(
                    [P, TOK, N]), ALU.mult)
                dve.drain().then_inc(qk2_ready, 1)

            def panel_taken(n):
                dve.wait_ge(gelu_done, n)
                dve.sem_inc(evac_done, 1)

            for p in range(1, 5):
                qk_norm(p - 1)
                lo(at, p, 5, 12)
            panel_taken(1)
            lo(at, 5, 4, 12)
            panel_taken(2)
            st = ln_stats.rearrange("p (t c s) -> p t c s", t=TOK, c=2)
            for t in range(TOK):
                for c in range(2):
                    v.bn_stats(st[:, t, c, :], vs[:, t, c * N:(c + 1) * N])
            dve.drain()
            for t in range(TOK):
                v.bn_aggr(ln_mv[:, 2 * t:2 * t + 2], st[:, t, :, :])
            dve.drain()
            inverse_root(17, ln_inv, ln_mv.rearrange("p (t s) -> p s t", s=2)[:, 1, :], 1)
            lo(at, 6, 4, 6)
            for t in range(TOK):
                v.tensor_scalar(vs[:, t, :], vs[:, t, :], ln_mv[:, 2 * t:2 * t + 1], ln_inv[:, t:t + 1],
                                ALU.subtract, ALU.mult)
            dve.drain()
            lo(at, 6, 6, 8)
            dve.wait_ge(loaded["ln"], 48)
            v.tensor_tensor(vs, vs, ln_g.unsqueeze(1).broadcast_to([P, TOK, SGU]), ALU.mult)
            dve.drain()
            lo(at, 6, 8, 12)
            panel_taken(3)
            v.tensor_tensor(vs, vs, ln_b.unsqueeze(1).broadcast_to([P, TOK, SGU]), ALU.add)
            dve.wait_ge(ws_ready, 1)
            v.memset(ws_t[CHUNK:P, :, 0:CHUNK], 0.0)
            dve.drain().then_inc(ln_done, 1)
            lo(at, 7, 4, 12)
            panel_taken(4)
            lo(at, 8, 4, 6)
            for g in range(GROUPS):
                dve.wait_ge(sgu_mm, g // 2 + 1)
                c = slice(g * P, (g + 1) * P)
                v.scalar_tensor_tensor(us[:, :, c],
                                       aux[:, g // 2, (g % 2) * S:(g % 2 + 1) * S].rearrange("p (t d) -> p t d", t=TOK),
                                       cols[:, 8 + g:9 + g], us[:, :, c], ALU.add, ALU.mult)
            dve.drain().then_inc(sgu_rows, 1)
            lo(at, 8, 6, 12)
            panel_taken(5)
            lo(at, 9, 4, 12)
            panel_taken(6)

            def head2(at, p, head, last=False):
                dve.wait_ge(z_split, head + 1)
                z = aux[:, 0, 0:384]
                v.tensor_scalar(z_pos, z, SB_SCALE, 0.0, ALU.mult, ALU.max)
                v.tensor_scalar(z_neg, z, SB_SCALE, 0.0, ALU.mult, ALU.min)
                dve.drain()
                dve.wait_ge(z_log, head + 1)
                v.tensor_tensor(z_pos, z_pos, z_abs, ALU.add)
                v.tensor_tensor(z_neg, z_neg, z_abs, ALU.subtract)
                dve.drain()
                for c in (0, 2 * P):
                    v.tensor_tensor(z_pos[:, c:c + P], z_pos[:, c:c + P], past, ALU.mult)
                dve.drain().then_inc(keep_ready, 1)
                lo(at, p, 4, 8)
                dve.wait_ge(tail_done, head + 1)
                v.tensor_tensor(z_neg, z_neg, aux[:, 1, 0:384], ALU.subtract).then_inc(log_a, 1)
                dve.wait_ge(a_exp, head + 1)
                for c in (0, 2 * P):
                    v.tensor_tensor(att[:, c:c + P], att[:, c:c + P], past, ALU.mult)
                dve.drain().then_inc(a_ready, 1)
                if last:
                    for kq in range(3):
                        refill(36, kq)
                        if kq:
                            lo(at, p, 6 + 2 * kq, 8 + 2 * kq)
                else:
                    lo(at, p, 8, 12)
                dve.wait_ge(gate_out, head + PAIRS + 1)
                dve.sem_inc(evac_done, 1)

            with dve.Fori(0, SB_HEADS // 2 - 1) as i:
                for p in range(2):
                    head2(At("gates2", i), p, i * 2 + p)
            for p in range(2):
                head2(At("gates2_last"), p, SB_HEADS - 2 + p, p == 1)
            at = At("mix2")
            dve.wait_ge(av_stored, 2 * PAIRS)

            def mix_turn(at, i):
                m = mix[:, :, bass.ds(i * N, N)]
                panel_done(at, 0)
                v.tensor_tensor(m, m, pairs[at.pair(0)][:], ALU.mult)
                dve.drain().then_inc(evac_done, 1)

            dve.sem_inc(side_go, 1)
            refill(36, 3)
            lo(at, 0, 4, 8)
            mix_turn(at, 0)
            lo(at, 0, 8, 12)
            panel_done(at, 1)
            add_branch(at.pair(1), 0)
            with dve.Fori(1, 3) as i:
                at = At("mix2", i)
                lo(at, 0, 4, 8)
                mix_turn(at, i)
                lo(at, 0, 8, 12)
                panel_done(at, 1)
                add_branch(at.pair(1), i * N)
            at = At("mix2", 3)

            def last_mix():
                panel_done(at, 1)
                add_branch(at.pair(1), 3 * N)

            bridge(40, at, 0, At("out2"), last_mix, lambda: mix_turn(at, 3))
            out_panels(At("out2"), At("ffn2_first"), 48, 3)
            at = At("ffn2_first")

            def relu_square(at, b, src):
                dve.wait_ge(act_ready, b + 1)
                for t in range(TOK):
                    v.scalar_tensor_tensor(hid[:, t, :], src[:, t, :], x_inv[:, t:t + 1], act_f[:, t, :],
                                           ALU.mult, ALU.mult)
                dve.drain().then_inc(evac_done, 1)
                dve.sem_inc(hid_ready, 1)

            lo(at, 0, 8, 12)
            x_norm(5, 18)
            relu_square(at, NB1, pairs[at.pair(0)][:])

            def block2(at, i, last=False):
                lo(at, 0, 4, 8)
                hid_turn(i + NB1)
                lo(at, 1, 0, 4)
                relu_square(at, i + (NB1 + 1), third)
                for j in range(4):
                    lo(at, 1 + j, 4, 6)
                    if last and j == 1:
                        hid_turn(NB1 + NB2 - 1, 4)
                    add_x(at, 1 + j, j * N, j % 2)

            with dve.Fori(0, NB2 - 2) as i:
                block2(At("ffn2", i), i)
            at = At("ffn2_last")
            block2(at, NB2 - 2, True)
            for j in range(4):
                if j < 2:
                    lo(at, 5 + j, 4, 6)
                add_x(at, 5 + j, j * N, j % 2)

        @block.tensor
        def _(pe):
            def group(at, p, g, left, c0, ps, start, stop):
                kch, n = at.panels[p]
                hi_t, lo_t = left
                for h in range(2):
                    k = 2 * g + h
                    pe.wait_ge(lo_ready, at.gran(p, k) + 1 + LO_CREDIT)
                    s = at.slot(p, k)
                    for c in range(2):
                        ch = 2 * k + c
                        for t in range(TOK):
                            tok = slice(t * P, (t + 1) * P)
                            x_hi, x_lo = hi_t[:, c0 + ch, tok], lo_t[:, c0 + ch, tok]
                            nc.tensor.matmul(ps[:, t, 0:n], x_hi, w_hi[:, s, c, 0:n],
                                             start=start and ch == 0, stop=False)
                            nc.tensor.matmul(ps[:, t, 0:n], x_hi, w_lo[:, s, c, 0:n], start=False, stop=False)
                            mm = nc.tensor.matmul(ps[:, t, 0:n], x_lo, w_hi[:, s, c, 0:n], start=False,
                                                  stop=stop and ch == kch - 1)
                    mm.then_inc(gran_used, 1)

            def bank_free(at, p):
                pe.wait_ge(evac_done, at.panel(p) - 1 + EVAC_CREDIT)

            def gemm(at, p, left, c0=0, groups=None, ps=None, start=True, stop=True):
                ps = pairs[at.pair(p)] if ps is None else ps
                kch = at.panels[p][0]
                groups = range(kch // 4) if groups is None else groups
                if groups[0] == 0:
                    bank_free(at, p)
                for g in groups:
                    group(at, p, g, left, c0, ps, start, stop)

            wide, low = (lhs_hi, lhs_lo), (low_hi, low_lo)

            def turn(dst, src):
                return nc.tensor.transpose(dst, src, ident[0:src.shape[0], :])

            def pieces(r, f, kq):
                pe.wait_ge(rows_ready, 8 * r + 2 * kq + 2)
                for p in (2 * kq, 2 * kq + 1):
                    if p >= 4:
                        pe.wait_ge(lhs_ready, 8 * f + p - 3)
                    for c in range(4):
                        ins = turn(aux[:, p % 4, c * P:(c + 1) * P],
                                   mix[:, p % 2, (4 * kq + c) * P:(4 * kq + c + 1) * P])
                    ins.then_inc(turned, 1)

            def gemm_after(at, f, left, c0=0, r=None, ps=None):
                for g in range(4):
                    pe.wait_ge(lhs_ready, 8 * f + 2 * g + 2)
                    gemm(at, 0, left, c0, [g], ps)
                    if g == 1:
                        pieces(r, f, 3)

            def last_panel(at, p, r, f):
                for g in range(4):
                    gemm(at, p, wide, groups=[g])
                    if g < 3:
                        pieces(r, f, g)

            pe.wait_ge(ident_loaded, 16)
            at = At("in")
            pieces(0, 0, 0)
            for g in range(4):
                if g < 3:
                    pieces(0, 0, g + 1)
                pe.wait_ge(lhs_ready, 2 * g + 2)
                gemm(at, 0, wide, groups=[g])
            for p in range(1, 4):
                gemm(at, p, wide)
            pe.wait_ge(evac_done, 2 + EVAC_CREDIT)
            pe.wait_ge(loaded["pool"], 32)
            for c in range(8):
                dst = aux[:, c // 2, (c % 2) * S:(c % 2 + 1) * S]
                ch = slice(c * P, (c + 1) * P)
                nc.tensor.matmul(dst, u_rows[:, 0, ch], pool_a[:, c // 2, 0:S], start=True, stop=False)
                mm = nc.tensor.matmul(dst[:, P:S], u_rows[:, 1, ch], pool_a[:, c // 2, S:S + P],
                                      start=False, stop=True)
                if c % 2:
                    mm.then_inc(pool_mm, 1)
            gemm(at, 4, wide)
            pe.wait_ge(pool_out, 1)
            for j in range(8):
                dst = aux[:, j // 2, (j % 2) * S:(j % 2 + 1) * S]
                g, d = j // 2, j % 2
                for c in range(2):
                    mm = nc.tensor.matmul(dst, w_grp[:, g, c, d * P:(d + 1) * P], act_t[:, 2 * g + c, :],
                                          start=c == 0, stop=c == 1)
                if j % 2:
                    mm.then_inc(pool_mm, 1)
            with pe.Fori(0, 2) as i:
                for p in range(2):
                    for g in range(2):
                        pe.wait_ge(low_ready, 4 * g + 4)
                        gemm(At("pool", i), p, low, groups=[g])

            def turn_low():
                pe.wait_ge(low_rows, 1)
                for q in range(4):
                    rows = cq_rows if q < 2 else ckv_rows
                    for c in range(4):
                        ins = turn(aux[:, q, c * P:(c + 1) * P], rows[:, q % 2, c * P:(c + 1) * P])
                    ins.then_inc(low_turned, 1)

            def turn_qk(u):
                pe.wait_ge(qk_done, u)
                for h in range(2):
                    for t in range(TOK):
                        c = slice(h * S + t * P, h * S + (t + 1) * P)
                        turn(aux[:, 0, c], q_rows[:, t, h, 0:NOPE])
                        turn(aux[:, 1, c], k_rows[:, t, h, 0:NOPE])
                        turn(aux[0:ROPE, 2, c], q_rows[:, t, h, NOPE:QK])
                        ins = turn(aux[0:ROPE, 3, c], k_rows[:, t, h, NOPE:QK])
                ins.then_inc(qk_turned, 1)

            def score(u):
                pe.wait_ge(qk_copied, u)
                for h in range(2):
                    for t in range(TOK):
                        c = slice(0, P) if t == 0 else slice(P, 3 * P)
                        keys = slice(0, (t + 1) * P)
                        tok = slice(t * P, (t + 1) * P)
                        nc.tensor.matmul(aux[:, h, c], q_tn[:, h, tok], k_tn[:, h, keys], start=True, stop=False)
                        mm = nc.tensor.matmul(aux[:, h, c], q_tr[0:ROPE, h, tok], k_tr[0:ROPE, h, keys],
                                              start=False, stop=True)
                mm.then_inc(scored, 1)

            def turn_p(u):
                pe.wait_ge(p_ready, u)
                for h in range(2):
                    for b in range(3):
                        ins = turn(aux[:, 2 + h, b * P:(b + 1) * P], probs[:, h, b * P:(b + 1) * P])
                ins.then_inc(p_turned, 1)

            def values(u):
                pe.wait_ge(p_copied, u)
                for h in range(2):
                    dst = aux[:, 0, h * S:(h + 1) * S]
                    nc.tensor.matmul(dst, v_rows[:, 0, h, :], p_t[:, h, 0:S], start=True, stop=False)
                    mm = nc.tensor.matmul(dst[:, P:S], v_rows[:, 1, h, :], p_t[:, h, S:S + P],
                                          start=False, stop=True)
                mm.then_inc(av_done, 1)

            def sub(at, p, u, has_last):
                gemm(at, p, wide, groups=[0, 1])
                if has_last:
                    turn_qk(u)
                else:
                    turn_low()
                gemm(at, p, wide, groups=[2])
                if has_last:
                    score(u)
                gemm(at, p, wide, groups=[3])
                if has_last:
                    turn_p(u)
                else:
                    pe.wait_ge(low_ready, 12)
                gemm(at, p + 1, low)
                if has_last:
                    values(u)
                gemm(at, p + 2, low, 4)

            sub(At("heads_first"), 0, 0, False)
            with pe.Fori(0, (PAIRS - 2) // 2) as i:
                for s in range(2):
                    sub(At("heads", i), 3 * s, i * 2 + (1 + s), True)
            sub(At("heads_last"), 0, PAIRS - 1, True)
            at = At("attn_o")
            pe.wait_ge(lhs_ready, 10)
            gemm(at, 0, wide, groups=[0], stop=False)
            pe.wait_ge(lhs_ready, 12)
            gemm(at, 0, wide, groups=[1], stop=False)
            turn_qk(PAIRS)
            pe.wait_ge(lhs_ready, 14)
            gemm(at, 0, wide, groups=[2], stop=False)
            score(PAIRS)
            gemm(at, 1, wide, groups=[0], stop=False)
            turn_p(PAIRS)
            gemm(at, 1, wide, groups=[1], stop=False)
            values(PAIRS)
            gemm(at, 1, wide, groups=[2], stop=False)
            pe.wait_ge(lhs_ready, 16)
            for p in range(2):
                gemm(at, 2 + p, wide, KC - 4, start=False)
            gemm(at, 4, wide)
            last_panel(at, 5, 1, 2)
            at = At("out")
            gemm_after(at, 2, wide, 0, 1)
            for p in range(1, 3):
                gemm(at, p, wide)
            last_panel(at, 3, 2, 3)

            def hid_turn(b):
                pe.wait_ge(hid_ready, b + 2)
                for t in range(TOK):
                    for c in range(4):
                        ins = turn(aux[:, t, c * P:(c + 1) * P], hid[:, t, c * P:(c + 1) * P])
                    ins.then_inc(hid_turned, 1)

            at = At("ffn_first")
            gemm_after(at, 3, wide, 0, 2)
            gemm(at, 1, wide)

            def block(at, i, last=False):
                gemm(at, 0, wide, groups=[0, 1])
                hid_turn(i)
                gemm(at, 0, wide, groups=[2, 3])
                gemm(at, 1, wide)
                pe.wait_ge(hid_lo_ready, i * 2 + 2)
                for j in range(4):
                    if last and j == 1:
                        hid_turn(NB1 - 1)
                    gemm(at, 2 + j, low)

            with pe.Fori(0, NB1 - 2) as i:
                block(At("ffn", i), i)
            at = At("ffn_last")
            block(at, NB1 - 2, True)
            pe.wait_ge(hid_lo_ready, 2 * NB1)
            for j in range(4):
                gemm(at, 6 + j, low, 4)
                if j:
                    pieces(3, 4, j - 1)

            at = At("in2")
            gemm_after(at, 4, wide, 0, 3)

            def turn_qk2(p):
                pe.wait_ge(qk2_ready, p + 1)
                if p:
                    pe.wait_ge(qk2_copied, 2 * p)
                for t in range(TOK):
                    for c in range(4):
                        ins = turn(aux[:, t, c * P:(c + 1) * P], qk_rows[:, t, c * P:(c + 1) * P])
                    ins.then_inc(qk2_turned, 1)

            def turn_spatial():
                pe.wait_ge(loaded["ln"], 48)
                pe.wait_ge(qk2_copied, 8)
                for g in range(GROUPS):
                    ins = turn(aux[:, g // 4, (g % 4) * P:(g % 4 + 1) * P], ws_raw[:, g, :])
                ins.then_inc(ws_turned, 1)

            def spatial():
                pe.wait_ge(ln_done, 1)
                for g in range(GROUPS):
                    mm = nc.tensor.matmul(aux[:, g // 2, (g % 2) * S:(g % 2 + 1) * S].rearrange("p (t d) -> p t d", t=TOK),
                                          ws_t[:, g, :], vs[:, :, g * P:(g + 1) * P], start=True, stop=True)
                    if g % 2:
                        mm.then_inc(sgu_mm, 1)

            def turn_gated():
                pe.wait_ge(sgu_rows, 1)
                for c in range(8):
                    for t in range(TOK):
                        ins = turn(aux[:, c // 2, (c % 2) * S + t * P:(c % 2) * S + (t + 1) * P],
                                   us[:, t, c * P:(c + 1) * P])
                    if c % 2:
                        ins.then_inc(sgu_turned, 1)

            for p in range(1, 10):
                gemm(at, p, wide, groups=[0])
                if p == 8:
                    spatial()
                if p == 9:
                    turn_gated()
                gemm(at, p, wide, groups=[1, 2])
                if p <= 4:
                    turn_qk2(p - 1)
                if p == 5:
                    turn_spatial()
                gemm(at, p, wide, groups=[3])

            def head2(at, p, head):
                pe.wait_ge(keys_copied, head + 1)
                q_head = qk_t[:, bass.ds(head, 1), :].rearrange("p a t -> p (a t)")
                nc.tensor.matmul(aux[:, 0, 0:S], k_head[:, 0:P], q_head, start=True, stop=True)
                nc.tensor.matmul(aux[:, 0, S:S + P], k_head[:, P:S],
                                 qk_t[:, bass.ds(head, 1), P:S].rearrange("p a t -> p (a t)"),
                                 start=True, stop=True).then_inc(z_done, 1)
                gemm(at, p, wide, groups=[0, 1])
                pe.wait_ge(keep_ready, head + 1)
                nc.tensor.matmul(aux[:, 1, 0:384], after, z_pos, start=True, stop=False)
                nc.tensor.matmul(aux[:, 1, P:S], ones, z_pos[:, S:S + P], start=False, stop=True
                                 ).then_inc(tail_done, 1)
                gemm(at, p, wide, groups=[2, 3])
                pe.wait_ge(a_ready, head + 1)
                pe.wait_ge(values_copied, head + 1)
                nc.tensor.matmul(aux[:, 2, 0:S], v_head[:, 0, :], att[:, 0:S], start=True, stop=False)
                nc.tensor.matmul(aux[:, 2, P:S], v_head[:, 1, :], att[:, S:S + P], start=False, stop=True
                                 ).then_inc(av_done, 1)

            with pe.Fori(0, SB_HEADS // 2 - 1) as i:
                for p in range(2):
                    head2(At("gates2", i), p, i * 2 + p)
            for p in range(2):
                head2(At("gates2_last"), p, SB_HEADS - 2 + p)
            at = At("mix2")
            for g in range(2):
                pe.wait_ge(lhs_ready, 8 * 5 + 2 * g + 2)
                gemm(at, 0, wide, 0, [g])
            for g in range(2):
                pe.wait_ge(lhs_ready, 8 * 5 + 2 * g + 6)
                gemm(at, 1, wide, 8, [g])
            with pe.Fori(1, 3) as i:
                gemm(At("mix2", i), 0, wide)
                gemm(At("mix2", i), 1, wide, 8)
            at = At("mix2", 3)
            for kq in range(4):
                gemm(at, kq // 2, wide, kq // 2 * 8, [kq % 2])
                if kq < 3:
                    pieces(4, 6, kq)
            at = At("out2")
            gemm_after(at, 6, wide, 0, 4)
            for p in range(1, 3):
                gemm(at, p, wide)
            last_panel(at, 3, 5, 7)

            at = At("ffn2_first")
            gemm_after(at, 7, wide, 0, 5)

            def block2(at, i, last=False):
                gemm(at, 0, wide, groups=[0, 1], ps=third)
                hid_turn(i + NB1)
                gemm(at, 0, wide, groups=[2, 3], ps=third)
                pe.wait_ge(hid_lo_ready, i * 2 + (2 * NB1 + 2))
                for j in range(4):
                    if last and j == 1:
                        hid_turn(NB1 + NB2 - 1)
                    gemm(at, 1 + j, low, ps=pairs[j % 2])

            with pe.Fori(0, NB2 - 2) as i:
                block2(At("ffn2", i), i)
            at = At("ffn2_last")
            block2(at, NB2 - 2, True)
            pe.wait_ge(hid_lo_ready, 2 * (NB1 + NB2))
            for j in range(4):
                gemm(at, 5 + j, low, 4, ps=pairs[j % 2])


_INS = ["x", "positions", "attn_norm_g", "w_in", "b_gate", "q_a_norm_g", "w_q_b", "kv_a_norm_g",
        "w_kv_b", "q_norm_g", "k_norm_g", "w_attn_o", "w_pool_grp", "pool_scale", "w_pool_o", "w_out",
        "ffn_norm_g", "w_ffn_gate", "w_ffn_up", "w_ffn_down", "g_mix_2", "w_in_2", "g_q_2", "g_k_2",
        "sgu_ln_g_2", "sgu_ln_b_2", "w_spatial_2", "b_spatial_2", "w_oa_2", "w_ob_2", "w_out_2",
        "g_ff_2", "w_ff1_2", "w_ff2_2"]


def shape_constants():
    r = np.arange(P)
    con = np.zeros((P, C_END), np.float32)
    con[:, C_ID:C_ID + P] = np.eye(P)
    for b in (0, 2):
        con[:, C_CAUSAL + b * P:C_CAUSAL + (b + 1) * P] = np.where(r[None, :] <= r[:, None], 0.0, -3e38)
    con[:, C_AFTER:C_AFTER + P] = r[:, None] > r[None, :]
    con[:, C_ONES:C_ONES + P] = 1.0
    con[:, C_PAST:C_PAST + P] = r[:, None] < r[None, :]
    half = np.arange(HALF, dtype=np.float32)
    con[:, C_FREQ:C_FREQ + HALF] = (np.float32(10000.0) ** (-half / np.float32(HALF)))[None, :]
    mats = np.zeros((P, 4, 384), np.float32)
    src = np.arange(S)[:, None]
    dst = np.arange(S)[None, :]
    for g, w in enumerate(POOL_WINDOWS):
        lo = np.maximum(dst + 1 - w, 0)
        a = np.where((src >= lo) & (src <= dst), 1.0 / (dst + 1 - lo), 0.0) - (src == dst)
        mats[:, g, 0:S] = a[0:P, :]
        mats[:, g, S:S + P] = a[P:S, P:S]
    return con, mats


def kernel(**inputs):
    import concourse.bacc as bacc
    from concourse.bass_utils import run_bass_kernel_spmd

    nc = bacc.Bacc("TRN2", target_bir_lowering=False, num_devices=1)
    arrays, args = {}, []
    con, mats = shape_constants()
    named = [(n, np.ascontiguousarray(inputs[n])) for n in _INS] + [("consts", con), ("pool_mats", mats)]
    for name, a in named:
        arrays[f"in_{name}"] = a
        args.append(nc.dram_tensor(f"in_{name}", a.shape, mybir.dt.from_np(a.dtype), kind="ExternalInput").ap())
    args.append(nc.dram_tensor("out_x", (1, S, D), F32, kind="ExternalOutput").ap())
    two_blocks(nc, *args)
    r = run_bass_kernel_spmd(nc, [arrays], core_ids=[0])
    return r.results[0]["out_x"]
```
